# Optimizing a Trainium2 kernel written in Bass

```python
import math
import jax, jax.numpy as jnp
from jax import lax
import numpy as np

D_MODEL = 1024
BATCH = 1
SEQ = 256
DEPTH = 2

CHUNK = 64
N_MIXERS = 2
N_SSD_LAYERS = (DEPTH + 1) // 2
N_ATTN_LAYERS = DEPTH // 2
EPS = 1e-6

SSD_EXPAND = 2
SSD_D_INNER = SSD_EXPAND * D_MODEL
SSD_HEAD_DIM = 64
SSD_HEADS = SSD_D_INNER // SSD_HEAD_DIM
SSD_GROUPS = 4
SSD_HEADS_PER_GROUP = SSD_HEADS // SSD_GROUPS
SSD_STATE = 128
SSD_CONV = 4
SSD_CONV_CH = SSD_D_INNER + 2 * SSD_GROUPS * SSD_STATE
SSD_IN = SSD_D_INNER + SSD_CONV_CH + SSD_HEADS

ATTN_HEADS = 8
ATTN_HEAD_DIM = D_MODEL // ATTN_HEADS // 2
ATTN_V_DIM = 2 * ATTN_HEAD_DIM
ATTN_IN = 3 * D_MODEL
ROPE_THETA = 500000.0
ROPE_DIM = ATTN_HEAD_DIM // 4
Q_BLOCK = 128

D_FF = 2816
FFN_CONV = 3


def rmsnorm(x, g):
    xf = x.astype(jnp.float32)
    y = xf * lax.rsqrt(jnp.mean(xf * xf, axis=-1, keepdims=True) + EPS)
    return (y * g).astype(x.dtype)

def causal_dwconv(x, w, b):
    k_width = w.shape[0]
    s = x.shape[1]
    xp = jnp.pad(x, ((0, 0), (k_width - 1, 0), (0, 0)))
    y = b
    for k in range(k_width):
        y = y + w[k] * xp[:, k:k + s]
    return y

def rope_tables(positions):
    inv_freq = ROPE_THETA ** (-jnp.arange(0, ROPE_DIM, 2, dtype=jnp.float32) / ROPE_DIM)
    ang = positions.astype(jnp.float32)[..., None] * inv_freq
    return jnp.cos(ang), jnp.sin(ang)

def apply_partial_rope(t, cos, sin):
    half = ROPE_DIM // 2
    c = cos[:, :, None, None, :]
    s = sin[:, :, None, None, :]
    tf = t.astype(jnp.float32)
    x1, x2, rest = tf[..., :half], tf[..., half:ROPE_DIM], tf[..., ROPE_DIM:]
    out = jnp.concatenate([x1 * c - x2 * s, x2 * c + x1 * s, rest], axis=-1)
    return out.astype(t.dtype)

def ssd_mixer(xn, in_w, conv_w, conv_b, dt_bias, a_log, d_skip, norm_g, out_w):
    b, s, _ = xn.shape
    nc = s // CHUNK
    G, R, P, N = SSD_GROUPS, SSD_HEADS_PER_GROUP, SSD_HEAD_DIM, SSD_STATE
    proj = xn @ in_w
    z = proj[..., :SSD_D_INNER]
    xbc = proj[..., SSD_D_INNER:SSD_D_INNER + SSD_CONV_CH]
    dt = proj[..., SSD_D_INNER + SSD_CONV_CH:]
    xbc = jax.nn.silu(causal_dwconv(xbc, conv_w, conv_b))
    xs = xbc[..., :SSD_D_INNER].reshape(b, nc, CHUNK, G, R, P)
    Bm = xbc[..., SSD_D_INNER:SSD_D_INNER + G * N].reshape(b, nc, CHUNK, G, N)
    Cm = xbc[..., SSD_D_INNER + G * N:].reshape(b, nc, CHUNK, G, N)
    dt = jax.nn.softplus(dt + dt_bias).reshape(b, nc, CHUNK, G, R)
    a = -jnp.exp(a_log).reshape(G, R)
    dA = (dt * a).transpose(0, 3, 4, 1, 2)
    x_dt = xs * dt[..., None]
    a_cs = jnp.cumsum(dA, axis=-1)
    seg = a_cs[..., :, None] - a_cs[..., None, :]
    tril = jnp.tril(jnp.ones((CHUNK, CHUNK), dtype=bool))
    lmat = jnp.where(tril, jnp.exp(jnp.where(tril, seg, -jnp.inf)), 0.0)
    cb = jnp.einsum("bclgn,bcsgn->bgcls", Cm, Bm)
    y_diag = jnp.einsum("bgrcls,bcsgrp->bclgrp", cb[:, :, None] * lmat, x_dt)
    decay = jnp.exp(a_cs[..., -1:] - a_cs)
    states = jnp.einsum("bclgn,bgrcl,bclgrp->cbgrpn", Bm, decay, x_dt)
    chunk_decay = jnp.exp(a_cs[..., -1]).transpose(3, 0, 1, 2)

    def step(h, inp):
        st, dec = inp
        return dec[..., None, None] * h + st, h

    _, h_in = lax.scan(step, jnp.zeros_like(states[0]), (states, chunk_decay))
    y_off = jnp.einsum("bclgn,cbgrpn,bgrcl->bclgrp", Cm, h_in, jnp.exp(a_cs))
    y = y_diag + y_off + xs * d_skip.reshape(G, R)[:, :, None]
    y = y.reshape(b, s, SSD_D_INNER)
    yg = (y * jax.nn.silu(z)).reshape(b, s, G, SSD_D_INNER // G)
    yg = rmsnorm(yg, 1.0).reshape(b, s, SSD_D_INNER) * norm_g
    return yg.astype(xn.dtype) @ out_w

def diff_attention(xn, cos, sin, in_w, q_norm_g, k_norm_g, lq1, lk1, lq2, lk2,
                   subln_g, out_w, lambda_init):
    b, s, _ = xn.shape
    H, HD = ATTN_HEADS, ATTN_HEAD_DIM
    proj = xn @ in_w
    q = proj[..., :D_MODEL].reshape(b, s, H, 2, HD)
    k = proj[..., D_MODEL:2 * D_MODEL].reshape(b, s, H, 2, HD)
    v = proj[..., 2 * D_MODEL:].reshape(b, s, H, ATTN_V_DIM)
    q = apply_partial_rope(rmsnorm(q, q_norm_g), cos, sin)
    k = apply_partial_rope(rmsnorm(k, k_norm_g), cos, sin)
    lam = (jnp.exp(jnp.sum(lq1.astype(jnp.float32) * lk1.astype(jnp.float32)))
           - jnp.exp(jnp.sum(lq2.astype(jnp.float32) * lk2.astype(jnp.float32)))
           + lambda_init)
    scale = 1.0 / math.sqrt(HD)
    outs = []
    for blk in range(s // Q_BLOCK):
        q0, q1 = blk * Q_BLOCK, (blk + 1) * Q_BLOCK
        qb = q[:, q0:q1]
        kc = k[:, :q1]
        vc = v[:, :q1]
        sc = jnp.einsum("bqhcd,bkhcd->bhcqk", qb, kc).astype(jnp.float32) * scale
        q_chunk = (q0 + jnp.arange(Q_BLOCK)) // CHUNK
        k_chunk = jnp.arange(q1) // CHUNK
        allowed = k_chunk[None, :] <= q_chunk[:, None]
        sc = jnp.where(allowed, sc, -jnp.inf)
        p = jax.nn.softmax(sc, axis=-1)
        attn = p[:, :, 0] - lam * p[:, :, 1]
        outs.append(jnp.einsum("bhqk,bkhe->bqhe", attn.astype(v.dtype), vc))
    o = jnp.concatenate(outs, axis=1)
    o = rmsnorm(o, subln_g) * (1.0 - lambda_init)
    return o.reshape(b, s, H * ATTN_V_DIM).astype(xn.dtype) @ out_w

def conv_ffn(xn, up_w, conv_w, conv_b, down_w):
    h = causal_dwconv(xn @ up_w, conv_w, conv_b)
    g, u = h[..., :D_FF], h[..., D_FF:]
    return (jax.nn.silu(g) * u) @ down_w

def first_inputs(seed: int = 0) -> dict:
    key = jax.random.key(seed)
    ks = jax.random.split(key, 32)
    f32 = jnp.float32

    def nrm(k, shape, std):
        return jax.random.normal(k, shape, f32) * std

    def gain(k, shape):
        return 1.0 + 0.05 * jax.random.normal(k, shape, f32)

    out_scale = 1.0 / math.sqrt(2 * DEPTH)
    x = jax.random.normal(ks[0], (BATCH, SEQ, D_MODEL), f32)
    start = jax.random.randint(ks[1], (BATCH,), 0, 64) * CHUNK
    positions = (start[:, None] + jnp.arange(SEQ)[None, :]).astype(jnp.int32)
    dt0 = jnp.exp(jax.random.uniform(ks[6], (N_SSD_LAYERS, SSD_HEADS), f32,
                                     math.log(0.001), math.log(0.1)))
    return {
        "x": x,
        "positions": positions,
        "norm_mix_g": gain(ks[2], (DEPTH, D_MODEL)),
        "norm_ffn_g": gain(ks[3], (DEPTH, D_MODEL)),
        "ssd_in_w": nrm(ks[4], (N_SSD_LAYERS, D_MODEL, SSD_IN), D_MODEL ** -0.5),
        "ssd_conv_w": nrm(ks[5], (N_SSD_LAYERS, SSD_CONV, SSD_CONV_CH), SSD_CONV ** -0.5),
        "ssd_conv_b": nrm(ks[7], (N_SSD_LAYERS, SSD_CONV_CH), 0.02),
        "ssd_dt_bias": dt0 + jnp.log(-jnp.expm1(-dt0)),
        "ssd_a_log": jnp.log(jax.random.uniform(ks[8], (N_SSD_LAYERS, SSD_HEADS), f32, 1.0, 16.0)),
        "ssd_d": gain(ks[9], (N_SSD_LAYERS, SSD_HEADS)),
        "ssd_norm_g": gain(ks[10], (N_SSD_LAYERS, SSD_D_INNER)),
        "ssd_out_w": nrm(ks[11], (N_SSD_LAYERS, SSD_D_INNER, D_MODEL), SSD_D_INNER ** -0.5 * out_scale),
        "attn_in_w": nrm(ks[12], (N_ATTN_LAYERS, D_MODEL, ATTN_IN), D_MODEL ** -0.5),
        "attn_q_norm_g": gain(ks[13], (N_ATTN_LAYERS, ATTN_HEAD_DIM)),
        "attn_k_norm_g": gain(ks[14], (N_ATTN_LAYERS, ATTN_HEAD_DIM)),
        "attn_lq1": nrm(ks[15], (N_ATTN_LAYERS, ATTN_HEAD_DIM), 0.1),
        "attn_lk1": nrm(ks[16], (N_ATTN_LAYERS, ATTN_HEAD_DIM), 0.1),
        "attn_lq2": nrm(ks[17], (N_ATTN_LAYERS, ATTN_HEAD_DIM), 0.1),
        "attn_lk2": nrm(ks[18], (N_ATTN_LAYERS, ATTN_HEAD_DIM), 0.1),
        "attn_subln_g": gain(ks[19], (N_ATTN_LAYERS, ATTN_V_DIM)),
        "attn_out_w": nrm(ks[20], (N_ATTN_LAYERS, D_MODEL, D_MODEL), D_MODEL ** -0.5 * out_scale),
        "ffn_up_w": nrm(ks[21], (DEPTH, D_MODEL, 2 * D_FF), D_MODEL ** -0.5),
        "ffn_conv_w": nrm(ks[22], (DEPTH, FFN_CONV, 2 * D_FF), FFN_CONV ** -0.5),
        "ffn_conv_b": nrm(ks[23], (DEPTH, 2 * D_FF), 0.02),
        "ffn_down_w": nrm(ks[24], (DEPTH, D_FF, D_MODEL), D_FF ** -0.5 * out_scale),
    }

def first_block(x, positions, norm_mix_g, norm_ffn_g,
              ssd_in_w, ssd_conv_w, ssd_conv_b, ssd_dt_bias, ssd_a_log, ssd_d,
              ssd_norm_g, ssd_out_w,
              attn_in_w, attn_q_norm_g, attn_k_norm_g, attn_lq1, attn_lk1,
              attn_lq2, attn_lk2, attn_subln_g, attn_out_w,
              ffn_up_w, ffn_conv_w, ffn_conv_b, ffn_down_w):
    cos, sin = rope_tables(positions)
    for i in range(DEPTH):
        j = i // N_MIXERS
        h = rmsnorm(x, norm_mix_g[i])
        if i % N_MIXERS == 0:
            x = x + ssd_mixer(h, ssd_in_w[j], ssd_conv_w[j], ssd_conv_b[j],
                              ssd_dt_bias[j], ssd_a_log[j], ssd_d[j],
                              ssd_norm_g[j], ssd_out_w[j])
        else:
            lambda_init = 0.8 - 0.6 * math.exp(-0.3 * i)
            x = x + diff_attention(h, cos, sin, attn_in_w[j], attn_q_norm_g[j],
                                   attn_k_norm_g[j], attn_lq1[j], attn_lk1[j],
                                   attn_lq2[j], attn_lk2[j], attn_subln_g[j],
                                   attn_out_w[j], lambda_init)
        h = rmsnorm(x, norm_ffn_g[i])
        x = x + conv_ffn(h, ffn_up_w[i], ffn_conv_w[i], ffn_conv_b[i], ffn_down_w[i])
    return x


HEAD_DIM = 64
MOBA_HEADS = D_MODEL // (2 * HEAD_DIM)
NSA_HEADS = D_MODEL // (2 * HEAD_DIM)
NSA_KV_GROUPS = 2
NSA_HPG = NSA_HEADS // NSA_KV_GROUPS
MOBA_BLOCK = 256
MOBA_TOPK = 3
CMP_LEN = 32
CMP_STRIDE = 16
SLC_BLOCK = 64
SLC_TOPN = 16
WINDOW = 512
Q_CHUNK = 128
RMS_EPS = 1e-6
NEG = -1e9
FORCE_BONUS = 1e4

MOBA_W = MOBA_HEADS * HEAD_DIM
NSA_W = NSA_HEADS * HEAD_DIM
KV_W = NSA_KV_GROUPS * HEAD_DIM
SPLITS = [MOBA_W] * 4 + [NSA_W] + [KV_W] * 6 + [3 * NSA_HEADS] + [NSA_W]
D_IN = sum(SPLITS)


def rmsnorm_2(x, g):
    xf = x.astype(jnp.float32)
    y = xf * lax.rsqrt(jnp.mean(xf * xf, axis=-1, keepdims=True) + RMS_EPS)
    return (y * g.astype(jnp.float32)).astype(x.dtype)

def alibi_slopes(n):
    return jnp.asarray(2.0 ** (-8.0 * np.arange(1, n + 1) / n), dtype=jnp.float32)

def cmp_to_slc_matrix(n_cmp, n_slc):
    i = np.arange(n_cmp)[:, None]
    j = np.arange(n_slc)[None, :]
    start = i * CMP_STRIDE
    end = start + CMP_LEN
    ov = (start < (j + 1) * SLC_BLOCK) & (end > j * SLC_BLOCK)
    return jnp.asarray(ov.astype(np.float32))

def compress_blocks(k, pe, w1, w2):
    B, S, G, dh = k.shape
    T = (S - CMP_LEN) // CMP_STRIDE + 1
    idx = np.arange(T)[:, None] * CMP_STRIDE + np.arange(CMP_LEN)[None, :]
    win = k[:, idx] + pe[:, None, :]
    win = win.transpose(0, 3, 1, 2, 4).reshape(B, G, T, CMP_LEN * dh)
    return jax.nn.gelu(win @ w1) @ w2

def hybrid_mixer(h, w_in, w_out, pe_k, pe_v, w_ck1, w_ck2, w_cv1, w_cv2):
    B, S, _ = h.shape
    dh = HEAD_DIM
    NC = S // Q_CHUNK
    NB = -(-S // MOBA_BLOCK)
    KM = min(MOBA_TOPK, NB)
    NBS = S // SLC_BLOCK
    NS = min(SLC_TOPN, NBS)
    T = (S - CMP_LEN) // CMP_STRIDE + 1
    scale = dh ** -0.5

    u = h @ w_in
    offs = np.cumsum(SPLITS)[:-1].tolist()
    (qm, km, vm, zm, qn, kc, vc, ks, vs, kw, vw, gl, zn) = jnp.split(u, offs, axis=-1)

    def heads(a, n):
        return a.reshape(B, S, n, dh).transpose(0, 2, 1, 3)

    pad = NB * MOBA_BLOCK - S
    qm = heads(qm, MOBA_HEADS) * scale
    km = jnp.pad(heads(km, MOBA_HEADS), ((0, 0), (0, 0), (0, pad), (0, 0))).reshape(B, MOBA_HEADS, NB, MOBA_BLOCK, dh)
    vm = jnp.pad(heads(vm, MOBA_HEADS), ((0, 0), (0, 0), (0, pad), (0, 0))).reshape(B, MOBA_HEADS, NB, MOBA_BLOCK, dh)
    kmean = jnp.mean(km, axis=3)

    G = NSA_KV_GROUPS
    qn = qn.reshape(B, S, G, NSA_HPG, dh).transpose(0, 2, 3, 1, 4) * scale
    kc = compress_blocks(kc.reshape(B, S, G, dh), pe_k, w_ck1, w_ck2)
    vc = compress_blocks(vc.reshape(B, S, G, dh), pe_v, w_cv1, w_cv2)
    ks = heads(ks, G).reshape(B, G, NBS, SLC_BLOCK, dh)
    vs = heads(vs, G).reshape(B, G, NBS, SLC_BLOCK, dh)
    kw = jnp.pad(heads(kw, G), ((0, 0), (0, 0), (WINDOW, 0), (0, 0)))
    vw = jnp.pad(heads(vw, G), ((0, 0), (0, 0), (WINDOW, 0), (0, 0)))
    gates = jax.nn.sigmoid(gl.astype(jnp.float32)).reshape(B, S, G, NSA_HPG, 3)

    slope_m = alibi_slopes(MOBA_HEADS)
    slope_n = alibi_slopes(NSA_HEADS).reshape(G, NSA_HPG)
    M = cmp_to_slc_matrix(T, NBS)
    hidx = jnp.arange(MOBA_HEADS)[:, None, None]
    gidx = jnp.arange(G)[:, None, None]

    def chunk(i):
        b = i // NC
        s0 = (i % NC) * Q_CHUNK
        t = s0 + jnp.arange(Q_CHUNK)
        take = lambda a: lax.dynamic_index_in_dim(a, b, 0, keepdims=False)

        q = lax.dynamic_slice_in_dim(take(qm), s0, Q_CHUNK, axis=1)
        Kb, Vb, Kmean = take(km), take(vm), take(kmean)
        cur = s0 // MOBA_BLOCK
        gsc = jnp.einsum('hqd,hnd->hqn', q, Kmean).astype(jnp.float32)
        gsc = jnp.where(jnp.arange(NB) < cur, gsc, NEG)
        _, sel = lax.top_k(gsc, KM)
        sel_ok = jnp.arange(KM) < cur
        k_sel = Kb[hidx, sel]
        v_sel = Vb[hidx, sel]
        s_sel = jnp.einsum('hqd,hqkbd->hqkb', q, k_sel).astype(jnp.float32)
        pos_sel = sel[..., None] * MOBA_BLOCK + jnp.arange(MOBA_BLOCK)
        d_sel = (t[None, :, None, None] - pos_sel).astype(jnp.float32)
        s_sel = jnp.where(sel_ok[None, None, :, None], s_sel - slope_m[:, None, None, None] * d_sel, NEG)
        k_own = lax.dynamic_index_in_dim(Kb, cur, 1, keepdims=False)
        v_own = lax.dynamic_index_in_dim(Vb, cur, 1, keepdims=False)
        s_own = jnp.einsum('hqd,hkd->hqk', q, k_own).astype(jnp.float32)
        d_own = t[:, None] - (cur * MOBA_BLOCK + jnp.arange(MOBA_BLOCK))[None, :]
        s_own = jnp.where(d_own >= 0, s_own - slope_m[:, None, None] * d_own.astype(jnp.float32), NEG)
        logits = jnp.concatenate([s_sel.reshape(MOBA_HEADS, Q_CHUNK, KM * MOBA_BLOCK), s_own], axis=-1)
        p = jax.nn.softmax(logits, axis=-1).astype(v_own.dtype)
        p_sel = p[..., :KM * MOBA_BLOCK].reshape(MOBA_HEADS, Q_CHUNK, KM, MOBA_BLOCK)
        o_m = (jnp.einsum('hqkb,hqkbd->hqd', p_sel, v_sel)
               + jnp.einsum('hqb,hbd->hqd', p[..., KM * MOBA_BLOCK:], v_own))
        o_m = o_m.transpose(1, 0, 2).reshape(Q_CHUNK, MOBA_W)

        qg = lax.dynamic_slice_in_dim(take(qn), s0, Q_CHUNK, axis=2)
        kcb, vcb = take(kc), take(vc)
        s_c = jnp.einsum('gjqd,gtd->gjqt', qg, kcb).astype(jnp.float32)
        d_c = t[:, None] - (jnp.arange(T) * CMP_STRIDE + CMP_LEN - 1)[None, :]
        ok_c = d_c >= 0
        s_c = jnp.where(ok_c, s_c - slope_n[:, :, None, None] * d_c.astype(jnp.float32), NEG)
        p_c = jax.nn.softmax(s_c, axis=-1) * ok_c
        o_c = jnp.einsum('gjqt,gtd->gjqd', p_c.astype(vcb.dtype), vcb)
        imp = jnp.einsum('gjqt,tn->gqn', p_c, M)
        blk = t // SLC_BLOCK
        jn = jnp.arange(NBS)[None, :]
        forced = (jn == 0) | (jn == blk[:, None]) | (jn == blk[:, None] - 1)
        imp = jnp.where(forced, FORCE_BONUS, imp)
        imp = jnp.where(jn <= blk[:, None], imp, NEG)
        _, sidx = lax.top_k(imp, NS)
        s_valid = sidx <= blk[None, :, None]
        ksb = take(ks)[gidx, sidx]
        vsb = take(vs)[gidx, sidx]
        s_s = jnp.einsum('gjqd,gqnbd->gjqnb', qg, ksb).astype(jnp.float32)
        d_s = t[None, :, None, None] - (sidx[..., None] * SLC_BLOCK + jnp.arange(SLC_BLOCK))
        ok_s = (d_s >= 0) & s_valid[..., None]
        s_s = jnp.where(ok_s[:, None], s_s - slope_n[:, :, None, None, None] * d_s[:, None].astype(jnp.float32), NEG)
        p_s = jax.nn.softmax(s_s.reshape(G, NSA_HPG, Q_CHUNK, NS * SLC_BLOCK), axis=-1)
        p_s = p_s.reshape(G, NSA_HPG, Q_CHUNK, NS, SLC_BLOCK).astype(vsb.dtype)
        o_s = jnp.einsum('gjqnb,gqnbd->gjqd', p_s, vsb)
        kwb = lax.dynamic_slice_in_dim(take(kw), s0, WINDOW + Q_CHUNK, axis=1)
        vwb = lax.dynamic_slice_in_dim(take(vw), s0, WINDOW + Q_CHUNK, axis=1)
        s_w = jnp.einsum('gjqd,gkd->gjqk', qg, kwb).astype(jnp.float32)
        pos_w = s0 - WINDOW + jnp.arange(WINDOW + Q_CHUNK)
        d_w = t[:, None] - pos_w[None, :]
        ok_w = (d_w >= 0) & (d_w < WINDOW) & (pos_w >= 0)[None, :]
        s_w = jnp.where(ok_w, s_w - slope_n[:, :, None, None] * d_w.astype(jnp.float32), NEG)
        p_w = jax.nn.softmax(s_w, axis=-1).astype(vwb.dtype)
        o_w = jnp.einsum('gjqk,gkd->gjqd', p_w, vwb)
        g = lax.dynamic_slice_in_dim(take(gates), s0, Q_CHUNK, axis=0).transpose(1, 2, 0, 3)
        g = g.astype(o_c.dtype)
        o_n = g[..., 0:1] * o_c + g[..., 1:2] * o_s + g[..., 2:3] * o_w
        o_n = o_n.transpose(2, 0, 1, 3).reshape(Q_CHUNK, NSA_W)
        return o_m, o_n

    o_m, o_n = lax.map(chunk, jnp.arange(B * NC))
    o_m = o_m.reshape(B, S, MOBA_W)
    o_n = o_n.reshape(B, S, NSA_W)
    y = jnp.concatenate([o_m * jax.nn.silu(zm), o_n * jax.nn.silu(zn)], axis=-1)
    return y @ w_out

def second_inputs(seed: int = 0) -> dict:
    key = jax.random.key(seed)
    ks = jax.random.split(key, 16)
    L, D, dh = DEPTH, D_MODEL, HEAD_DIM
    nrm = lambda k, shape, s: jax.random.normal(k, shape, jnp.float32) * s
    return {
        "x": nrm(ks[0], (BATCH, SEQ, D), 1.0),
        "c": nrm(ks[1], (BATCH, D), 1.0),
        "w_ada": nrm(ks[2], (L, D, 3 * D), D ** -0.5),
        "b_ada": nrm(ks[3], (L, 3 * D), 0.01),
        "g_pre": 1.0 + nrm(ks[4], (L, D), 0.1),
        "g_post": 1.0 + nrm(ks[5], (L, D), 0.1),
        "w_in": nrm(ks[6], (L, D, D_IN), D ** -0.5),
        "w_out": nrm(ks[7], (L, D, D), D ** -0.5),
        "pe_k": nrm(ks[8], (L, CMP_LEN, dh), 0.1),
        "pe_v": nrm(ks[9], (L, CMP_LEN, dh), 0.1),
        "w_ck1": nrm(ks[10], (L, CMP_LEN * dh, dh), (CMP_LEN * dh) ** -0.5),
        "w_ck2": nrm(ks[11], (L, dh, dh), dh ** -0.5),
        "w_cv1": nrm(ks[12], (L, CMP_LEN * dh, dh), (CMP_LEN * dh) ** -0.5),
        "w_cv2": nrm(ks[13], (L, dh, dh), dh ** -0.5),
    }

def second_block(x, c, w_ada, b_ada, g_pre, g_post, w_in, w_out, pe_k, pe_v, w_ck1, w_ck2, w_cv1, w_cv2):
    D = x.shape[-1]
    cs = jax.nn.silu(c)
    for l in range(DEPTH):
        mod = cs @ w_ada[l] + b_ada[l]
        shift, scale, gate = mod[:, None, :D], mod[:, None, D:2 * D], mod[:, None, 2 * D:]
        h = rmsnorm_2(x, g_pre[l]) * (1.0 + scale) + shift
        y = hybrid_mixer(h, w_in[l], w_out[l], pe_k[l], pe_v[l], w_ck1[l], w_ck2[l], w_cv1[l], w_cv2[l])
        x = x + gate * rmsnorm_2(y, g_post[l])
    return x


def setup_inputs(seed=0):
    out = dict(first_inputs(seed))
    for name, value in second_inputs(seed + 1).items():
        if name != "x":
            out[name + "_2"] = value
    return out


def reference(
    x, positions, norm_mix_g, norm_ffn_g, ssd_in_w, ssd_conv_w, ssd_conv_b, ssd_dt_bias,
    ssd_a_log, ssd_d, ssd_norm_g, ssd_out_w, attn_in_w, attn_q_norm_g, attn_k_norm_g, attn_lq1,
    attn_lk1, attn_lq2, attn_lk2, attn_subln_g, attn_out_w, ffn_up_w, ffn_conv_w, ffn_conv_b,
    ffn_down_w, c_2, w_ada_2, b_ada_2, g_pre_2, g_post_2, w_in_2, w_out_2, pe_k_2, pe_v_2,
    w_ck1_2, w_ck2_2, w_cv1_2, w_cv2_2,
):
    x = first_block(
        x, positions, norm_mix_g, norm_ffn_g, ssd_in_w, ssd_conv_w, ssd_conv_b, ssd_dt_bias,
        ssd_a_log, ssd_d, ssd_norm_g, ssd_out_w, attn_in_w, attn_q_norm_g, attn_k_norm_g,
        attn_lq1, attn_lk1, attn_lq2, attn_lk2, attn_subln_g, attn_out_w, ffn_up_w, ffn_conv_w,
        ffn_conv_b, ffn_down_w,
    )
    return second_block(
        x, c_2, w_ada_2, b_ada_2, g_pre_2, g_post_2, w_in_2, w_out_2, pe_k_2, pe_v_2, w_ck1_2,
        w_ck2_2, w_cv1_2, w_cv2_2,
    )


_drawn_inputs = setup_inputs


def setup_inputs(seed=0):
    import zlib

    import numpy as np

    out = dict(_drawn_inputs(seed))
    spreads = {}
    factors = {'ssd_conv_b': 3.223,
     'attn_q_norm_g': 3.396,
     'attn_k_norm_g': 3.476,
     'attn_lk1': 3.623,
     'attn_lq2': 2.825,
     'attn_lk2': 5.681,
     'attn_subln_g': 3.458,
     'ffn_conv_b': 4.284,
     'b_ada_2': 3.351,
     'pe_k_2': 25.615,
     'pe_v_2': 3.009}
    for name, (base, spread) in spreads.items():
        noise = np.random.default_rng([zlib.crc32(name.encode()), seed]).standard_normal(out[name].shape)
        drawn = base * np.exp(spread * noise) if base else spread * noise
        out[name] = __import__('jax').numpy.asarray(drawn.astype(out[name].dtype))
    for name, factor in factors.items():
        out[name] = (out[name] * factor).astype(out[name].dtype)
    return out
```

```python
from contextlib import ExitStack
import math
import numpy as np

import concourse.bass as bass
from concourse import mybir

F32 = mybir.dt.float32
F32R = mybir.dt.float32r
I32 = mybir.dt.int32
ALU = mybir.AluOpType
ACT = mybir.ActivationFunctionType
AX = mybir.AxisListType

P = 128
S = 256
TT = S // P
D = 1024
KD = D // P
DEPTH = 2
SSD_INNER, SSD_HEADS, SSD_GROUPS, SSD_P, SSD_N, SSD_TAPS = 2048, 32, 4, 64, 128, 4
XS_TILES = SSD_INNER // P
CONV_TILES = XS_TILES + 2 * SSD_GROUPS
A_HEADS, HD = 8, 64
D_FF, FFN_TAPS = 2816, 3
FF_TILES = D_FF // P
ROPE_DIM, ROPE_THETA = 16, 500000.0
CHUNK = 64
LAMBDA_INIT = 0.8 - 0.6 * math.exp(-0.3 * 1)
H_HEADS, H_GROUPS = 8, 2
CMP_LEN, CMP_STRIDE = 32, 16
CMP_T = (S - CMP_LEN) // CMP_STRIDE + 1
HPG = H_HEADS // H_GROUPS
CMP_PAIRS = CMP_LEN * HD // P
EPS = 1e-6
NEG = -1e9
FAR = -1e30
VSG = 2 * P + 3 * H_HEADS
UNIT_MAX = KD // 2 * VSG
RAW_MAX = 2 * UNIT_MAX
TWO_PI_PARTS = (6.28125, 0.0019340515136718750, 1.2556240e-06)

PARAMS = {}


def _param(name, n):
    PARAMS[name] = (PARAMS.get("_n", 0), n)
    PARAMS["_n"] = PARAMS.get("_n", 0) + n


for _name, _n in (("mix_g", DEPTH * KD), ("ffn_g", DEPTH * KD),
                  ("ssd_conv", (SSD_TAPS + 1) * CONV_TILES), ("ssd_norm_g", XS_TILES), ("ssd_d", XS_TILES),
                  ("dt_bias", 1), ("a_log", 1),
                  ("ffn_conv", DEPTH * (FFN_TAPS + 1) * 2 * FF_TILES),
                  ("q_g", 1), ("k_g", 1), ("subln_g", 1), ("lam", 4 * HD),
                  ("c", KD), ("b_ada", DEPTH * 3 * KD), ("g_pre", DEPTH * KD), ("g_post", DEPTH * KD)):
    _param(_name, _n)
NPARAMS = PARAMS["_n"]

CONSTS = {}


def _const(name, n):
    CONSTS[name] = (CONSTS.get("_n", 0), n)
    CONSTS["_n"] = CONSTS.get("_n", 0) + n


for _name, _n in (("ident", P), ("ones", P), ("block_ones", P), ("rope_perm", P), ("inv_freq", 1),
                  ("chunk_mask", S), ("causal_far", P), ("cmp_bias", TT * H_HEADS * CMP_T), ("cmp_ok", TT * CMP_T)):
    _const(_name, _n)
NCONSTS = CONSTS["_n"]


def constants():
    c = np.zeros((P, NCONSTS), np.float32)

    def put(name, a):
        at, n = CONSTS[name]
        c[:, at:at + n] = np.asarray(a, np.float32).reshape(P, n)

    r = np.arange(P)
    put("ident", np.eye(P))
    put("ones", np.ones((P, P)))
    put("block_ones", (r[:, None] // HD) == (r[None, :] // HD))
    perm = np.zeros((P, P))
    half = ROPE_DIM // 2
    for base in (0, HD):
        for i in range(half):
            perm[base + half + i, base + i] = -1.0
            perm[base + i, base + half + i] = 1.0
    put("rope_perm", perm)
    inv = np.float32(ROPE_THETA) ** (-np.arange(0, ROPE_DIM, 2, dtype=np.float32) / np.float32(ROPE_DIM))
    col = np.zeros(P)
    for base in (0, HD):
        col[base:base + half] = inv
        col[base + half:base + 2 * half] = inv
    put("inv_freq", col)
    chunk = np.where((r[None, :] // CHUNK) <= (r[:, None] // CHUNK), 0.0, FAR)
    put("chunk_mask", np.concatenate([np.zeros((P, P)), chunk], 1))
    put("causal_far", np.where(r[None, :] >= r[:, None], 0.0, FAR))
    slopes = (2.0 ** (-8.0 * np.arange(1, H_HEADS + 1) / H_HEADS)).astype(np.float32)
    t = np.arange(S).reshape(TT, P)
    ends = np.arange(CMP_T) * CMP_STRIDE + CMP_LEN - 1
    dist = (t[:, :, None] - ends).astype(np.float32)
    bias = np.where(dist[:, :, None, :] >= 0, -slopes[:, None] * dist[:, :, None, :], NEG)
    put("cmp_bias", bias.transpose(1, 0, 2, 3))
    put("cmp_ok", (dist >= 0).transpose(1, 0, 2))
    far = (P + r[:, None] - r[None, :]).astype(np.float32)
    own = (r[:, None] - r[None, :]).astype(np.float32)
    alibi = np.zeros((P, H_HEADS, S), np.float32)
    for h in range(H_HEADS):
        alibi[:, h, 0:P] = -slopes[h] * far
        alibi[:, h, P:S] = np.where(own >= 0, -slopes[h] * own, NEG)
    return c, alibi.reshape(P, H_HEADS * S)


class Queue:

    def __init__(self, engine, sem):
        self.engine, self.sem, self.count, self.seen = engine, sem, 0, {}

    def wait(self, tickets):
        for t in tickets:
            if t is None:
                continue
            sem, value = t
            if self.seen.get(id(sem), 0) < value:
                self.seen[id(sem)] = value
                self.engine.wait_ge(sem, value)

    def do(self, emit, after=(), signal=True):
        self.wait(after)
        ins = emit(self.engine)
        if not signal:
            return None
        self.count += 1
        ins.then_inc(self.sem, 1)
        return (self.sem, self.count)

    def last(self):
        return (self.sem, self.count) if self.count else None


class Ring:

    def __init__(self, slots):
        self.slots, self.free, self.at = slots, [[] for _ in slots], 0

    def take(self):
        for _ in self.slots:
            n = self.at
            self.at = (self.at + 1) % len(self.slots)
            if self.free[n] is not None:
                after, self.free[n] = self.free[n], None
                return n, self.slots[n], after
        raise AssertionError("no free slot")

    def give(self, n, tickets):
        assert self.free[n] is None
        self.free[n] = list(tickets)


class Split:

    def __init__(self, hi, lo, width):
        self.hi, self.lo, self.width, self.hi_t, self.lo_t = hi, lo, width, {}, {}

    def part(self, which, k, a=0, b=None):
        b = self.width if b is None else b
        return (self.hi if which == "hi" else self.lo)[:, k * self.width + a:k * self.width + b]


def build_program(nc, d):
    ctx = ExitStack()
    with ctx:
        def sb(name, shape, dt=F32):
            return ctx.enter_context(nc.sbuf_tensor(name, shape, dt))

        def sem(name):
            return ctx.enter_context(nc.semaphore(name))

        params_sb = sb("params_sb", [P, NPARAMS])
        consts_sb = sb("consts_sb", [P, NCONSTS])
        xT = sb("xT", [P, KD * S])
        sq = sb("sq", [P, KD * S])
        h_hi, h_lo = sb("h_hi", [P, KD * S], F32R), sb("h_lo", [P, KD * S], F32R)
        GU_SLOTS = 6
        g_hi, g_lo = sb("g_hi", [P, GU_SLOTS * S], F32R), sb("g_lo", [P, GU_SLOTS * S], F32R)
        RAW_SLOTS, SPLIT_SLOTS = 3, 3
        raw_sb = sb("raw_sb", [P, RAW_SLOTS * RAW_MAX])
        w_hi = sb("w_hi", [P, SPLIT_SLOTS * UNIT_MAX], F32R)
        w_lo = sb("w_lo", [P, SPLIT_SLOTS * UNIT_MAX], F32R)
        std_sb = sb("std_sb", [P, S])
        rstd_sb = sb("rstd_sb", [P, S])
        mod_sb = sb("mod_sb", [P, 3 * KD])
        cs_sb = sb("cs_sb", [P, KD])
        small = sb("small", [P, 64])
        ARENA = 20 * 1024
        arena = sb("arena", [P, ARENA])
        banks = Ring([ctx.enter_context(nc.psum_tensor(f"bank{i}", [P, 512], F32)) for i in range(8)])

        def par(name, at=0, n=1, rows=P):
            o = PARAMS[name][0] + at
            return params_sb[0:rows, o:o + n]

        def con(name, at=0, n=None, rows=P):
            o, size = CONSTS[name]
            n = size if n is None else n
            return consts_sb[0:rows, o + at:o + at + n]

        T, V, A, L = (Queue(engine, sem(n)) for engine, n in (
            (nc.tensor, "s_pe"), (nc.vector, "s_dve"), (nc.scalar, "s_act"), (nc.sync, "s_sp")))
        raw_sems = [sem(f"s_raw{i}") for i in range(RAW_SLOTS)]
        s_params, s_consts, s_x, s_pos, s_alibi, s_out = (sem(n) for n in (
            "s_params", "s_consts", "s_x", "s_pos", "s_alibi", "s_out"))
        s_cmp = [sem(f"s_cmp{i}") for i in range(DEPTH)]

        def load(out, src, s, value, after=()):
            L.wait(after)
            L.engine.dma_start(out, src).then_inc(s, 16)
            return (s, value)

        class Arena:
            def __init__(self):
                self.at = 0

            def get(self, n, shape=None):
                a = arena[:, self.at:self.at + n]
                self.at += n
                assert self.at <= ARENA, self.at
                return a

        plan = []

        def plan_tiles(name, n, units, size, split=True):
            for i in range(n):
                plan.append((name, i, units, size, split))

        def plan_ffn(layer):
            for i in range(FF_TILES + 2):
                if i < FF_TILES:
                    plan.append((f"w_up{layer}", i, 2, KD * P, True))
                if i % 2 and i >= 3:
                    plan.append((f"w_down{layer}", (i - 3) // 2, 2, D, True))

        plan_tiles("w_dt", 1, 1, KD * P)
        plan_tiles("w_ssd_in", (CONV_TILES + XS_TILES) // 2, 2, KD * P)
        plan_tiles("w_ssd_out", XS_TILES // 2, 2, D)
        plan_ffn(0)
        plan_tiles("w_attn_in", 2 * KD // 2, 2, KD * P)
        plan_tiles("w_attn_v", D // S, 2, KD * P)
        plan_tiles("w_ada0", 3 * KD // 2, 1, 2 * KD * P, split=False)
        plan_tiles("w_attn_out", KD // 2, 2, KD * P)
        plan_ffn(1)
        for n in range(DEPTH):
            plan_tiles(f"w_kv{n}", 2, 2, KD * P)
            plan_tiles(f"w_vsg{n}", 1, 2, KD // 2 * VSG)
            plan_tiles(f"w_vm{n}", 2, 2, KD * P)
            plan_tiles(f"w_qz{n}", 10, 2, KD * P)
            if n == 0:
                plan_tiles("w_ada1", 3 * KD // 2, 1, 2 * KD * P, split=False)
            plan_tiles(f"w_out{n}", KD // 2, 2, KD * P)

        class Stream:
            def __init__(self):
                self.loaded = self.used_chunk = 0
                self.raw_free = [[] for _ in range(RAW_SLOTS)]
                self.raw_t = {}
                self.units = []
                for i, (_, _, units, _, split) in enumerate(plan):
                    if split:
                        self.units += [(i, u) for u in range(units)]
                self.prepared = self.used = 0
                self.split_free = [[] for _ in range(SPLIT_SLOTS)]
                self.split_t = {}

            def load_ahead(self):
                while self.loaded < len(plan) and self.raw_free[self.loaded % RAW_SLOTS] is not None:
                    i = self.loaded
                    name, n, units, size, _ = plan[i]
                    slot = i % RAW_SLOTS
                    self.raw_t[i] = load(raw_sb[:, slot * RAW_MAX:slot * RAW_MAX + units * size], d[name][n],
                                         raw_sems[slot], 16 * (i // RAW_SLOTS + 1), self.raw_free[slot])
                    self.raw_free[slot] = None
                    self.loaded += 1

            def prepare(self, upto):
                while self.prepared < min(upto, len(self.units)):
                    u = self.prepared
                    chunk, part = self.units[u]
                    if chunk not in self.raw_t or self.split_free[u % SPLIT_SLOTS] is None:
                        return
                    _, _, units, size, _ = plan[chunk]
                    slot = u % SPLIT_SLOTS
                    raw_at = (chunk % RAW_SLOTS) * RAW_MAX + part * size
                    raw = raw_sb[:, raw_at:raw_at + size]
                    hi = w_hi[:, slot * UNIT_MAX:slot * UNIT_MAX + size]
                    lo = w_lo[:, slot * UNIT_MAX:slot * UNIT_MAX + size]
                    t_hi = A.do(lambda e, o=hi, i=raw: e.activation(o, i, ACT.Copy),
                                [self.raw_t[chunk]] + self.split_free[slot])
                    t_lo = V.do(lambda e, o=lo, i=raw, h=hi: e.tensor_tensor(o, i, h.bitcast(F32), ALU.subtract),
                                [self.raw_t[chunk], t_hi] + self.split_free[slot])
                    self.split_t[u] = (t_hi, t_lo, hi, lo)
                    self.split_free[slot] = None
                    if part == units - 1:
                        self.raw_free[chunk % RAW_SLOTS] = [t_lo]
                        self.load_ahead()
                    self.prepared += 1

            def unit(self, name):
                u = self.used
                assert plan[self.units[u][0]][0] == name, (name, plan[self.units[u][0]])
                self.prepare(u + 2)
                assert u in self.split_t
                self.used += 1
                return u, self.split_t[u]

            def done(self, u, ticket):
                self.split_free[u % SPLIT_SLOTS] = [ticket]
                self.prepare(self.used + 1)

            def raw_chunk(self, i):
                slot = i % RAW_SLOTS
                return raw_sb[:, slot * RAW_MAX:(slot + 1) * RAW_MAX], self.raw_t[i]

            def raw_done(self, i, ticket):
                self.raw_free[i % RAW_SLOTS] = [ticket]
                self.load_ahead()

        W = Stream()

        def mm(out, lhsT, rhs, start, stop, after=(), signal=False):
            return T.do(lambda e: e.matmul(out, lhsT, rhs, start=start, stop=stop, skip_group_check=True),
                        after, signal)

        delayed = []

        def later(n, fn):
            delayed.append([n, fn])

        def tick():
            ready = [x for x in delayed if x[0] <= 1]
            for x in delayed:
                x[0] -= 1
            delayed[:] = [x for x in delayed if x not in ready]
            for _, fn in ready:
                fn()

        def flush():
            while delayed:
                tick()

        def project(name, tiles, k_tiles, acts, epilogue):
            per = KD
            for m in tiles:
                n, bank, free = banks.take()
                out = bank[:, 0:S]
                first = True
                for part in range(k_tiles // per):
                    u, (t_hi, t_lo, hi, lo) = W.unit(name)
                    for k in range(per):
                        kk = part * per + k
                        wh, wl = hi[:, k * P:(k + 1) * P], lo[:, k * P:(k + 1) * P]
                        mm(out, wh, acts.part("hi", kk), first, False,
                           [t_hi, acts.hi_t.get(kk)] + (free if first else []))
                        first = False
                        mm(out, wh, acts.part("lo", kk), False, False, [acts.lo_t.get(kk)])
                        end = kk == k_tiles - 1
                        t = mm(out, wl, acts.part("hi", kk), False, end, [t_lo], signal=k == per - 1)
                    W.done(u, t)
                banks.give(n, epilogue(m, out, t))
                tick()

        class OuterProjection:

            def __init__(self, name, k_tiles):
                self.name, self.k_tiles, self.k = name, k_tiles, 0
                self.banks = [banks.take() for _ in range(KD // 2)]

            def step(self, a_hi, a_lo, t_a_hi, t_a_lo):
                u, (t_hi, t_lo, hi, lo) = W.unit(self.name)
                self.t = []
                last = self.k == self.k_tiles - 1
                for m in range(KD):
                    n, bank, free = self.banks[m // 2]
                    out = bank[:, (m % 2) * S:(m % 2 + 1) * S]
                    wh, wl = hi[:, m * P:(m + 1) * P], lo[:, m * P:(m + 1) * P]
                    mm(out, wh, a_hi, self.k == 0 and m % 2 == 0, False,
                       [t_hi, t_a_hi] + (free if self.k == 0 else []))
                    mm(out, wh, a_lo, False, False, [t_a_lo])
                    self.t.append(mm(out, wl, a_hi, False, last, [t_lo], signal=m % 2 == 1))
                W.done(u, self.t[-1])
                self.k += 1
                return self.t[-1]

            def finish(self, epilogue):
                assert self.k == self.k_tiles
                for b, (n, bank, _) in enumerate(self.banks):
                    tickets = []
                    for j in range(2):
                        tickets += epilogue(2 * b + j, bank[:, j * S:(j + 1) * S], self.t[2 * b + 1])
                    banks.give(n, tickets)
                    tick()

        def project_rows(name, width, acts, epilogue):
            taken = [banks.take() for _ in range(TT)]
            half = KD // 2
            for part in range(2):
                u, (t_hi, t_lo, hi, lo) = W.unit(name)
                for tt in range(TT):
                    n, bank, free = taken[tt]
                    out = bank[:, 0:width]
                    for k in range(half):
                        kk = part * half + k
                        wh, wl = hi[:, k * width:(k + 1) * width], lo[:, k * width:(k + 1) * width]
                        ah, al = (acts.part(w, kk, tt * P, (tt + 1) * P) for w in ("hi", "lo"))
                        mm(out, ah, wh, kk == 0, False,
                           [t_hi, acts.hi_t.get(kk)] + (free if kk == 0 else []))
                        mm(out, ah, wl, False, False, [t_lo])
                        t = mm(out, al, wh, False, kk == KD - 1, [acts.lo_t.get(kk)], signal=k == half - 1)
                    if part == 1:
                        taken[tt] = (n, bank, t)
                W.done(u, t)
            for tt, (n, bank, t) in enumerate(taken):
                banks.give(n, epilogue(tt, bank, t))
            tick()

        def split_tile(dst, k, full, t_full, free=()):
            hi, lo = dst.part("hi", k), dst.part("lo", k)
            t = A.do(lambda e: e.activation(hi, full, ACT.Copy), [t_full] + list(free))
            dst.hi_t[k] = t
            dst.lo_t[k] = V.do(lambda e: e.tensor_tensor(lo, full, hi.bitcast(F32), ALU.subtract),
                                  [t, t_full] + list(free))
            return [dst.hi_t[k], dst.lo_t[k]]

        H = Split(h_hi, h_lo, S)
        gu_ring = Ring(list(range(GU_SLOTS)))

        def tile(buf, k, a=0, b=S):
            return buf[:, k * S + a:k * S + b]

        t_x = load(xT[:, :], d["x"], s_x, 16)
        t_params = load(params_sb[:, :], d["params"], s_params, 16)
        t_consts = load(consts_sb[:, :], d["consts"], s_consts, 16)
        W.load_ahead()

        eps_col = small[:, 0:1]
        t_eps = V.do(lambda e: e.memset(eps_col, EPS))
        half_pi = math.pi / 2

        ones = con("ones")

        def square_sums(n_tiles, src, ready):
            n, bank, free = banks.take()
            for k in range(n_tiles):
                t = A.do(lambda e, k=k: e.activation(tile(sq, k), tile(src, k), ACT.Square), ready(k))
                t = mm(bank[:, 0:S], ones, tile(sq, k), k == 0, k == n_tiles - 1,
                       [t, t_consts] + (free if k == 0 else []), signal=True)
            return n, bank, t

        def rstd_of(bank, t_bank, count, out=None, width=S):
            out = rstd_sb[:, 0:width] if out is None else out
            std = std_sb[:, 0:width]
            t_std = A.do(lambda e: e.activation(std, bank[:, 0:width], ACT.Sqrt, bias=eps_col,
                                                scale=1.0 / count), [t_bank, t_eps, V.last()])
            return V.do(lambda e: e.reciprocal(out, std), [t_std]), t_std

        def norm_into_h(sums, gain, shift=None):
            n, bank, t_bank = sums
            t_rstd, t_free = rstd_of(bank, t_bank, D)
            banks.give(n, [t_free])
            for k in range(KD):
                t = V.do(lambda e, k=k: e.scalar_tensor_tensor(tile(sq, k), tile(xT, k), gain(k),
                                                               rstd_sb[:, :], ALU.mult, ALU.mult),
                         [t_rstd, t_params, T.last()])
                if shift is None:
                    split_tile(H, k, tile(sq, k), t)
                else:
                    H.hi_t[k] = A.do(lambda e, k=k: e.activation(H.part("hi", k), tile(sq, k), ACT.Identity,
                                                                 bias=shift(k)), [t])
                    H.lo_t[k] = V.do(lambda e, k=k: e.scalar_tensor_tensor(
                        H.part("lo", k), tile(sq, k), shift(k), H.part("hi", k).bitcast(F32),
                        ALU.add, ALU.subtract), [t, H.hi_t[k]])

        def residual_epilogue(sums):
            def epilogue(m, bank, t):
                t_add = V.do(lambda e: e.tensor_tensor(tile(xT, m), bank, tile(xT, m), ALU.add), [t])
                t_sq = A.do(lambda e: e.activation(tile(sq, m), tile(xT, m), ACT.Square), [t_add])

                def add_up():
                    n, sums_bank, free, _ = sums
                    sums[3] = mm(sums_bank[:, 0:S], ones, tile(sq, m), m == 0, m == KD - 1,
                                 [t_sq] + (free if m == 0 else []), signal=True)
                later(1, add_up)
                return [t_add]
            return epilogue

        def take_sums():
            n, bank, free = banks.take()
            return [n, bank, free, None]

        sums = square_sums(KD, xT, lambda k: [t_x])
        norm_into_h(sums, lambda k: par("mix_g", k))

        ar = Arena()
        z_sb = ar.get(XS_TILES * S)
        xs_sb = ar.get(XS_TILES * S)
        b_sb = ar.get(SSD_GROUPS * S)
        c_sb = ar.get(SSD_GROUPS * S)
        acc_ring = Ring([ar.get(S) for _ in range(3)])
        cb_sb = ar.get(3 * P)
        tok = ar.get(5 * SSD_HEADS)
        dt_w = ar.get(5 * P + 6 * S)
        hT = SSD_HEADS
        stack = dt_w[0:hT, 0:5 * P]
        dts, e_ab, u_ab, w_ab, acs = (dt_w[0:hT, 5 * P + i * S:5 * P + (i + 1) * S] for i in range(5))
        dA = dt_w[0:hT, 5 * P + 5 * S:5 * P + 6 * S]
        state = {}

        def dt_epilogue(_, bank, t):
            step = lambda fn, after=(): V.do(fn, [V.last()] + list(after))
            t_v = step(lambda e: e.tensor_scalar(dts, bank[0:hT, 0:S], par("dt_bias", rows=hT), None, ALU.add), [t])
            step(lambda e: e.tensor_scalar(w_ab, dts, -1.0, None, ALU.mult))
            step(lambda e: e.tensor_tensor(w_ab, dts, w_ab, ALU.max))
            t_e = A.do(lambda e: e.activation(e_ab, w_ab, ACT.Exp, scale=-1.0), [V.last()])
            step(lambda e: e.tensor_scalar(u_ab, e_ab, 1.0, None, ALU.add), [t_e])
            t_ln = A.do(lambda e: e.activation(acs, u_ab, ACT.Ln), [V.last()])
            t_a = A.do(lambda e: e.activation(small[0:hT, 1:2], par("a_log", rows=hT), ACT.Exp), [t_params])
            step(lambda e: e.scalar_tensor_tensor(e_ab, u_ab, -1.0, e_ab, ALU.add, ALU.subtract))
            step(lambda e: e.reciprocal(u_ab, u_ab), [t_ln])
            step(lambda e: e.tensor_tensor(e_ab, e_ab, u_ab, ALU.mult))
            step(lambda e: e.tensor_tensor(acs, acs, e_ab, ALU.subtract), [t_ln])
            step(lambda e: e.scalar_tensor_tensor(dts, dts, 0.0, acs, ALU.max, ALU.add))
            step(lambda e: e.tensor_scalar(dA, dts, small[0:hT, 1:2], -1.0, ALU.mult, ALU.mult), [t_a])
            step(lambda e: e.memset(w_ab, 1.0))
            for tt in range(TT):
                step(lambda e, tt=tt: e.tensor_tensor_scan(acs[:, tt * P:(tt + 1) * P], w_ab[:, tt * P:(tt + 1) * P],
                                                           dA[:, tt * P:(tt + 1) * P], 0.0, ALU.mult, ALU.add))
            step(lambda e: e.tensor_copy(stack[:, 0:S], dts))
            step(lambda e: e.tensor_scalar(stack[:, S:2 * S], acs, -1.0, None, ALU.mult))
            t_stack = step(lambda e: e.tensor_scalar(stack[:, 2 * S:2 * S + P], acs[:, 0:P], -1.0, acs[:, P - 1:P],
                                                     ALU.mult, ALU.add))
            state["acs_hi"] = A.do(lambda e: e.activation(acs_hi[:, :], acs, ACT.Copy), [t_stack])
            state["acs"] = V.do(lambda e: e.tensor_tensor(acs_lo[:, :], acs, acs_hi[:, :].bitcast(F32), ALU.subtract),
                                [state["acs_hi"]])

            def turn():
                n, b, free = banks.take()
                for i in range(5):
                    t = T.do(lambda e, i=i: e.transpose(b[:, i * hT:(i + 1) * hT], stack[:, i * P:(i + 1) * P],
                                                        con("ident", 0, hT, hT)),
                             [t_stack, t_consts] + free, signal=True)
                state["tok"] = V.do(lambda e: e.tensor_copy(tok, b[:, 0:5 * hT]), [t])
                banks.give(n, [state["tok"]])
            later(3, turn)
            return [t_v]

        acs_hi = sb("acs_hi", [hT, S], F32R)
        acs_lo = sb("acs_lo", [hT, S], F32R)
        sel = sb("sel", [hT, hT * 2], F32R)
        mask_r = sb("mask_r", [P, P], F32R)
        ident_r = sb("ident_r", [P, P], F32R)
        t_sel = A.do(lambda e: e.activation(sel[:, 0:hT], con("ident", 0, hT, hT), ACT.Copy), [t_consts])
        t_mask = A.do(lambda e: e.activation(mask_r[:, :], con("causal_far"), ACT.Copy), [t_consts])
        t_ident_r = A.do(lambda e: e.activation(ident_r[:, :], con("ident"), ACT.Copy), [t_consts])

        def conv_taps(bank, t, taps, weight, bias):
            n, acc, free = acc_ring.take()
            t_acc = A.do(lambda e: e.activation(acc, bank[:, 0:S], ACT.Identity, bias=bias,
                                                scale=weight(taps - 1)), [t, t_params] + free)
            for back in range(1, taps):
                t_acc = V.do(lambda e, back=back: e.scalar_tensor_tensor(
                    acc[:, back:S], bank[:, 0:S - back], weight(taps - 1 - back), acc[:, back:S],
                    ALU.mult, ALU.add), [t_acc])
            return n, acc, t_acc

        conv_out = ([b_sb[:, g * S:(g + 1) * S] for g in range(SSD_GROUPS)]
                    + [c_sb[:, g * S:(g + 1) * S] for g in range(SSD_GROUPS)]
                    + [tile(xs_sb, k) for k in range(XS_TILES)])
        conv_col = ([XS_TILES + g for g in range(2 * SSD_GROUPS)] + list(range(XS_TILES)))
        conv_t = {}

        def ssd_in_epilogue(m, bank, t):
            if m < CONV_TILES:
                col = conv_col[m]
                n, acc, t_acc = conv_taps(bank, t, SSD_TAPS, lambda k: par("ssd_conv", k * CONV_TILES + col),
                                          par("ssd_conv", SSD_TAPS * CONV_TILES + col))
                conv_t[m] = A.do(lambda e: e.activation(conv_out[m], acc, ACT.Silu), [t_acc])
                acc_ring.give(n, [conv_t[m]])
                return [t_acc]
            k = m - CONV_TILES
            conv_t[m] = A.do(lambda e: e.activation(tile(z_sb, k), bank[:, 0:S], ACT.Silu), [t])
            return [conv_t[m]]

        project("w_dt", [0], KD, H, dt_epilogue)
        project("w_ssd_in", range(CONV_TILES + XS_TILES), KD, H, ssd_in_epilogue)
        flush()

        pair_rings = Ring([sq[:, i * 768:i * 768 + 384] for i in range(2)])
        m_ring = Ring([sq[:, i * 768 + 384:i * 768 + 768] for i in range(2)])
        ar2 = Arena()
        ar2.at = ar.at
        xs_tok_ring = Ring([ar2.get(TT * 512)])
        GH = SSD_HEADS // SSD_GROUPS
        gt = XS_TILES // SSD_GROUPS
        gsum_sb = cb_sb
        ms_sb = dt_w[:, 0:SSD_GROUPS * S]
        cb_free = []
        y_t = {}
        ms_t = []
        t_all_in = [conv_t[m] for m in (CONV_TILES + XS_TILES - 1, CONV_TILES - 1)]
        for g in range(SSD_GROUPS):
            n, bank, free = banks.take()
            bg, cg = b_sb[:, g * S:(g + 1) * S], c_sb[:, g * S:(g + 1) * S]
            mm(bank[:, 0:S], bg[:, 0:P], cg, True, True, t_all_in + free)
            t = mm(bank[:, S:S + P], bg[:, P:S], cg[:, P:S], False, True, signal=True)
            t_cb = V.do(lambda e: e.tensor_copy(cb_sb, bank[:, 0:3 * P]), [t, V.last()] + cb_free)
            banks.give(n, [t_cb])
            xn, xt, xfree = xs_tok_ring.take()
            for tt in range(TT):
                n, bank, free = banks.take()
                for j in range(gt):
                    t = T.do(lambda e, j=j, tt=tt, bank=bank: e.transpose(
                        bank[:, j * P:(j + 1) * P], tile(xs_sb, g * gt + j, tt * P, (tt + 1) * P), con("ident")),
                        free, signal=True)
                t_xt = A.do(lambda e, tt=tt, bank=bank: e.activation(xt[:, tt * 512:(tt + 1) * 512], bank[:, :], ACT.Copy),
                            [t] + xfree)
                banks.give(n, [t_xt])
            ybank = {}

            def decays(h):
                n, b, free = banks.take()
                oneh = sel[:, h:h + 1].to_broadcast([hT, P])
                mm(b[:, 0:S], oneh, acs_hi[:, :], True, False, free + [t_sel, state["acs_hi"]])
                mm(b[:, 0:S], oneh, acs_lo[:, :], False, False, [state["acs"]])
                mm(b[:, S:S + P], oneh, acs_hi[:, P:S], False, False)
                mm(b[:, S:S + P], oneh, acs_lo[:, P:S], False, False)
                mm(b[:, 0:P], ident_r[:, :], mask_r[:, :], False, False, [t_mask, t_ident_r])
                t = mm(b[:, S:S + P], ident_r[:, :], mask_r[:, :], False, True, signal=True)
                pn, dec, pfree = pair_rings.take()
                bias = (tok[:, 2 * hT + h:2 * hT + h + 1], tok[:, 4 * hT + h:4 * hT + h + 1],
                        tok[:, 3 * hT + h:3 * hT + h + 1])
                for i in range(3):
                    te = A.do(lambda e, i=i: e.activation(dec[:, i * P:(i + 1) * P], b[:, i * P:(i + 1) * P],
                                                          ACT.Exp, bias=bias[i]), [t, state["tok"]] + pfree)
                banks.give(n, [te])
                mn, mt, mfree = m_ring.take()
                V.do(lambda e: e.scalar_tensor_tensor(mt[:, 0:S], dec[:, 0:S], tok[:, h:h + 1], cb_sb[:, 0:S],
                                                      ALU.mult, ALU.mult), [te, t_cb] + mfree)
                tm = V.do(lambda e: e.scalar_tensor_tensor(mt[:, S:S + P], dec[:, S:S + P], tok[:, hT + h:hT + h + 1],
                                                           cb_sb[:, S:S + P], ALU.mult, ALU.mult))
                pair_rings.give(pn, [tm])
                return mn, mt, tm

            def head_y(h, made):
                mn, mt, tm = made
                j, half = (h % GH) // 2, h % 2
                if half == 0:
                    ybank[j] = banks.take()
                n, b, free = ybank[j]
                out = b[half * SSD_P:(half + 1) * SSD_P, 0:S]
                c0 = (h % GH) * SSD_P
                mm(out, xt[:, c0:c0 + SSD_P], mt[:, 0:S], True, False, [tm, t_xt] + free)
                t = mm(b[half * SSD_P:(half + 1) * SSD_P, P:S], xt[:, 512 + c0:512 + c0 + SSD_P], mt[:, S:S + P],
                       False, True, signal=True)
                m_ring.give(mn, [t])
                if half == 1:
                    k = g * gt + j
                    t1 = V.do(lambda e: e.scalar_tensor_tensor(tile(xs_sb, k), tile(xs_sb, k), par("ssd_d", k),
                                                               b[:, 0:S], ALU.mult, ALU.add), [t])
                    y_t[k] = V.do(lambda e: e.tensor_tensor(tile(z_sb, k), tile(z_sb, k), tile(xs_sb, k), ALU.mult),
                                  [t1])
                    banks.give(n, [t1])
                    s_t[k] = A.do(lambda e: e.activation(tile(xs_sb, k), tile(z_sb, k), ACT.Square), [y_t[k]])
                return t
            s_t = {}
            made = [decays(g * GH)]
            for i in range(GH):
                if i + 1 < GH:
                    made.append(decays(g * GH + i + 1))
                t_last = head_y(g * GH + i, made[i])
            cb_free = [V.last()]
            xs_tok_ring.give(xn, [t_last])
            n, b, free = banks.take()
            for j in range(gt):
                k = g * gt + j
                t = mm(b[:, 0:S], ones, tile(xs_sb, k), j == 0, j == gt - 1, [s_t[k]] + free, signal=True)
            ms_t.append(V.do(lambda e, g=g, b=b: e.tensor_copy(ms_sb[:, g * S:(g + 1) * S], b[:, 0:S]),
                             [t, state["tok"], state["acs_hi"]]))
            banks.give(n, [ms_t[-1]])
        t_std = A.do(lambda e: e.activation(ms_sb, ms_sb, ACT.Sqrt, bias=eps_col, scale=1.0 / (gt * P)), [ms_t[-1]])
        t_r = V.do(lambda e: e.reciprocal(ms_sb, ms_sb), [t_std])
        ssd_out = OuterProjection("w_ssd_out", XS_TILES)
        for k in range(XS_TILES):
            g = k // gt
            t = V.do(lambda e, k=k, g=g: e.scalar_tensor_tensor(
                tile(z_sb, k), tile(z_sb, k), par("ssd_norm_g", k), ms_sb[:, g * S:(g + 1) * S],
                ALU.mult, ALU.mult), [t_r, A.last()])
            slot, _, free = gu_ring.take()
            part = Split(g_hi, g_lo, S)
            split_tile(part, slot, tile(z_sb, k), t, free)
            gu_ring.give(slot, [ssd_out.step(part.part("hi", slot), part.part("lo", slot),
                                             part.hi_t[slot], part.lo_t[slot])])
        sums = take_sums()
        ssd_out.finish(residual_epilogue(sums))
        flush()

        def ffn(layer, sums):
            norm_into_h((sums[0], sums[1], sums[3]), lambda k: par("ffn_g", layer * KD + k))
            base = layer * (FFN_TAPS + 1) * 2 * FF_TILES
            ar = Arena()
            nonlocal_ring = Ring([ar.get(S) for _ in range(4)])
            gate_ring = Ring([ar.get(S) for _ in range(2)])
            prod_ring = Ring([ar.get(S) for _ in range(3)])
            hold = {}

            def epilogue(m, bank, t):
                i, is_up = m // 2, m % 2
                col = base + (FF_TILES if is_up else 0) + i
                n, acc, free = nonlocal_ring.take()
                t_acc = A.do(lambda e: e.activation(acc, bank[:, 0:S], ACT.Identity,
                                                    bias=par("ffn_conv", col + FFN_TAPS * 2 * FF_TILES),
                                                    scale=par("ffn_conv", col + (FFN_TAPS - 1) * 2 * FF_TILES)),
                             [t] + free)
                for back in range(1, FFN_TAPS):
                    t_acc = V.do(lambda e, back=back: e.scalar_tensor_tensor(
                        acc[:, back:S], bank[:, 0:S - back],
                        par("ffn_conv", col + (FFN_TAPS - 1 - back) * 2 * FF_TILES), acc[:, back:S],
                        ALU.mult, ALU.add), [t_acc])
                if not is_up:
                    gn, gate, gfree = gate_ring.take()
                    tg = A.do(lambda e: e.activation(gate, acc, ACT.Silu), [t_acc] + gfree)
                    nonlocal_ring.give(n, [tg])
                    hold[i] = (gn, gate, tg)
                else:
                    gn, gate, tg = hold[i]
                    pn, prod, pfree = prod_ring.take()
                    tp = V.do(lambda e: e.tensor_tensor(prod, gate, acc, ALU.mult), [tg, t_acc] + pfree)
                    nonlocal_ring.give(n, [tp])
                    gate_ring.give(gn, [tp])
                    slot, _, sfree = gu_ring.take()
                    part = Split(g_hi, g_lo, S)
                    prod_ring.give(pn, split_tile(part, slot, prod, tp, sfree))
                    products[i] = (slot, part)
                return [t_acc]

            products = {}
            down = OuterProjection(f"w_down{layer}", FF_TILES)
            for i in range(FF_TILES + 2):
                if i < FF_TILES:
                    project(f"w_up{layer}", [2 * i, 2 * i + 1], KD, H, epilogue)
                if i % 2 and i >= 3:
                    for k in (i - 3, i - 2):
                        slot, part = products.pop(k)
                        gu_ring.give(slot, [down.step(part.part("hi", slot), part.part("lo", slot),
                                                      part.hi_t[slot], part.lo_t[slot])])
            out_sums = take_sums()
            down.finish(residual_epilogue(out_sums))
            flush()
            return out_sums

        sums = ffn(0, sums)

        t_cs = A.do(lambda e: e.activation(cs_sb[:, :], par("c", 0, KD), ACT.Silu), [t_params])

        class Ada:

            def __init__(self, layer):
                self.layer, self.m = layer, 0
                self.n, self.bank, self.free = banks.take()
                self.first = next(i for i, p in enumerate(plan) if p[0] == f"w_ada{layer}")

            def step(self):
                if self.m >= 3 * KD:
                    return
                i = self.first + self.m // 2
                W.load_ahead()
                raw, t_raw = W.raw_chunk(i)
                for j in range(2):
                    m = self.m + j
                    for k in range(KD):
                        at = (j * KD + k) * P
                        t = mm(self.bank[:, m:m + 1], raw[:, at:at + P], cs_sb[:, k:k + 1],
                               m == 0 and k == 0, k == KD - 1, [t_raw, t_cs] + self.free, signal=k == KD - 1)
                W.raw_done(i, t)
                self.m += 2
                self.t = t

            def finish(self):
                while self.m < 3 * KD:
                    self.step()
                lay = self.layer
                t = V.do(lambda e: e.tensor_tensor(mod_sb[:, :], self.bank[:, 0:3 * KD],
                                                   par("b_ada", lay * 3 * KD, 3 * KD), ALU.add), [self.t, t_mod[0]])
                banks.give(self.n, [t])
                t = V.do(lambda e: e.scalar_tensor_tensor(mod_sb[:, KD:2 * KD], mod_sb[:, KD:2 * KD], 1.0,
                                                          par("g_pre", lay * KD, KD), ALU.add, ALU.mult), [t])
                t = V.do(lambda e: e.tensor_tensor(mod_sb[:, 2 * KD:3 * KD], mod_sb[:, 2 * KD:3 * KD],
                                                   par("g_post", lay * KD, KD), ALU.mult), [t])
                t_mod[0] = t
        t_mod = [None]

        def attend(units, scratch, filler):
            e_ring = Ring([scratch.get(2 * S) for _ in range(4)])
            p_ring = Ring([scratch.get(2 * S) for _ in range(3)])
            n_ring = Ring([scratch.get(2) for _ in range(4)])
            made = {}

            def scores(i):
                u = units[i]
                nk = u["nk"]
                n, bank, free = banks.take()
                en, eb, efree = e_ring.take()
                nn, nm, nfree = n_ring.take()
                for j, (q, k, _) in enumerate(u["scores"]):
                    t = mm(bank[:, j * S:j * S + nk], q, k, j == 0, True, u["after"] + (free if j == 0 else []),
                           signal=True)
                for j, (_, _, bias) in enumerate(u["scores"]):
                    tv = V.do(lambda e, j=j, bias=bias: e.tensor_tensor_reduce(
                        eb[:, j * S:j * S + nk], bank[:, j * S:j * S + nk], bias, -1.0, 3.0e38,
                        ALU.add, ALU.min, nm[:, j:j + 1]), [t] + efree + nfree + u["after"])
                    te = A.do(lambda e, j=j: e.activation(eb[:, j * S:j * S + nk], eb[:, j * S:j * S + nk], ACT.Exp,
                                                          bias=nm[:, j:j + 1], scale=-1.0,
                                                          accum_out=u["sums"][j]), [tv])
                banks.give(n, [tv])
                n_ring.give(nn, [te])
                u["sums_t"] = te
                made[i] = [en, eb, te]

            def turn(i):
                u = units[i]
                nk = u["nk"]
                en, eb, te = made[i]
                n, bank, free = banks.take()
                pn, pb, pfree = p_ring.take()
                kts = nk // P
                for j in range(2):
                    for kt in range(kts):
                        at = (j * kts + kt) * P
                        t = T.do(lambda e, at=at, j=j, kt=kt: e.transpose(
                            bank[:, at:at + P], eb[:, j * S + kt * P:j * S + (kt + 1) * P], con("ident")),
                            [te] + free, signal=True)
                e_ring.give(en, [t])
                w = 2 * kts * P
                if i % 2:
                    tc = A.do(lambda e: e.activation(pb[:, 0:w], bank[:, 0:w], ACT.Copy), [t] + pfree)
                else:
                    tc = V.do(lambda e: e.tensor_copy(pb[:, 0:w], bank[:, 0:w]), [t] + pfree)
                banks.give(n, [tc])
                made[i] = [pn, pb, tc]

            def values(i):
                u = units[i]
                kts = u["nk"] // P
                pn, pb, tc = made.pop(i)
                u["before"]()
                for j in range(2):
                    out, starts, free = u["out"][j]()
                    for kt in range(kts):
                        at = (j * kts + kt) * P
                        t = mm(out, pb[:, at:at + P], u["values"][j][kt], starts and kt == 0, kt == kts - 1,
                               [tc] + free + u["after"], signal=kt == kts - 1)
                p_ring.give(pn, [t])
                u["then"](t, u)

            for i in range(len(units) + 3):
                if i < len(units):
                    scores(i)
                if filler and i % 1 == 0:
                    filler()
                if 2 <= i < len(units) + 2:
                    turn(i - 2)
                if i >= 3:
                    values(i - 3)

        norm_into_h((sums[0], sums[1], sums[3]), lambda k: par("mix_g", KD + k))
        ar = Arena()
        q_sb, k_sb = ar.get(KD * S), ar.get(KD * S)
        v_sb = ar.get(TT * D)
        cos_sb, sin_sb = ar.get(S), ar.get(S)
        pos_f, ang, kk_f = ar.get(S), ar.get(S), ar.get(S)
        pos_i = arena[:, ar.at:ar.at + S].bitcast(I32)
        ar.at += S
        sq_ring = Ring([ar.get(S) for _ in range(3)])
        rs_ring = Ring([ar.get(S) for _ in range(3)])
        t_pos = load(pos_i, d["positions"], s_pos, 16, [T.last(), V.last(), A.last()])
        chain = lambda fn, after=(): V.do(fn, [V.last()] + list(after))
        chain(lambda e: e.tensor_copy(pos_f, pos_i), [t_pos, T.last(), A.last()])
        chain(lambda e: e.tensor_scalar(ang, pos_f, con("inv_freq"), None, ALU.mult))
        chain(lambda e: e.tensor_scalar(kk_f, ang, 1.0 / (2 * math.pi), 12582912.0, ALU.mult, ALU.add))
        chain(lambda e: e.tensor_scalar(kk_f, kk_f, -12582912.0, None, ALU.add))
        for part in TWO_PI_PARTS:
            chain(lambda e, part=part: e.scalar_tensor_tensor(ang, kk_f, -part, ang, ALU.mult, ALU.add))
        chain(lambda e: e.tensor_scalar(ang, ang, 3.1415925, -3.1415925, ALU.min, ALU.max))
        t_sin = A.do(lambda e: e.activation(sin_sb, ang, ACT.Sin), [V.last()])
        chain(lambda e: e.tensor_scalar(kk_f, ang, -1.0, None, ALU.mult))
        chain(lambda e: e.tensor_tensor(kk_f, kk_f, ang, ALU.max))
        chain(lambda e: e.tensor_scalar(kk_f, kk_f, -1.0, half_pi, ALU.mult, ALU.add))
        t_cos = A.do(lambda e: e.activation(cos_sb, kk_f, ACT.Sin), [V.last()])
        qg = small[:, 2:3]
        chain(lambda e: e.tensor_scalar(qg, par("q_g"), 1.0 / math.sqrt(HD), None, ALU.mult), [t_params])
        for i in range(2):
            chain(lambda e, i=i: e.tensor_tensor_reduce(kk_f[:, 0:HD], par("lam", 2 * i * HD, HD),
                                                        par("lam", (2 * i + 1) * HD, HD), 1.0, 0.0, ALU.mult, ALU.add,
                                                        small[:, 4 + i:5 + i]), [t_cos])
        t_lam = A.do(lambda e: e.activation(small[:, 6:8], small[:, 4:6], ACT.Exp), [V.last()])
        lam = small[:, 8:9]
        chain(lambda e: e.tensor_tensor(lam, small[:, 6:7], small[:, 7:8], ALU.subtract), [t_lam])
        chain(lambda e: e.tensor_scalar(lam, lam, LAMBDA_INIT, None, ALU.add))
        sg = small[:, 3:4]
        t_small = chain(lambda e: e.tensor_scalar(sg, par("subln_g"), 1.0 - LAMBDA_INIT, None, ALU.mult))

        def qk_epilogue(m, bank, t):
            dst = tile(q_sb, m) if m < KD else tile(k_sb, m - KD)
            gain = qg if m < KD else par("k_g")
            t_raw = A.do(lambda e: e.activation(dst, bank[:, 0:S], ACT.Copy), [t])
            sn, s2, sfree = sq_ring.take()
            t_sq = A.do(lambda e: e.activation(s2, bank[:, 0:S], ACT.Square), [t] + sfree)

            def head_sums():
                n, b, free = banks.take()
                ts = mm(b[:, 0:S], con("block_ones"), s2, True, True, [t_sq] + free, signal=True)
                rn, rs, rfree = rs_ring.take()
                t1 = A.do(lambda e: e.activation(rs, b[:, 0:S], ACT.Sqrt, bias=eps_col, scale=1.0 / HD),
                          [ts] + rfree)
                banks.give(n, [t1])
                t2 = V.do(lambda e: e.reciprocal(rs, rs), [t1])
                t3 = V.do(lambda e: e.scalar_tensor_tensor(dst, dst, gain, rs, ALU.mult, ALU.mult), [t2, t_raw, t_small])
                rs_ring.give(rn, [t3])

                def rotate():
                    n, b, free = banks.take()
                    tr = mm(b[:, 0:S], con("rope_perm"), dst, True, True, [t3] + free, signal=True)
                    t4 = V.do(lambda e: e.tensor_tensor(s2, b[:, 0:S], sin_sb, ALU.mult), [tr, t_sin])
                    banks.give(n, [t4])
                    t5 = V.do(lambda e: e.tensor_tensor(dst, dst, cos_sb, ALU.mult), [t_cos, tr])
                    qk_t[m] = V.do(lambda e: e.tensor_tensor(dst, dst, s2, ALU.add), [t4, t5])
                    sq_ring.give(sn, [qk_t[m]])
                later(1, rotate)
            later(1, head_sums)
            return [t_sq]
        qk_t = {}
        project("w_attn_in", range(2 * KD), KD, H, qk_epilogue)
        v_t = []
        for c in range(D // S):
            def v_epilogue(tt, bank, t, c=c):
                v_t.append(A.do(lambda e: e.activation(v_sb[:, tt * D + c * S:tt * D + (c + 1) * S], bank[:, 0:S],
                                                       ACT.Copy), [t]))
                return [v_t[-1]]
            project_rows("w_attn_v", S, H, v_epilogue)
        flush()

        ready = [qk_t[m] for m in range(2 * KD)] + v_t
        sc = Arena()
        sc.at = ar.at - 11 * S
        sums_sb = sc.get(2 * A_HEADS * TT)
        rl_sb = sc.get(2 * A_HEADS * TT)
        ss_sb = sc.get(A_HEADS * TT)
        sc.at = max(sc.at, ar.at - 11 * S + 64)
        o_tok = [sq[:, qb * D:(qb + 1) * D] for qb in range(TT)]
        ada = Ada(0)
        units = []
        obanks = {}
        junk = sb("junk", [P, P])[:, :]
        row_at = lambda qb, h, c: (qb * A_HEADS + h) * 2 + c
        for qb in range(TT):
            nk = (qb + 1) * P
            for pair in range(A_HEADS // 2):
                for c in range(2):
                    heads = (2 * pair, 2 * pair + 1)

                    def before(qb=qb, pair=pair, c=c):
                        if c == 0:
                            obanks[(qb, pair)] = banks.take()

                    def out_fn(j, qb=qb, pair=pair, c=c):
                        def fn():
                            n, b, free = obanks[(qb, pair)]
                            at = j * 2 * P + c * P
                            return b[:, at:at + P], j == 0 and c == 0, free
                        return fn

                    def then(t, u, qb=qb, pair=pair, c=c, heads=heads):
                        if c == 0:
                            return
                        n, b, _ = obanks[(qb, pair)]
                        first = row_at(qb, heads[0], 0)
                        rl = rl_sb[:, first:first + 4]
                        t1 = V.do(lambda e: e.reciprocal(rl, sums_sb[:, first:first + 4]), [u["sums_t"]])
                        rl_1 = rl.rearrange("p (h c) -> p h c", c=2)[:, :, 1:2]
                        t2 = V.do(lambda e: e.tensor_scalar(rl_1, rl_1, lam, None, ALU.mult), [t1])
                        for j, h in enumerate(heads):
                            o = o_tok[qb][:, h * P:(h + 1) * P]
                            at = j * 2 * P
                            t3 = V.do(lambda e: e.tensor_scalar(o, b[:, at + P:at + 2 * P], rl[:, 2 * j + 1:2 * j + 2], None,
                                                                ALU.mult), [t, t2])
                            t4 = V.do(lambda e: e.scalar_tensor_tensor(o, b[:, at:at + P], rl[:, 2 * j:2 * j + 1], o,
                                                                       ALU.mult, ALU.subtract), [t3])
                            ss = qb * A_HEADS + h
                            t5 = A.do(lambda e: e.activation(junk, o, ACT.Square, accum_out=ss_sb[:, ss:ss + 1]),
                                      [t4, A.last()])
                        banks.give(n, [t4])
                        if pair == A_HEADS // 2 - 1:
                            head_norm(qb, t5)
                    units.append(dict(
                        nk=nk, after=ready, before=before, then=then,
                        scores=[(q_sb[c * HD:(c + 1) * HD, h * S + qb * P:h * S + (qb + 1) * P],
                                 k_sb[c * HD:(c + 1) * HD, h * S:h * S + nk], con("chunk_mask", S - nk, nk))
                                for h in heads],
                        values=[[v_sb[:, kt * D + h * P:kt * D + (h + 1) * P] for kt in range(qb + 1)] for h in heads],
                        out=[out_fn(0), out_fn(1)],
                        sums=[sums_sb[:, row_at(qb, h, c):row_at(qb, h, c) + 1] for h in heads]))

        def head_norm(qb, t):
            ss = ss_sb[:, qb * A_HEADS:(qb + 1) * A_HEADS]
            t1 = A.do(lambda e: e.activation(ss, ss, ACT.Sqrt, bias=eps_col, scale=1.0 / (2 * HD)), [t])
            t2 = V.do(lambda e: e.reciprocal(ss, ss), [t1])
            o3 = o_tok[qb].rearrange("p (h c) -> p h c", h=A_HEADS)
            t3 = V.do(lambda e: e.tensor_tensor(o3, o3, ss.unsqueeze(2).to_broadcast([P, A_HEADS, P]), ALU.mult), [t2])
            for half in range(2):
                n, b, free = banks.take()
                for j in range(4):
                    h = half * 4 + j
                    t4 = T.do(lambda e, j=j, h=h, b=b: e.transpose(b[:, j * P:(j + 1) * P],
                                                                  o_tok[qb][:, h * P:(h + 1) * P], con("ident")),
                              [t3] + free, signal=True)
                b3 = b[:, :].rearrange("p (h c) -> p h c", h=4)
                hi = h_hi[:, half * 4 * S:(half + 1) * 4 * S].rearrange("p (h c) -> p h c", h=4)[:, :, qb * P:(qb + 1) * P]
                lo = h_lo[:, half * 4 * S:(half + 1) * 4 * S].rearrange("p (h c) -> p h c", h=4)[:, :, qb * P:(qb + 1) * P]
                t5 = A.do(lambda e, hi=hi, b3=b3: e.activation(hi, b3, ACT.Copy, scale=sg), [t4])
                t6 = V.do(lambda e, hi=hi, lo=lo, b3=b3: e.scalar_tensor_tensor(lo, b3, sg, hi.bitcast(F32),
                                                                                ALU.mult, ALU.subtract), [t5])
                banks.give(n, [t6])
                for j in range(4):
                    Y.hi_t[half * 4 + j], Y.lo_t[half * 4 + j] = t5, t6
        Y = Split(h_hi, h_lo, S)
        attend(units, sc, ada.step)
        ada.finish()
        sums = take_sums()
        project("w_attn_out", range(KD), KD, Y, residual_epilogue(sums))
        flush()
        sums = ffn(1, sums)

        alibi = sb("alibi_sb", [P, H_HEADS * S])
        t_alibi = load(alibi[:, :], d["alibi"], s_alibi, 16)
        hyb = {}

        def hybrid(layer, sums):
            shift = lambda k: mod_sb[:, k:k + 1]
            norm_into_h((sums[0], sums[1], sums[3]), lambda k: mod_sb[:, KD + k:KD + k + 1], shift)
            ar = Arena()
            qn_sb, qm_sb, km_sb = ar.get(4 * S), ar.get(4 * S), ar.get(4 * S)
            zs = ar.get(8 * S)
            kdup = {"s": ar.get(2 * S), "w": ar.get(2 * S)}
            vm = ar.get(TT * 512)
            vsw = ar.get(TT * VSG)
            kc_dup = ar.get(2 * 32)
            vc_dup = ar.get(H_GROUPS * HD)
            gates = ar.get(TT * 24)
            coef = ar.get(TT * 4 * H_HEADS)
            lsum = ar.get(TT * 4 * H_HEADS)
            pc = ar.get(TT * H_HEADS * 32)
            o_n = ar.get(512)
            o_t = ar.get(512)
            st = ar.get(2 * H_HEADS)
            sc = Arena()
            sc.at = ar.at
            slab = {"k": ar.get(3 * S), "v": ar.get(3 * S)}
            ck = ar.get(2 * CMP_PAIRS * HD)
            ck2 = ar.get(2 * HD)
            gel = ar.get(2 * 32)
            done = [T.last(), V.last(), A.last()]
            t_ck = load(ck, d[f"ck1_{layer}"], s_cmp[layer], 16, done)
            t_ck = load(ck2[0:HD, :], d[f"ck2_{layer}"], s_cmp[layer], 32)
            t_zero = {}
            for kind in "kv":
                t_zero[kind] = V.do(lambda e, b=slab[kind]: e.memset(b, 0.0), done)
            pe_dst = {kind: slab[kind][:, 2 * S:2 * S + CMP_LEN].rearrange("p (j two) -> p j two", two=2)[:, :, 0:1]
                      for kind in "kv"}
            pe_sb = st[:, 0:0]
            pe_in = gel
            t_ck = load(pe_in[:, 0:2 * CMP_PAIRS], d[f"pe_{layer}"], s_cmp[layer], 48)
            t_pe = {}
            for i, kind in enumerate("kv"):
                t_pe[kind] = V.do(lambda e, kind=kind, i=i: e.tensor_copy(
                    pe_dst[kind], pe_in[:, i * CMP_PAIRS:(i + 1) * CMP_PAIRS].unsqueeze(2)), [t_ck, t_zero[kind]])
            got = {}

            def kv_epilogue(m, bank, t):
                if m < 2:
                    b = slab["kv"[m]]
                    for g in range(2):
                        src = bank[g * HD:(g + 1) * HD, :]
                        V.do(lambda e, src=src, g=g: e.tensor_copy(b[0:HD, g * S:(g + 1) * S], src[:, 0:S]),
                             [t, t_pe["kv"[m]]])
                        t1 = V.do(lambda e, src=src, g=g: e.tensor_copy(b[HD:P, g * S:g * S + S - 1], src[:, 1:S]),
                                  [t])
                else:
                    b = kdup["sw"[m - 2]]
                    for g in range(2):
                        src = bank[g * HD:(g + 1) * HD, 0:S]
                        for half in range(2):
                            t1 = A.do(lambda e, src=src, g=g, half=half: e.activation(
                                b[half * HD:(half + 1) * HD, g * S:(g + 1) * S], src, ACT.Copy), [t] + done)
                got[("kv", m)] = t1
                return [t1]

            def vsg_epilogue(tt, bank, t):
                t1 = A.do(lambda e: e.activation(vsw[:, tt * VSG:(tt + 1) * VSG], bank[:, 0:VSG], ACT.Copy), [t] + done)
                got[("vsg", tt)] = t1
                t2 = A.do(lambda e: e.activation(gates[:, tt * 24:(tt + 1) * 24], bank[:, 2 * P:VSG], ACT.Sigmoid), [t])
                got[("gates", tt)] = t2
                return [t2]

            def qz_epilogue(m, bank, t):
                kind, k = ("qn", "qm", "km", "zm", "zn")[m // 4], m % 4
                if kind in ("zm", "zn"):
                    dst = tile(zs, k + (4 if kind == "zn" else 0))
                    got[m] = A.do(lambda e: e.activation(dst, bank[:, 0:S], ACT.Silu), [t] + done)
                else:
                    dst = tile({"qn": qn_sb, "qm": qm_sb, "km": km_sb}[kind], k)
                    scale = 1.0 if kind == "km" else HD ** -0.5
                    got[m] = A.do(lambda e: e.activation(dst, bank[:, 0:S], ACT.Copy, scale=scale), [t] + done)
                return [got[m]]

            project(f"w_kv{layer}", range(4), KD, H, kv_epilogue)
            project_rows(f"w_vsg{layer}", VSG, H, vsg_epilogue)

            zero_t = V.do(lambda e: e.memset(pc, 0.0), done)
            for i, kind in enumerate("kv"):
                n, bank, free = banks.take()
                s3 = slab[kind].rearrange("p (g t) -> p g t", g=3)
                for j in range(CMP_PAIRS):
                    rhs = s3[:, :, 2 * j:2 * j + (CMP_T - 1) * CMP_STRIDE + 1:CMP_STRIDE]
                    at = (i * CMP_PAIRS + j) * HD
                    t = mm(bank[0:HD, 0:3 * CMP_T].rearrange("p (g t) -> p g t", g=3), ck[:, at:at + HD], rhs,
                           j == 0, j == CMP_PAIRS - 1, [t_ck, got[("kv", i)]] + free, signal=j == CMP_PAIRS - 1)
                gp = gel[0:HD, 0:2 * 32].rearrange("p (g t) -> p g t", g=2)[:, :, 0:CMP_T]
                t1 = V.do(lambda e, bank=bank: e.tensor_copy(st[0:HD, 0:1], bank[0:HD, 2 * CMP_T:2 * CMP_T + 1]),
                          [t, t_pe["v"]] + done)
                t2 = A.do(lambda e, bank=bank, gp=gp: e.activation(
                    gp, bank[0:HD, 0:2 * CMP_T].rearrange("p (g t) -> p g t", g=2),
                    ACT.Gelu_apprx_tanh, bias=st[0:HD, 0:1]), [t1, t_pe["v"], T.last()])
                banks.give(n, [t2])
                n, bank, free = banks.take()
                for g in range(2):
                    gx = gel[0:HD, g * 32:g * 32 + CMP_T]
                    if kind == "k":
                        for half in range(2):
                            t = mm(bank[half * HD:(half + 1) * HD, g * 32:g * 32 + CMP_T], ck2[0:HD, 0:HD], gx,
                                   g == 0, True, [t2] + free, signal=True)
                    else:
                        t = mm(bank[0:CMP_T, g * HD:(g + 1) * HD], gx, ck2[0:HD, HD:2 * HD], g == 0, True,
                               [t2] + free, signal=True)
                if kind == "k":
                    t3 = V.do(lambda e, bank=bank: e.tensor_copy(
                        kc_dup.rearrange("p (g t) -> p g t", g=2)[:, :, 0:CMP_T],
                        bank[:, 0:64].rearrange("p (g t) -> p g t", g=2)[:, :, 0:CMP_T]), [t])
                else:
                    for r in range(4):
                        t3 = V.do(lambda e, bank=bank, r=r: e.tensor_copy(
                            vc_dup[32 * r:32 * r + CMP_T, :], bank[0:CMP_T, 0:2 * HD]), [t])
                got[("cmp", kind)] = t3
                banks.give(n, [t3])
            for c in range(2):
                def vm_epilogue(tt, bank, t, c=c):
                    got[("vm", tt, c)] = A.do(lambda e: e.activation(
                        vm[:, tt * 512 + c * S:tt * 512 + (c + 1) * S], bank[:, 0:S], ACT.Copy), [t] + done)
                    return [got[("vm", tt, c)]]
                project_rows(f"w_vm{layer}", S, H, vm_epilogue)
            project(f"w_qz{layer}", range(20), KD, H, qz_epilogue)
            flush()

            ready = [A.last(), V.last(), t_alibi]
            ada = Ada(1) if layer == 0 else None
            Y = Split(h_hi, h_lo, S)
            units = []
            obank = {}
            KINDS = ("m", "s", "w")
            HEAD_PAIRS = ((0, 2), (1, 3), (4, 6), (5, 7))

            def head(kind, h, qb):
                r = (h % 2) * HD
                g = h // HPG
                q = (qm_sb if kind == "m" else qn_sb)[r:r + HD, (h // 2) * S + qb * P:(h // 2) * S + (qb + 1) * P]
                nk = (qb + 1) * P
                if kind == "m":
                    return q, km_sb[r:r + HD, (h // 2) * S:(h // 2) * S + nk], [
                        vm[:, kt * 512 + h * HD:kt * 512 + (h + 1) * HD] for kt in range(qb + 1)]
                at = 0 if kind == "s" else P
                return q, kdup[kind][r:r + HD, g * S:g * S + nk], [
                    vsw[:, kt * VSG + at + g * HD:kt * VSG + at + (g + 1) * HD] for kt in range(qb + 1)]

            def scale_out(bank, coefs, out, after):
                return V.do(lambda e: e.tensor_tensor(
                    out.rearrange("p (h c) -> p h c", h=H_HEADS), bank[:, :].rearrange("p (h c) -> p h c", h=H_HEADS),
                    coefs.unsqueeze(2).to_broadcast([P, H_HEADS, HD]), ALU.mult), after)

            def to_channels(o, t_o, qb, first_tile):
                n, b, free = banks.take()
                for j in range(4):
                    t = T.do(lambda e, j=j: e.transpose(b[:, j * P:(j + 1) * P], o[:, j * P:(j + 1) * P], con("ident")),
                             [t_o] + free, signal=True)
                view = lambda buf: buf[:, first_tile * S:(first_tile + 4) * S].rearrange(
                    "p (h c) -> p h c", h=4)[:, :, qb * P:(qb + 1) * P]
                full = view(zs)
                t1 = V.do(lambda e: e.tensor_tensor(full, b[:, :].rearrange("p (h c) -> p h c", h=4), full, ALU.mult), [t])
                banks.give(n, [t1])
                t2 = A.do(lambda e: e.activation(view(h_hi), full, ACT.Copy), [t1])
                t3 = V.do(lambda e: e.tensor_tensor(view(h_lo), full, view(h_hi).bitcast(F32), ALU.subtract), [t2])
                for j in range(4):
                    Y.hi_t[first_tile + j], Y.lo_t[first_tile + j] = t2, t3
                return t

            def compressed(qb):
                n, b, free = banks.take()
                for h in sorted(range(H_HEADS), key=lambda h: h % 2):
                    r = (h % 2) * HD
                    turn_rows = [t] if h == 1 else []
                    t = mm(b[:, h * CMP_T:(h + 1) * CMP_T],
                           qn_sb[r:r + HD, (h // 2) * S + qb * P:(h // 2) * S + (qb + 1) * P],
                           kc_dup[r:r + HD, (h // HPG) * 32:(h // HPG) * 32 + CMP_T], h == 0, True,
                           ready + free + turn_rows, signal=True)
                v3 = pc[:, qb * 256:(qb + 1) * 256].rearrange("p (h t) -> p h t", h=H_HEADS)[:, :, 0:CMP_T]
                b3 = b[:, 0:H_HEADS * CMP_T].rearrange("p (h t) -> p h t", h=H_HEADS)
                bias = con("cmp_bias", qb * H_HEADS * CMP_T, H_HEADS * CMP_T).rearrange("p (h t) -> p h t", h=H_HEADS)
                ok = con("cmp_ok", qb * CMP_T, CMP_T).unsqueeze(1).to_broadcast([P, H_HEADS, CMP_T])
                mx, sm = st[:, 0:H_HEADS], st[:, H_HEADS:2 * H_HEADS]
                wide = lambda a: a.unsqueeze(2).to_broadcast([P, H_HEADS, CMP_T])
                t = V.do(lambda e: e.tensor_tensor(v3, b3, bias, ALU.add), [t, zero_t])
                banks.give(n, [t])
                t = V.do(lambda e: e.tensor_reduce(mx, v3, AX.X, ALU.max), [t, V.last()])
                t = V.do(lambda e: e.tensor_tensor(v3, v3, wide(mx), ALU.subtract), [t])
                t = A.do(lambda e: e.activation(v3, v3, ACT.Exp), [t])
                t = V.do(lambda e: e.tensor_reduce(sm, v3, AX.X, ALU.add), [t])
                t = V.do(lambda e: e.reciprocal(sm, sm), [t])
                g3 = gates[:, qb * 24:(qb + 1) * 24].rearrange("p (h i) -> p h i", i=3)
                t = V.do(lambda e: e.tensor_tensor(sm.unsqueeze(2), sm.unsqueeze(2), g3[:, :, 0:1], ALU.mult), [t])
                t_c = t
                t = V.do(lambda e: e.tensor_tensor(v3, v3, ok, ALU.mult), [t])
                n, b, free = banks.take()
                for g in range(2):
                    t = T.do(lambda e, g=g: e.transpose(b[:, g * P:(g + 1) * P],
                                                        pc[:, qb * 256 + g * P:qb * 256 + (g + 1) * P], con("ident")),
                             [t_c, V.last()] + free, signal=True)
                pT = o_t[:, 0:256]
                t = V.do(lambda e: e.tensor_copy(pT, b[:, 0:256]), [t, V.last(), T.last()])
                banks.give(n, [t])
                n, b, free = banks.take()
                t2 = None
                for h in sorted(range(H_HEADS), key=lambda h: h % HPG):
                    r, g = (h % HPG) * 32, h // HPG
                    turn_rows = [t2] if h < HPG else []
                    t2 = mm(b[:, h * HD:(h + 1) * HD], pT[r:r + CMP_T, g * P:(g + 1) * P],
                            vc_dup[r:r + CMP_T, g * HD:(g + 1) * HD], h == 0, True, [t] + free + turn_rows, signal=True)
                t = scale_out(b, sm, o_n, [t2, V.last()] + o_n_free)
                banks.give(n, [t])
            o_n_free = []

            for qb in range(TT):
                for kn, kind in enumerate(KINDS):
                    for hn, heads_of in enumerate(HEAD_PAIRS):
                        def before(qb=qb, kind=kind, hn=hn):
                            if hn == 0:
                                if kind == "m":
                                    compressed(qb)
                                obank[kind] = banks.take()

                        def out_fn(j, kind=kind, hn=hn, heads_of=heads_of):
                            def fn():
                                n, b, free = obank[kind]
                                h = heads_of[j]
                                return b[:, h * HD:(h + 1) * HD], hn == 0 and j == 0, free
                            return fn

                        def then(t, u, qb=qb, kn=kn, kind=kind, hn=hn):
                            if hn != len(HEAD_PAIRS) - 1:
                                return
                            n, b, _ = obank[kind]
                            at = (qb * 4 + kn) * H_HEADS
                            cf = coef[:, at:at + H_HEADS]
                            t1 = V.do(lambda e: e.reciprocal(cf, lsum[:, at:at + H_HEADS]), [u["sums_t"]])
                            if kind != "m":
                                g3 = gates[:, qb * 24:(qb + 1) * 24].rearrange("p (h i) -> p h i", i=3)
                                t1 = V.do(lambda e: e.tensor_tensor(cf.unsqueeze(2), cf.unsqueeze(2), g3[:, :, kn:kn + 1],
                                                                    ALU.mult), [t1])
                            t2 = scale_out(b, cf, o_t, [t, t1, T.last()])
                            banks.give(n, [t2])
                            if kind == "m":
                                to_channels(o_t, t2, qb, 0)
                                return
                            t3 = V.do(lambda e: e.tensor_tensor(o_n, o_n, o_t, ALU.add), [t2])
                            if kind == "w":
                                o_n_free[:] = [to_channels(o_n, t3, qb, 4)]
                        heads = [head(kind, h, qb) for h in heads_of]
                        nk = (qb + 1) * P
                        at = (qb * 4 + kn) * H_HEADS
                        u = dict(nk=nk, after=ready, before=before, then=then,
                                 scores=[(q, k, alibi[:, h * S + S - nk:(h + 1) * S])
                                         for h, (q, k, _) in zip(heads_of, heads)],
                                 values=[v for _, _, v in heads], out=[out_fn(0), out_fn(1)],
                                 sums=[lsum[:, at + h:at + h + 1] for h in heads_of])
                        units.append(u)
            attend(units, sc, ada.step if ada else None)

            y_sb = sq
            ys = arena[:, 0:KD * S]
            n_s, s_bank, s_free = banks.take()
            sum_t = [None]

            def out_epilogue(m, bank, t):
                t1 = V.do(lambda e: e.tensor_copy(tile(y_sb, m), bank[:, 0:S]), [t])
                t2 = A.do(lambda e: e.activation(tile(ys, m), tile(y_sb, m), ACT.Square), [t1])

                def add_up():
                    sum_t[0] = mm(s_bank[:, 0:S], ones, tile(ys, m), m == 0, m == KD - 1,
                                  [t2] + s_free, signal=True)
                later(1, add_up)
                return [t1]
            project(f"w_out{layer}", range(KD), KD, Y, out_epilogue)
            flush()
            t_rstd, t_free = rstd_of(s_bank, sum_t[0], D)
            banks.give(n_s, [t_free])
            nxt = take_sums()
            for k in range(KD):
                t1 = V.do(lambda e, k=k: e.scalar_tensor_tensor(tile(y_sb, k), tile(y_sb, k),
                                                                mod_sb[:, 2 * KD + k:2 * KD + k + 1], rstd_sb[:, :],
                                                                ALU.mult, ALU.mult), [t_rstd])
                t2 = V.do(lambda e, k=k: e.tensor_tensor(tile(xT, k), tile(xT, k), tile(y_sb, k), ALU.add), [t1])
                x_t[k] = t2
                if layer == DEPTH - 1:
                    continue
                t3 = A.do(lambda e, k=k: e.activation(tile(ys, k), tile(xT, k), ACT.Square), [t2, sum_t[0]])
                nxt[3] = mm(nxt[1][:, 0:S], ones, tile(ys, k), k == 0, k == KD - 1, [t3] + nxt[2], signal=True)
            if ada:
                ada.finish()
            return nxt

        x_t = {}
        for layer in range(DEPTH):
            sums = hybrid(layer, sums)
        for half in range(2):
            c = slice(half * KD * S // 2, (half + 1) * KD * S // 2)
            load(d["out"][:, c], xT[:, c], s_out, 16 * (half + 1), [x_t[(half + 1) * KD // 2 - 1]])
        L.wait([(s_out, 32)])
        assert W.loaded == len(plan) and W.used == len(W.units)


def _columns(a):
    a = np.asarray(a)
    n = a.shape[-1] // P
    a = a.reshape(-1, n, P)
    return a.transpose(2, 0, 1).reshape(P, -1)


def _tiles(w, per_chunk):
    k, m = w.shape[0] // P, w.shape[1] // P
    a = w.reshape(k, P, m, P).transpose(2, 1, 0, 3)
    a = a.reshape(m // per_chunk, per_chunk, P, k * P).transpose(0, 2, 1, 3)
    return np.ascontiguousarray(a.reshape(m // per_chunk, P, per_chunk * k * P))


def _rows(w, width):
    k, n = w.shape[0] // P, w.shape[1] // width
    return np.ascontiguousarray(w.reshape(k, P, n, width).transpose(2, 1, 0, 3).reshape(n, P, k * width))


def _pairs(w):
    k, m = w.shape[0] // P, w.shape[1]
    return np.ascontiguousarray(w.reshape(k // 2, 2, P, m).transpose(0, 2, 1, 3).reshape(k // 2, P, 2 * m))


def layout(i):
    a = {k: np.asarray(v) for k, v in i.items()}
    out = {}
    out["x"] = np.ascontiguousarray(a["x"][0].T.reshape(KD, P, S).transpose(1, 0, 2).reshape(P, KD * S))
    out["positions"] = np.ascontiguousarray(np.broadcast_to(a["positions"][0][None, :], (P, S)))
    p = np.zeros((P, NPARAMS), np.float32)

    def put(name, v, rows=P):
        at, n = PARAMS[name]
        p[0:rows, at:at + n] = np.asarray(v).reshape(rows, n)

    put("mix_g", _columns(a["norm_mix_g"]))
    put("ffn_g", _columns(a["norm_ffn_g"]))
    put("ssd_conv", _columns(np.concatenate([a["ssd_conv_w"][0], a["ssd_conv_b"]], 0)))
    put("ssd_norm_g", _columns(a["ssd_norm_g"]))
    put("ssd_d", _columns(np.repeat(a["ssd_d"][0], SSD_P)))
    put("dt_bias", a["ssd_dt_bias"][0], SSD_HEADS)
    put("a_log", a["ssd_a_log"][0], SSD_HEADS)
    put("ffn_conv", np.concatenate([_columns(np.concatenate([a["ffn_conv_w"][n], a["ffn_conv_b"][n:n + 1]], 0))
                                    for n in range(DEPTH)], 1))
    put("q_g", np.tile(a["attn_q_norm_g"][0], 2))
    put("k_g", np.tile(a["attn_k_norm_g"][0], 2))
    put("subln_g", a["attn_subln_g"][0])
    put("lam", np.broadcast_to(np.concatenate([a[f"attn_{n}"][0] for n in ("lq1", "lk1", "lq2", "lk2")])[None, :],
                               (P, 4 * HD)))
    put("c", _columns(a["c_2"]))
    put("b_ada", _columns(a["b_ada_2"]))
    put("g_pre", _columns(a["g_pre_2"]))
    put("g_post", _columns(a["g_post_2"]))
    out["params"] = p
    w = a["ssd_in_w"][0]
    z, xs, bc, dt = (w[:, 0:SSD_INNER], w[:, SSD_INNER:2 * SSD_INNER],
                     w[:, 2 * SSD_INNER:2 * SSD_INNER + 2 * SSD_GROUPS * SSD_N], w[:, -SSD_HEADS:])
    out["w_dt"] = _tiles(np.concatenate([dt, np.zeros((D, P - SSD_HEADS), np.float32)], 1), 1)
    out["w_ssd_in"] = _tiles(np.concatenate([bc, xs, z], 1), 2)
    out["w_ssd_out"] = _pairs(a["ssd_out_w"][0])
    for n in range(DEPTH):
        up = a["ffn_up_w"][n].reshape(D, 2, FF_TILES, P).transpose(0, 2, 1, 3).reshape(D, 2 * D_FF)
        out[f"w_up{n}"] = _tiles(up, 2)
        out[f"w_down{n}"] = _pairs(a["ffn_down_w"][n])
        out[f"w_ada{n}"] = _tiles(a["w_ada_2"][n], 2)
        u = a["w_in_2"][n]
        qm, km, vm, zm, qn = (u[:, j * 512:(j + 1) * 512] for j in range(5))
        kc, vc, ks, vs, kw, vw = (u[:, 2560 + j * P:2560 + (j + 1) * P] for j in range(6))
        gl, zn = u[:, 3328:3352], u[:, 3352:3864]
        out[f"w_kv{n}"] = _tiles(np.concatenate([kc, vc, ks, kw], 1), 2)
        out[f"w_vsg{n}"] = _rows(np.concatenate([vs, vw, gl], 1), VSG)
        out[f"w_vm{n}"] = _rows(vm, S)
        out[f"w_qz{n}"] = _tiles(np.concatenate([qn, qm, km, zm, zn], 1), 2)
        out[f"w_out{n}"] = _tiles(a["w_out_2"][n], 2)
        ck1 = np.stack([a["w_ck1_2"][n], a["w_cv1_2"][n]]).reshape(2, CMP_PAIRS, P, HD)
        out[f"ck1_{n}"] = np.ascontiguousarray(ck1.transpose(2, 0, 1, 3).reshape(P, 2 * CMP_PAIRS * HD))
        out[f"ck2_{n}"] = np.concatenate([a["w_ck2_2"][n], a["w_cv2_2"][n]], 1)
        pe = np.stack([a["pe_k_2"][n], a["pe_v_2"][n]]).reshape(2, CMP_PAIRS, P)
        out[f"pe_{n}"] = np.ascontiguousarray(pe.transpose(2, 0, 1).reshape(P, 2 * CMP_PAIRS))
    qkv = a["attn_in_w"][0]
    out["w_attn_in"] = _tiles(qkv[:, 0:2 * D], 2)
    out["w_attn_v"] = _rows(qkv[:, 2 * D:], S)
    out["w_attn_out"] = _tiles(a["attn_out_w"][0], 2)
    out["consts"], out["alibi"] = constants()
    return out


def kernel(**inputs):
    import concourse.bacc as _bacc
    from concourse import mybir as _mybir
    from concourse.bass_utils import run_bass_kernel_spmd as _run

    nc = _bacc.Bacc("TRN2", target_bir_lowering=False, num_devices=1)
    arrays = layout(inputs)
    d = {name: nc.dram_tensor(name, a.shape, _mybir.dt.from_np(a.dtype), kind="ExternalInput").ap()
         for name, a in arrays.items()}
    d["out"] = nc.dram_tensor("out", (P, KD * S), F32, kind="ExternalOutput").ap()
    build_program(nc, d)
    r = _run(nc, [arrays], core_ids=[0])
    got = np.asarray(r.results[0]["out"])
    return np.ascontiguousarray(got.reshape(P, KD, S).transpose(2, 1, 0).reshape(1, S, D))
```

```python
from contextlib import ExitStack
import math
import numpy as np

import concourse.bass as bass
from concourse import mybir

F32 = mybir.dt.float32
F32R = mybir.dt.float32r
I32 = mybir.dt.int32
ALU = mybir.AluOpType
ACT = mybir.ActivationFunctionType
AX = mybir.AxisListType

P = 128
S = 256
TT = S // P
D = 1024
KD = D // P
DEPTH = 2
SSD_INNER, SSD_HEADS, SSD_GROUPS, SSD_P, SSD_N, SSD_TAPS = 2048, 32, 4, 64, 128, 4
XS_TILES = SSD_INNER // P
CONV_TILES = XS_TILES + 2 * SSD_GROUPS
A_HEADS, HD = 8, 64
D_FF, FFN_TAPS = 2816, 3
FF_TILES = D_FF // P
ROPE_DIM, ROPE_THETA = 16, 500000.0
CHUNK = 64
LAMBDA_INIT = 0.8 - 0.6 * math.exp(-0.3 * 1)
H_HEADS, H_GROUPS = 8, 2
CMP_LEN, CMP_STRIDE = 32, 16
CMP_T = (S - CMP_LEN) // CMP_STRIDE + 1
HPG = H_HEADS // H_GROUPS
CMP_W = 32
CMP_PAIRS = CMP_LEN * HD // P
EPS = 1e-6
NEG = -1e9
FAR = -1e30
VSG = 2 * P + 3 * H_HEADS
UNIT_MAX = KD // 2 * VSG
RAW_MAX = 2 * UNIT_MAX
ADA_W = 3 * D // 2
ADA_AT = tuple(range(3, 3 + 2 * KD))
TWO_PI_PARTS = (6.28125, 0.0019340515136718750, 1.2556240e-06)

PARAMS = {}


def _param(name, n):
    PARAMS[name] = (PARAMS.get("_n", 0), n)
    PARAMS["_n"] = PARAMS.get("_n", 0) + n


for _name, _n in (("mix_g", DEPTH * KD), ("ffn_g", DEPTH * KD),
                  ("ssd_conv", (SSD_TAPS + 1) * CONV_TILES), ("ssd_norm_g", XS_TILES), ("ssd_d", XS_TILES),
                  ("dt_bias", 1), ("a_log", 1),
                  ("ffn_conv", DEPTH * (FFN_TAPS + 1) * 2 * FF_TILES),
                  ("q_g", 1), ("k_g", 1), ("subln_g", 1), ("lam", 4 * HD),
                  ("c", KD), ("b_ada", DEPTH * 3 * KD), ("g_pre", DEPTH * KD), ("g_post", DEPTH * KD)):
    _param(_name, _n)
NPARAMS = PARAMS["_n"]

CONSTS = {}


def _const(name, n):
    CONSTS[name] = (CONSTS.get("_n", 0), n)
    CONSTS["_n"] = CONSTS.get("_n", 0) + n


for _name, _n in (("ident", P), ("ones", P), ("block_ones", P), ("rope_perm", P), ("inv_freq", 1),
                  ("chunk_mask", S), ("causal_far", P), ("cmp_bias", TT * H_HEADS * CMP_T), ("cmp_ok", TT * CMP_T)):
    _const(_name, _n)
NCONSTS = CONSTS["_n"]


def constants():
    c = np.zeros((P, NCONSTS), np.float32)

    def put(name, a):
        at, n = CONSTS[name]
        c[:, at:at + n] = np.asarray(a, np.float32).reshape(P, n)

    r = np.arange(P)
    put("ident", np.eye(P))
    put("ones", np.ones((P, P)))
    put("block_ones", (r[:, None] // HD) == (r[None, :] // HD))
    perm = np.zeros((P, P))
    half = ROPE_DIM // 2
    for base in (0, HD):
        for i in range(half):
            perm[base + half + i, base + i] = -1.0
            perm[base + i, base + half + i] = 1.0
    put("rope_perm", perm)
    inv = np.float32(ROPE_THETA) ** (-np.arange(0, ROPE_DIM, 2, dtype=np.float32) / np.float32(ROPE_DIM))
    col = np.zeros(P)
    for base in (0, HD):
        col[base:base + half] = inv
        col[base + half:base + 2 * half] = inv
    put("inv_freq", col)
    chunk = np.where((r[None, :] // CHUNK) <= (r[:, None] // CHUNK), 0.0, FAR)
    put("chunk_mask", np.concatenate([np.zeros((P, P)), chunk], 1))
    put("causal_far", np.where(r[None, :] >= r[:, None], 0.0, FAR))
    slopes = (2.0 ** (-8.0 * np.arange(1, H_HEADS + 1) / H_HEADS)).astype(np.float32)
    t = np.arange(S).reshape(TT, P)
    ends = np.arange(CMP_T) * CMP_STRIDE + CMP_LEN - 1
    dist = (t[:, :, None] - ends).astype(np.float32)
    bias = np.where(dist[:, :, None, :] >= 0, -slopes[:, None] * dist[:, :, None, :], NEG)
    put("cmp_bias", bias.transpose(1, 0, 2, 3))
    put("cmp_ok", (dist >= 0).transpose(1, 0, 2))
    far = (P + r[:, None] - r[None, :]).astype(np.float32)
    own = (r[:, None] - r[None, :]).astype(np.float32)
    alibi = np.zeros((P, H_HEADS, S), np.float32)
    for h in range(H_HEADS):
        alibi[:, h, 0:P] = -slopes[h] * far
        alibi[:, h, P:S] = np.where(own >= 0, -slopes[h] * own, NEG)
    return c, alibi.reshape(P, H_HEADS * S)


class Queue:

    def __init__(self, engine, sem):
        self.engine, self.sem, self.count, self.seen = engine, sem, 0, {}

    def wait(self, tickets):
        for t in tickets:
            if t is None:
                continue
            sem, value = t
            if self.seen.get(id(sem), 0) < value:
                self.seen[id(sem)] = value
                self.engine.wait_ge(sem, value)

    def do(self, emit, after=(), signal=True):
        self.wait(after)
        ins = emit(self.engine)
        if not signal:
            return None
        self.count += 1
        ins.then_inc(self.sem, 1)
        return (self.sem, self.count)

    def last(self):
        return (self.sem, self.count) if self.count else None


class Ring:

    def __init__(self, slots):
        self.slots, self.free = slots, [(n, []) for n in range(len(slots))]

    def take(self):
        n, after = self.free.pop(0)
        return n, self.slots[n], after

    def give(self, n, tickets):
        assert n not in [m for m, _ in self.free]
        self.free.append((n, list(tickets)))


class Split:

    def __init__(self, hi, lo, width):
        self.hi, self.lo, self.width, self.hi_t, self.lo_t = hi, lo, width, {}, {}

    def part(self, which, k, a=0, b=None):
        b = self.width if b is None else b
        return (self.hi if which == "hi" else self.lo)[:, k * self.width + a:k * self.width + b]


def build_program(nc, d):
    ctx = ExitStack()
    with ctx:
        def sb(name, shape, dt=F32):
            return ctx.enter_context(nc.sbuf_tensor(name, shape, dt))

        def sem(name):
            return ctx.enter_context(nc.semaphore(name))

        params_sb = sb("params_sb", [P, NPARAMS])
        consts_sb = sb("consts_sb", [P, NCONSTS])
        xT = sb("xT", [P, KD * S])
        sq = sb("sq", [P, KD * S])
        h_hi, h_lo = sb("h_hi", [P, KD * S], F32R), sb("h_lo", [P, KD * S], F32R)
        GU_SLOTS = 6
        g_hi, g_lo = sb("g_hi", [P, GU_SLOTS * S], F32R), sb("g_lo", [P, GU_SLOTS * S], F32R)
        RAW_SLOTS, SPLIT_SLOTS = 4, 5
        raw_sb = sb("raw_sb", [P, RAW_SLOTS * RAW_MAX])
        w_hi = sb("w_hi", [P, SPLIT_SLOTS * UNIT_MAX], F32R)
        w_lo = sb("w_lo", [P, SPLIT_SLOTS * UNIT_MAX], F32R)
        rstd_sb = sb("rstd_sb", [P, S])
        mod_sb = sb("mod_sb", [P, DEPTH * 3 * KD])
        cs_sb = sb("cs_sb", [P, KD])
        small = sb("small", [P, 64])
        ARENA = 16000
        arena = sb("arena", [P, ARENA])
        banks = Ring([ctx.enter_context(nc.psum_tensor(f"bank{i}", [P, 512], F32)) for i in range(8)])

        def par(name, at=0, n=1, rows=P):
            o = PARAMS[name][0] + at
            return params_sb[0:rows, o:o + n]

        def con(name, at=0, n=None, rows=P):
            o, size = CONSTS[name]
            n = size if n is None else n
            return consts_sb[0:rows, o + at:o + at + n]

        T, V, A, L = (Queue(engine, sem(n)) for engine, n in (
            (nc.tensor, "s_pe"), (nc.vector, "s_dve"), (nc.scalar, "s_act"), (nc.sync, "s_sp")))
        raw_sems = [sem(f"s_raw{i}") for i in range(RAW_SLOTS)]
        s_params, s_consts, s_x, s_pos, s_alibi, s_out = (sem(n) for n in (
            "s_params", "s_consts", "s_x", "s_pos", "s_alibi", "s_out"))
        ADA_SLOTS = 2
        s_ada = [sem(f"s_ada{i}") for i in range(ADA_SLOTS)]
        s_cmp = [sem(f"s_cmp{i}") for i in range(DEPTH)]

        def load(out, src, s, value, after=()):
            L.wait(after)
            L.engine.dma_start(out, src).then_inc(s, 16)
            return (s, value)

        class Arena:
            def __init__(self):
                self.at = 0

            def get(self, n, shape=None):
                a = arena[:, self.at:self.at + n]
                self.at += n
                assert self.at <= ARENA, self.at
                return a

        plan = []

        def plan_tiles(name, n, units, size):
            for i in range(n):
                plan.append((name, i, units, size))

        def plan_ffn(layer):
            for i in range(FF_TILES + 2):
                if i < FF_TILES:
                    plan.append((f"w_up{layer}", i, 2, KD * P))
                if i % 2 and i >= 3:
                    plan.append((f"w_down{layer}", (i - 3) // 2, 2, D))

        plan_tiles("w_dt", 1, 1, KD * P)
        GROUP_HEADS = SSD_HEADS // SSD_GROUPS
        GROUP_TILES = XS_TILES // SSD_GROUPS
        Z_PAIRS, OUT_PAIRS = XS_TILES // 2, XS_TILES // 2

        def core_schedule():
            z, out = 1, 0
            for h in range(SSD_HEADS):
                g, i = divmod(h, GROUP_HEADS)
                if i in (1, 5) and z < Z_PAIRS:
                    yield h, "z", z
                    z += 1
                if g and i in (4, 7):
                    yield h, "out", out
                    out += 1

        plan_tiles("w_ssd_in", CONV_TILES // 2 + 1, 2, KD * P)
        for _, what, n in core_schedule():
            plan.append(("w_ssd_in", CONV_TILES // 2 + n, 2, KD * P) if what == "z"
                        else ("w_ssd_out", n, 2, D))
        for n in range(OUT_PAIRS - GROUP_TILES // 2, OUT_PAIRS):
            plan.append(("w_ssd_out", n, 2, D))
        plan_ffn(0)
        plan_tiles("w_attn_in", 2 * KD // 2, 2, KD * P)
        plan_tiles("w_attn_v", D // S, 2, KD * P)
        plan_tiles("w_attn_out", KD // 2, 2, KD * P)
        plan_ffn(1)
        for n in range(DEPTH):
            plan_tiles(f"w_kv{n}", 2, 2, KD * P)
            plan_tiles(f"w_vsg{n}", 1, 2, KD // 2 * VSG)
            plan_tiles(f"w_vm{n}", 2, 2, KD * P)
            plan_tiles(f"w_qz{n}", 10, 2, KD * P)
            plan_tiles(f"w_out{n}", KD // 2, 2, KD * P)

        class Stream:
            def __init__(self):
                self.loaded = self.used_chunk = 0
                self.raw_free = [[] for _ in range(RAW_SLOTS)]
                self.raw_t = {}
                self.units = []
                for i, (_, _, units, _) in enumerate(plan):
                    self.units += [(i, u) for u in range(units)]
                self.prepared = self.used = 0
                self.split_free = [[] for _ in range(SPLIT_SLOTS)]
                self.split_t = {}

            def load_ahead(self):
                while self.loaded < len(plan) and self.raw_free[self.loaded % RAW_SLOTS] is not None:
                    i = self.loaded
                    name, n, units, size = plan[i]
                    slot = i % RAW_SLOTS
                    self.raw_t[i] = load(raw_sb[:, slot * RAW_MAX:slot * RAW_MAX + units * size], d[name][n],
                                         raw_sems[slot], 16 * (i // RAW_SLOTS + 1), self.raw_free[slot])
                    self.raw_free[slot] = None
                    self.loaded += 1

            def prepare(self, upto):
                while self.prepared < min(upto, len(self.units)):
                    u = self.prepared
                    chunk, part = self.units[u]
                    if chunk not in self.raw_t or self.split_free[u % SPLIT_SLOTS] is None:
                        return
                    _, _, units, size = plan[chunk]
                    slot = u % SPLIT_SLOTS
                    raw_at = (chunk % RAW_SLOTS) * RAW_MAX + part * size
                    raw = raw_sb[:, raw_at:raw_at + size]
                    hi = w_hi[:, slot * UNIT_MAX:slot * UNIT_MAX + size]
                    lo = w_lo[:, slot * UNIT_MAX:slot * UNIT_MAX + size]
                    t_hi = A.do(lambda e, o=hi, i=raw: e.activation(o, i, ACT.Copy),
                                [self.raw_t[chunk]] + self.split_free[slot])
                    t_lo = V.do(lambda e, o=lo, i=raw, h=hi: e.tensor_tensor(o, i, h.bitcast(F32), ALU.subtract),
                                [self.raw_t[chunk], t_hi] + self.split_free[slot])
                    self.split_t[u] = (t_hi, t_lo, hi, lo)
                    self.split_free[slot] = None
                    if part == units - 1:
                        self.raw_free[chunk % RAW_SLOTS] = [t_lo]
                        self.load_ahead()
                    self.prepared += 1

            def unit(self, name):
                u = self.used
                assert plan[self.units[u][0]][0] == name, (name, plan[self.units[u][0]])
                self.prepare(u + SPLIT_SLOTS - 1)
                assert u in self.split_t
                self.used += 1
                return u, self.split_t[u]

            def done(self, u, ticket):
                self.split_free[u % SPLIT_SLOTS] = [ticket]
                self.prepare(self.used + SPLIT_SLOTS - 1)

        W = Stream()

        def mm(out, lhsT, rhs, start, stop, after=(), signal=False):
            return T.do(lambda e: e.matmul(out, lhsT, rhs, start=start, stop=stop, skip_group_check=True),
                        after, signal)

        delayed = []

        def later(n, fn):
            delayed.append([n, fn])

        def tick():
            ready = [x for x in delayed if x[0] <= 0]
            for x in delayed:
                x[0] -= 1
            delayed[:] = [x for x in delayed if x not in ready]
            for _, fn in ready:
                fn()

        def flush():
            while delayed:
                tick()

        def project(name, tiles, k_tiles, acts, epilogue):
            per = KD
            for m in tiles:
                n, bank, free = banks.take()
                out = bank[:, 0:S]
                first = True
                for part in range(k_tiles // per):
                    u, (t_hi, t_lo, hi, lo) = W.unit(name)
                    for k in range(per):
                        kk = part * per + k
                        wh, wl = hi[:, k * P:(k + 1) * P], lo[:, k * P:(k + 1) * P]
                        mm(out, wh, acts.part("hi", kk), first, False,
                           [t_hi, acts.hi_t.get(kk)] + (free if first else []))
                        first = False
                        mm(out, wh, acts.part("lo", kk), False, False, [acts.lo_t.get(kk)])
                        end = kk == k_tiles - 1
                        t = mm(out, wl, acts.part("hi", kk), False, end, [t_lo], signal=k == per - 1)
                    W.done(u, t)
                banks.give(n, epilogue(m, out, t))
                tick()

        class OuterProjection:

            def __init__(self, name, k_tiles):
                self.name, self.k_tiles, self.k = name, k_tiles, 0
                self.banks = [banks.take() for _ in range(KD // 2)]

            def step(self, a_hi, a_lo, t_a_hi, t_a_lo):
                u, (t_hi, t_lo, hi, lo) = W.unit(self.name)
                self.t = []
                last = self.k == self.k_tiles - 1
                for m in range(KD):
                    n, bank, free = self.banks[m // 2]
                    out = bank[:, (m % 2) * S:(m % 2 + 1) * S]
                    wh, wl = hi[:, m * P:(m + 1) * P], lo[:, m * P:(m + 1) * P]
                    mm(out, wh, a_hi, self.k == 0 and m % 2 == 0, False,
                       [t_hi, t_a_hi] + (free if self.k == 0 else []))
                    mm(out, wh, a_lo, False, False, [t_a_lo])
                    self.t.append(mm(out, wl, a_hi, False, last, [t_lo], signal=m % 2 == 1))
                W.done(u, self.t[-1])
                self.k += 1
                return self.t[-1]

            def finish(self, epilogue):
                assert self.k == self.k_tiles
                for b, (n, bank, _) in enumerate(self.banks):
                    tickets = []
                    for j in range(2):
                        tickets += epilogue(2 * b + j, bank[:, j * S:(j + 1) * S], self.t[2 * b + 1])
                    banks.give(n, tickets)
                    tick()

        def project_rows(name, width, acts, epilogue):
            taken = [banks.take() for _ in range(TT)]
            half = KD // 2
            for part in range(2):
                u, (t_hi, t_lo, hi, lo) = W.unit(name)
                for tt in range(TT):
                    n, bank, free = taken[tt]
                    out = bank[:, 0:width]
                    for k in range(half):
                        kk = part * half + k
                        wh, wl = hi[:, k * width:(k + 1) * width], lo[:, k * width:(k + 1) * width]
                        ah, al = (acts.part(w, kk, tt * P, (tt + 1) * P) for w in ("hi", "lo"))
                        mm(out, ah, wh, kk == 0, False,
                           [t_hi, acts.hi_t.get(kk)] + (free if kk == 0 else []))
                        mm(out, ah, wl, False, False, [t_lo])
                        t = mm(out, al, wh, False, kk == KD - 1, [acts.lo_t.get(kk)], signal=k == half - 1)
                    if part == 1:
                        taken[tt] = (n, bank, t)
                W.done(u, t)
            for tt, (n, bank, t) in enumerate(taken):
                banks.give(n, epilogue(tt, bank, t))
            tick()

        def split_tile(dst, k, full, t_full, free=()):
            hi, lo = dst.part("hi", k), dst.part("lo", k)
            t = A.do(lambda e: e.activation(hi, full, ACT.Copy), [t_full] + list(free))
            dst.hi_t[k] = t
            dst.lo_t[k] = V.do(lambda e: e.tensor_tensor(lo, full, hi.bitcast(F32), ALU.subtract),
                                  [t, t_full] + list(free))
            return [dst.hi_t[k], dst.lo_t[k]]

        H = Split(h_hi, h_lo, S)
        gu_ring = Ring(list(range(GU_SLOTS)))

        def tile(buf, k, a=0, b=S):
            return buf[:, k * S + a:k * S + b]

        t_x = load(xT[:, :], d["x"], s_x, 16)
        t_params = load(params_sb[:, :], d["params"], s_params, 16)
        t_consts = load(consts_sb[:, :], d["consts"], s_consts, 16)
        W.load_ahead()

        eps_col = small[:, 0:1]
        t_eps = V.do(lambda e: e.memset(eps_col, EPS))
        half_pi = math.pi / 2

        ones = con("ones")

        def square_sums(n_tiles, src, ready):
            n, bank, free = banks.take()
            for k in range(n_tiles):
                t = A.do(lambda e, k=k: e.activation(tile(sq, k), tile(src, k), ACT.Square), ready(k))
                t = mm(bank[:, 0:S], ones, tile(sq, k), k == 0, k == n_tiles - 1,
                       [t, t_consts] + (free if k == 0 else []), signal=True)
            return n, bank, t

        def rstd_of(bank, t_bank, count, after, out=None):
            out = rstd_sb[:, :] if out is None else out
            t_ln = A.do(lambda e: e.activation(out, bank, ACT.Ln, bias=eps_col, scale=1.0 / count),
                        [t_bank, t_eps] + list(after))
            return A.do(lambda e: e.activation(out, out, ACT.Exp, scale=-0.5), [t_ln]), t_ln

        def norm_into_h(sums, gain, shift=None):
            n, bank, t_bank = sums
            t_rstd, t_free = rstd_of(bank[:, 0:S], t_bank, D, [V.last()])
            banks.give(n, [t_free])
            for k in range(KD):
                t = V.do(lambda e, k=k: e.scalar_tensor_tensor(tile(sq, k), tile(xT, k), gain(k),
                                                               rstd_sb[:, :], ALU.mult, ALU.mult),
                         [t_rstd, t_params, T.last()])
                if shift is None:
                    split_tile(H, k, tile(sq, k), t)
                else:
                    H.hi_t[k] = A.do(lambda e, k=k: e.activation(H.part("hi", k), tile(sq, k), ACT.Identity,
                                                                 bias=shift(k)), [t])
                    H.lo_t[k] = V.do(lambda e, k=k: e.scalar_tensor_tensor(
                        H.part("lo", k), tile(sq, k), shift(k), H.part("hi", k).bitcast(F32),
                        ALU.add, ALU.subtract), [t, H.hi_t[k]])

        def residual_epilogue(sums):
            def epilogue(m, bank, t):
                t_add = V.do(lambda e: e.tensor_tensor(tile(xT, m), bank, tile(xT, m), ALU.add), [t])
                t_sq = A.do(lambda e: e.activation(tile(sq, m), tile(xT, m), ACT.Square), [t_add])

                def add_up():
                    n, sums_bank, free, _ = sums
                    sums[3] = mm(sums_bank[:, 0:S], ones, tile(sq, m), m == 0, m == KD - 1,
                                 [t_sq] + (free if m == 0 else []), signal=True)
                later(1, add_up)
                return [t_add]
            return epilogue

        def take_sums():
            n, bank, free = banks.take()
            return [n, bank, free, None]

        sums = square_sums(KD, xT, lambda k: [t_x])
        norm_into_h(sums, lambda k: par("mix_g", k))

        ar = Arena()
        z_sb = ar.get(XS_TILES * S)
        xs_sb = ar.get(XS_TILES * S)
        b_sb = ar.get(SSD_GROUPS * S)
        c_sb = ar.get(SSD_GROUPS * S)
        acc_ring = Ring([ar.get(S) for _ in range(4)])
        cb_ring = Ring([ar.get(3 * P) for _ in range(2)])
        ms_sb = ar.get(S)
        xs_tok_ring = Ring([ar.get(TT * GROUP_TILES * P) for _ in range(2)])
        tok = ar.get(5 * SSD_HEADS)
        dt_w = z_sb[:, 0:5 * P + 6 * S]
        hT = SSD_HEADS
        stack = dt_w[0:hT, 0:5 * P]
        dts, e_ab, u_ab, w_ab, acs = (dt_w[0:hT, 5 * P + i * S:5 * P + (i + 1) * S] for i in range(5))
        dA = dt_w[0:hT, 5 * P + 5 * S:5 * P + 6 * S]
        state = {}

        def dt_epilogue(_, bank, t):
            step = lambda fn, after=(): V.do(fn, [V.last()] + list(after))
            t_v = step(lambda e: e.tensor_scalar(dts, bank[0:hT, 0:S], par("dt_bias", rows=hT), None, ALU.add), [t])
            step(lambda e: e.tensor_scalar(w_ab, dts, -1.0, None, ALU.mult))
            step(lambda e: e.tensor_tensor(w_ab, dts, w_ab, ALU.max))
            t_e = A.do(lambda e: e.activation(e_ab, w_ab, ACT.Exp, scale=-1.0), [V.last()])
            step(lambda e: e.tensor_scalar(u_ab, e_ab, 1.0, None, ALU.add), [t_e])
            t_ln = A.do(lambda e: e.activation(acs, u_ab, ACT.Ln), [V.last()])
            t_a = A.do(lambda e: e.activation(small[0:hT, 1:2], par("a_log", rows=hT), ACT.Exp), [t_params])
            step(lambda e: e.scalar_tensor_tensor(e_ab, u_ab, -1.0, e_ab, ALU.add, ALU.subtract))
            step(lambda e: e.reciprocal(u_ab, u_ab), [t_ln])
            step(lambda e: e.tensor_tensor(e_ab, e_ab, u_ab, ALU.mult))
            step(lambda e: e.tensor_tensor(acs, acs, e_ab, ALU.subtract), [t_ln])
            step(lambda e: e.scalar_tensor_tensor(dts, dts, 0.0, acs, ALU.max, ALU.add))
            step(lambda e: e.tensor_scalar(dA, dts, small[0:hT, 1:2], -1.0, ALU.mult, ALU.mult), [t_a])
            step(lambda e: e.memset(w_ab, 1.0))
            for tt in range(TT):
                step(lambda e, tt=tt: e.tensor_tensor_scan(acs[:, tt * P:(tt + 1) * P], w_ab[:, tt * P:(tt + 1) * P],
                                                           dA[:, tt * P:(tt + 1) * P], 0.0, ALU.mult, ALU.add))
            step(lambda e: e.tensor_copy(stack[:, 0:S], dts))
            step(lambda e: e.tensor_scalar(stack[:, S:2 * S], acs, -1.0, None, ALU.mult))
            t_stack = step(lambda e: e.tensor_scalar(stack[:, 2 * S:2 * S + P], acs[:, 0:P], -1.0, acs[:, P - 1:P],
                                                     ALU.mult, ALU.add))
            state["acs_hi"] = A.do(lambda e: e.activation(acs_hi[:, :], acs, ACT.Copy), [t_stack])
            state["acs"] = V.do(lambda e: e.tensor_tensor(acs_lo[:, :], acs, acs_hi[:, :].bitcast(F32), ALU.subtract),
                                [state["acs_hi"]])

            def turn():
                n, b, free = banks.take()
                for i in range(5):
                    t = T.do(lambda e, i=i: e.transpose(b[:, i * hT:(i + 1) * hT], stack[:, i * P:(i + 1) * P],
                                                        con("ident", 0, hT, hT)),
                             [t_stack, t_consts] + free, signal=True)
                state["tok"] = V.do(lambda e: e.tensor_copy(tok, b[:, 0:5 * hT]), [t])
                banks.give(n, [state["tok"]])
            later(3, turn)
            return [t_v]

        acs_hi = sb("acs_hi", [hT, S], F32R)
        acs_lo = sb("acs_lo", [hT, S], F32R)
        sel = sb("sel", [hT, hT * 2], F32R)
        mask_r = sb("mask_r", [P, P], F32R)
        ident_r = sb("ident_r", [P, P], F32R)
        t_sel = A.do(lambda e: e.activation(sel[:, 0:hT], con("ident", 0, hT, hT), ACT.Copy), [t_consts])
        t_mask = A.do(lambda e: e.activation(mask_r[:, :], con("causal_far"), ACT.Copy), [t_consts])
        t_ident_r = A.do(lambda e: e.activation(ident_r[:, :], con("ident"), ACT.Copy), [t_consts])

        def conv_taps(bank, t, taps, weight, bias):
            n, acc, free = acc_ring.take()
            t_acc = A.do(lambda e: e.activation(acc, bank[:, 0:S], ACT.Identity, bias=bias,
                                                scale=weight(taps - 1)), [t, t_params] + free)
            for back in range(1, taps):
                t_acc = V.do(lambda e, back=back: e.scalar_tensor_tensor(
                    acc[:, back:S], bank[:, 0:S - back], weight(taps - 1 - back), acc[:, back:S],
                    ALU.mult, ALU.add), [t_acc])
            return n, acc, t_acc

        conv_out = ([b_sb[:, g * S:(g + 1) * S] for g in range(SSD_GROUPS)]
                    + [c_sb[:, g * S:(g + 1) * S] for g in range(SSD_GROUPS)]
                    + [tile(xs_sb, k) for k in range(XS_TILES)])
        conv_col = ([XS_TILES + g for g in range(2 * SSD_GROUPS)] + list(range(XS_TILES)))
        conv_t = {}

        def ssd_in_epilogue(m, bank, t):
            if m < CONV_TILES:
                col = conv_col[m]
                n, acc, t_acc = conv_taps(bank, t, SSD_TAPS, lambda k: par("ssd_conv", k * CONV_TILES + col),
                                          par("ssd_conv", SSD_TAPS * CONV_TILES + col))

                def silu_it():
                    conv_t[m] = A.do(lambda e: e.activation(conv_out[m], acc, ACT.Silu), [t_acc])
                    acc_ring.give(n, [conv_t[m]])
                later(1, silu_it)
                return [t_acc]
            k = m - CONV_TILES
            conv_t[m] = A.do(lambda e: e.activation(tile(z_sb, k), bank[:, 0:S], ACT.Copy),
                             [t, state["tok"], state["acs"]])
            return [conv_t[m]]

        project("w_dt", [0], KD, H, dt_epilogue)
        project("w_ssd_in", range(CONV_TILES + 2), KD, H, ssd_in_epilogue)
        flush()

        AHEAD = 3
        m_ring = Ring([sq[:, i * 3 * P:(i + 1) * 3 * P] for i in range(AHEAD + 1)])
        dec_ring = Ring([ar.get(3 * P) for _ in range(3)])
        ssd_out = OuterProjection("w_ssd_out", XS_TILES)
        in_group, ybank, y_t = {}, {}, {}
        GT = GROUP_TILES

        def open_group(g):
            n, bank, free = banks.take()
            bg, cg = b_sb[:, g * S:(g + 1) * S], c_sb[:, g * S:(g + 1) * S]
            mm(bank[:, 0:S], bg[:, 0:P], cg, True, True, [conv_t[CONV_TILES - 1]] + free)
            t = mm(bank[:, S:S + P], bg[:, P:S], cg[:, P:S], False, True, signal=True)
            cn, cb, cfree = cb_ring.take()
            t_cb = V.do(lambda e: e.tensor_copy(cb, bank[:, 0:3 * P]), [t] + cfree)
            banks.give(n, [t_cb])
            xn, xt, xfree = xs_tok_ring.take()
            for tt in range(TT):
                n, bank, free = banks.take()
                for j in range(GT):
                    t = T.do(lambda e: e.transpose(bank[:, j * P:(j + 1) * P],
                                                   tile(xs_sb, g * GT + j, tt * P, (tt + 1) * P), con("ident")),
                             free, signal=True)
                t_xt = A.do(lambda e: e.activation(xt[:, tt * GT * P:(tt + 1) * GT * P], bank[:, :], ACT.Copy),
                            [t] + xfree)
                banks.give(n, [t_xt])
            in_group[g] = (cn, cb, t_cb, xn, xt, t_xt)

        def decays(h):
            _, cb, t_cb, _, _, _ = in_group[h // GROUP_HEADS]
            n, b, free = banks.take()
            oneh = sel[:, h:h + 1].to_broadcast([hT, P])
            mm(b[:, 0:S], oneh, acs_hi[:, :], True, False, free + [t_sel, state["acs_hi"]])
            mm(b[:, 0:S], oneh, acs_lo[:, :], False, False, [state["acs"]])
            mm(b[:, S:S + P], oneh, acs_hi[:, P:S], False, False)
            mm(b[:, S:S + P], oneh, acs_lo[:, P:S], False, False)
            mm(b[:, 0:P], ident_r[:, :], mask_r[:, :], False, False, [t_mask, t_ident_r])
            t = mm(b[:, S:S + P], ident_r[:, :], mask_r[:, :], False, True, signal=True)
            dn, dec, dfree = dec_ring.take()
            bias = [tok[:, i * hT + h:i * hT + h + 1] for i in (2, 4, 3)]
            for i in range(3):
                te = A.do(lambda e: e.activation(dec[:, i * P:(i + 1) * P], b[:, i * P:(i + 1) * P],
                                                 ACT.Exp, bias=bias[i]), [t, state["tok"]] + dfree)
            banks.give(n, [te])
            mn, mt, mfree = m_ring.take()
            V.do(lambda e: e.scalar_tensor_tensor(mt[:, 0:S], dec[:, 0:S], tok[:, h:h + 1], cb[:, 0:S],
                                                  ALU.mult, ALU.mult), [te, t_cb] + mfree)
            tm = V.do(lambda e: e.scalar_tensor_tensor(mt[:, S:S + P], dec[:, S:S + P], tok[:, hT + h:hT + h + 1],
                                                       cb[:, S:S + P], ALU.mult, ALU.mult))
            dec_ring.give(dn, [tm])
            return mn, mt, tm

        def head_y(h, made):
            g, i = divmod(h, GROUP_HEADS)
            cn, _, _, xn, xt, t_xt = in_group[g]
            mn, mt, tm = made
            half, k = h % 2, h // 2
            if half == 0:
                ybank[k] = banks.take()
            n, b, free = ybank[k]
            rows = slice(half * SSD_P, (half + 1) * SSD_P)
            c0 = i * SSD_P
            mm(b[rows, 0:S], xt[:, c0:c0 + SSD_P], mt[:, 0:S], True, False, [tm, t_xt] + free)
            t = mm(b[rows, P:S], xt[:, GT * P + c0:GT * P + c0 + SSD_P], mt[:, S:S + P], False, True, signal=True)
            m_ring.give(mn, [t])
            if half == 1:
                y_t[k] = V.do(lambda e: e.scalar_tensor_tensor(tile(xs_sb, k), tile(xs_sb, k), par("ssd_d", k),
                                                               b[:, 0:S], ALU.mult, ALU.add), [t])
                banks.give(n, [y_t[k]])
            if i == GROUP_HEADS - 1:
                cb_ring.give(cn, [tm])
                xs_tok_ring.give(xn, [t])

        gated = {}

        def gate_group(g):
            zg, yg = (buf[:, g * GT * S:(g + 1) * GT * S] for buf in (z_sb, xs_sb))
            t = A.do(lambda e: e.activation(zg, zg, ACT.Silu), [conv_t[CONV_TILES + (g + 1) * GT - 1]])
            t = V.do(lambda e: e.tensor_tensor(zg, zg, yg, ALU.mult), [t, y_t[(g + 1) * GT - 1]])
            gated[g] = A.do(lambda e: e.activation(yg, zg, ACT.Square), [t])

        normed = {}

        def norm_group(g):
            n, b, free = banks.take()
            for j in range(GT):
                t = mm(b[:, 0:S], ones, tile(xs_sb, g * GT + j), j == 0, j == GT - 1, [gated[g]] + free, signal=True)
            t_ms, t_free = rstd_of(b[:, 0:S], t, GT * P, [V.last()], ms_sb)
            banks.give(n, [t_free])
            for j in range(GT):
                k = g * GT + j
                normed[k] = V.do(lambda e: e.scalar_tensor_tensor(tile(z_sb, k), tile(z_sb, k), par("ssd_norm_g", k),
                                                                  ms_sb, ALU.mult, ALU.mult), [t_ms])

        def split_for_out(k):
            slot, _, free = gu_ring.take()
            part = Split(g_hi, g_lo, S)
            split_tile(part, slot, tile(z_sb, k), normed[k], free)
            return slot, part

        def out_steps(n):
            ready_parts = [split_for_out(k) for k in (2 * n, 2 * n + 1)]
            for slot, part in ready_parts:
                gu_ring.give(slot, [ssd_out.step(part.part("hi", slot), part.part("lo", slot),
                                                 part.hi_t[slot], part.lo_t[slot])])

        schedule = {}
        for h, what, n in core_schedule():
            schedule.setdefault(h, []).append((what, n))
        open_group(0)
        made = {h: decays(h) for h in range(AHEAD)}
        for h in range(SSD_HEADS):
            g, i = divmod(h, GROUP_HEADS)
            if i == GROUP_HEADS - AHEAD - 1 and g + 1 < SSD_GROUPS:
                open_group(g + 1)
            if h + AHEAD < SSD_HEADS:
                made[h + AHEAD] = decays(h + AHEAD)
            if g and i == 0:
                gate_group(g - 1)
            if g and i == 2:
                norm_group(g - 1)
            for what, n in schedule.get(h, []):
                if what == "z":
                    m = CONV_TILES + 2 * n
                    project("w_ssd_in", [m, m + 1], KD, H, ssd_in_epilogue)
                else:
                    out_steps(n)
            head_y(h, made.pop(h))
        gate_group(SSD_GROUPS - 1)
        norm_group(SSD_GROUPS - 1)
        for n in range(OUT_PAIRS - GT // 2, OUT_PAIRS):
            out_steps(n)
        sums = take_sums()
        ssd_out.finish(residual_epilogue(sums))
        flush()

        class Ada:

            def __init__(self, layer, acc, raw):
                self.layer, self.acc, self.raw, self.i = layer, acc, raw, 0
                self.raw_t = {}
                for i in range(len(raw)):
                    self.load(i, [T.last(), V.last(), A.last()])

            def load(self, i, after):
                slot = i % len(self.raw)
                uses = (self.layer * 2 * KD + i) // len(self.raw) + 1
                self.raw_t[i] = load(self.raw[slot], d[f"w_ada{self.layer}"][i], s_ada[slot], 16 * uses, after)

            def step(self):
                half, k = divmod(self.i, KD)
                raw, t_raw = self.raw[self.i % len(self.raw)], self.raw_t[self.i]
                acc = self.acc[half]
                col = cs_sb[:, k:k + 1]
                if k == 0:
                    t = V.do(lambda e: e.tensor_scalar(acc, raw, col, None, ALU.mult), [t_raw, t_cs])
                else:
                    t = V.do(lambda e: e.scalar_tensor_tensor(acc, raw, col, acc, ALU.mult, ALU.add),
                             [t_raw, self.t])
                if self.i + len(self.raw) < 2 * KD:
                    self.load(self.i + len(self.raw), [t])
                self.t = t
                self.i += 1

            def finish(self):
                assert self.i == 2 * KD
                lay = self.layer
                mod = mod_sb[:, lay * 3 * KD:(lay + 1) * 3 * KD]
                n, bank, free = banks.take()
                for m in range(3 * KD):
                    half, j = divmod(m, ADA_W // P)
                    t = mm(bank[:, m:m + 1], self.acc[half][:, j * P:(j + 1) * P], ones[:, 0:1], m == 0, True,
                           [self.t] + free, signal=True)
                t = V.do(lambda e: e.tensor_tensor(mod, bank[:, 0:3 * KD], par("b_ada", lay * 3 * KD, 3 * KD), ALU.add),
                         [t])
                banks.give(n, [t])
                t = V.do(lambda e: e.scalar_tensor_tensor(mod[:, KD:2 * KD], mod[:, KD:2 * KD], 1.0,
                                                          par("g_pre", lay * KD, KD), ALU.add, ALU.mult), [t])
                t_mod[lay] = V.do(lambda e: e.tensor_tensor(mod[:, 2 * KD:3 * KD], mod[:, 2 * KD:3 * KD],
                                                            par("g_post", lay * KD, KD), ALU.mult), [t])
        t_cs = A.do(lambda e: e.activation(cs_sb[:, :], par("c", 0, KD), ACT.Silu), [t_params])
        t_mod = {}

        def ffn(layer, sums):
            norm_into_h((sums[0], sums[1], sums[3]), lambda k: par("ffn_g", layer * KD + k))
            base = layer * (FFN_TAPS + 1) * 2 * FF_TILES
            ar = Arena()
            acc_ring = Ring([ar.get(S) for _ in range(5)])
            gate_ring = Ring([ar.get(S) for _ in range(2)])
            prod_ring = Ring([ar.get(S) for _ in range(3)])
            hold = {}

            def epilogue(m, bank, t):
                i, is_up = m // 2, m % 2
                col = base + (FF_TILES if is_up else 0) + i
                n, acc, free = acc_ring.take()
                t_acc = A.do(lambda e: e.activation(acc, bank[:, 0:S], ACT.Identity,
                                                    bias=par("ffn_conv", col + FFN_TAPS * 2 * FF_TILES),
                                                    scale=par("ffn_conv", col + (FFN_TAPS - 1) * 2 * FF_TILES)),
                             [t] + free)
                for back in range(1, FFN_TAPS):
                    t_acc = V.do(lambda e, back=back: e.scalar_tensor_tensor(
                        acc[:, back:S], bank[:, 0:S - back],
                        par("ffn_conv", col + (FFN_TAPS - 1 - back) * 2 * FF_TILES), acc[:, back:S],
                        ALU.mult, ALU.add), [t_acc])
                if not is_up:
                    def gate_it():
                        gn, gate, gfree = gate_ring.take()
                        tg = A.do(lambda e: e.activation(gate, acc, ACT.Silu), [t_acc] + gfree)
                        acc_ring.give(n, [tg])
                        hold[i] = (gn, gate, tg)
                    later(1, gate_it)
                    return [t_acc]

                def multiply():
                    gn, gate, tg = hold[i]
                    pn, prod, pfree = prod_ring.take()
                    tp = V.do(lambda e: e.tensor_tensor(prod, gate, acc, ALU.mult), [tg, t_acc] + pfree)
                    acc_ring.give(n, [tp])
                    gate_ring.give(gn, [tp])
                    slot, _, sfree = gu_ring.take()
                    part = Split(g_hi, g_lo, S)
                    prod_ring.give(pn, split_tile(part, slot, prod, tp, sfree))
                    products[i] = (slot, part)
                later(1, multiply)
                return [t_acc]

            products = {}
            down = OuterProjection(f"w_down{layer}", FF_TILES)
            ada = Ada(layer, [ar.get(ADA_W) for _ in range(2)], [ar.get(ADA_W) for _ in range(ADA_SLOTS)])
            for i in range(FF_TILES + 2):
                if i in ADA_AT:
                    ada.step()
                if i < FF_TILES:
                    project(f"w_up{layer}", [2 * i, 2 * i + 1], KD, H, epilogue)
                if i == FF_TILES:
                    flush()
                if i % 2 and i >= 3:
                    for k in (i - 3, i - 2):
                        slot, part = products.pop(k)
                        gu_ring.give(slot, [down.step(part.part("hi", slot), part.part("lo", slot),
                                                      part.hi_t[slot], part.lo_t[slot])])
            ada.finish()
            out_sums = take_sums()
            down.finish(residual_epilogue(out_sums))
            flush()
            return out_sums

        sums = ffn(0, sums)

        def attend(units, scratch, groups):
            e_ring = Ring([scratch.get(groups * 2 * S) for _ in range(4)])
            p_ring = Ring([scratch.get(2 * S) for _ in range(3)])
            n_ring = Ring([scratch.get(4 * groups) for _ in range(4)])
            made = {}

            def scores(i):
                u = units[i]
                nk = u["nk"]
                en, eb, efree = e_ring.take()
                nn, columns, nfree = n_ring.take()
                sums = columns[:, 2 * groups:4 * groups]
                for g in range(groups):
                    n, bank, free = banks.take()
                    pair = u["scores"][2 * g:2 * g + 2]
                    for j, (q, k, _) in enumerate(pair):
                        t = mm(bank[:, j * S:j * S + nk], q, k, j == 0, True, u["after"] + free, signal=True)
                    for j, (_, _, bias) in enumerate(pair):
                        c = 2 * g + j
                        e_tile = eb[:, c * S:c * S + nk]
                        tv = V.do(lambda e: e.tensor_tensor_reduce(
                            e_tile, bank[:, j * S:j * S + nk], bias, -1.0, 3.0e38,
                            ALU.add, ALU.min, columns[:, c:c + 1]), [t] + efree + nfree + u["after"])
                        te = A.do(lambda e: e.activation(e_tile, e_tile, ACT.Exp, bias=columns[:, c:c + 1],
                                                         scale=-1.0, accum_out=sums[:, c:c + 1]), [tv])
                    banks.give(n, [tv])
                made[i] = [en, eb, nn, sums, te]

            def weigh(i):
                en, eb, nn, sums, te = made[i]
                t = V.do(lambda e: e.reciprocal(sums, sums), [te])
                t = units[i]["weigh"](eb, sums, t)
                n_ring.give(nn, [t])
                made[i] = [en, eb, t]

            def turn(i):
                nk = units[i]["nk"]
                en, eb, te = made[i]
                n, bank, free = banks.take()
                pn, pb, pfree = p_ring.take()
                kts = nk // P
                for j in range(2):
                    for kt in range(kts):
                        at = (j * kts + kt) * P
                        t = T.do(lambda e: e.transpose(bank[:, at:at + P], eb[:, j * S + kt * P:j * S + (kt + 1) * P],
                                                       con("ident")), [te] + free, signal=True)
                e_ring.give(en, [t])
                w = 2 * kts * P
                if i % 2:
                    tc = A.do(lambda e: e.activation(pb[:, 0:w], bank[:, 0:w], ACT.Copy), [t] + pfree)
                else:
                    tc = V.do(lambda e: e.tensor_copy(pb[:, 0:w], bank[:, 0:w]), [t] + pfree)
                banks.give(n, [tc])
                made[i] = [pn, pb, tc]

            def values(i):
                u = units[i]
                kts = u["nk"] // P
                pn, pb, tc = made.pop(i)
                bank, after = u["bank"]()
                for j in range(2):
                    for kt in range(kts):
                        at = (j * kts + kt) * P
                        t = mm(u["out"](bank, j), u["values"][j][kt], pb[:, at:at + P], u["start"] and kt == 0,
                               kt == kts - 1, [tc] + after + u["after"], signal=kt == kts - 1)
                p_ring.give(pn, [t])
                u["then"](t)

            for i in range(len(units) + 3):
                if i < len(units):
                    scores(i)
                if 1 <= i < len(units) + 1:
                    weigh(i - 1)
                if 2 <= i < len(units) + 2:
                    turn(i - 2)
                if i >= 3:
                    values(i - 3)
                tick()
            flush()

        norm_into_h((sums[0], sums[1], sums[3]), lambda k: par("mix_g", KD + k))
        ar = Arena()
        q_sb, k_sb = ar.get(KD * S), ar.get(KD * S)
        v_sb = ar.get(TT * D)
        cos_sb, sin_sb = ar.get(S), ar.get(S)
        pos_f, ang, kk_f = ar.get(S), ar.get(S), ar.get(S)
        pos_i = arena[:, ar.at:ar.at + S].bitcast(I32)
        ar.at += S
        sq_ring = Ring([ar.get(S) for _ in range(4)])
        rs_ring = Ring([ar.get(S) for _ in range(3)])
        t_pos = load(pos_i, d["positions"], s_pos, 16, [T.last(), V.last(), A.last()])
        chain = lambda fn, after=(): V.do(fn, [V.last()] + list(after))
        chain(lambda e: e.tensor_copy(pos_f, pos_i), [t_pos, T.last(), A.last()])
        chain(lambda e: e.tensor_scalar(ang, pos_f, con("inv_freq"), None, ALU.mult))
        chain(lambda e: e.tensor_scalar(kk_f, ang, 1.0 / (2 * math.pi), 12582912.0, ALU.mult, ALU.add))
        chain(lambda e: e.tensor_scalar(kk_f, kk_f, -12582912.0, None, ALU.add))
        for part in TWO_PI_PARTS:
            chain(lambda e, part=part: e.scalar_tensor_tensor(ang, kk_f, -part, ang, ALU.mult, ALU.add))
        chain(lambda e: e.tensor_scalar(ang, ang, 3.1415925, -3.1415925, ALU.min, ALU.max))
        t_sin = A.do(lambda e: e.activation(sin_sb, ang, ACT.Sin), [V.last()])
        chain(lambda e: e.tensor_scalar(kk_f, ang, -1.0, None, ALU.mult))
        chain(lambda e: e.tensor_tensor(kk_f, kk_f, ang, ALU.max))
        chain(lambda e: e.tensor_scalar(kk_f, kk_f, -1.0, half_pi, ALU.mult, ALU.add))
        t_cos = A.do(lambda e: e.activation(cos_sb, kk_f, ACT.Sin), [V.last()])
        qg = small[:, 2:3]
        chain(lambda e: e.tensor_scalar(qg, par("q_g"), 1.0 / math.sqrt(HD), None, ALU.mult), [t_params])
        for i in range(2):
            chain(lambda e, i=i: e.tensor_tensor_reduce(kk_f[:, 0:HD], par("lam", 2 * i * HD, HD),
                                                        par("lam", (2 * i + 1) * HD, HD), 1.0, 0.0, ALU.mult, ALU.add,
                                                        small[:, 4 + i:5 + i]), [t_cos])
        t_lam = A.do(lambda e: e.activation(small[:, 6:8], small[:, 4:6], ACT.Exp), [V.last()])
        lam = small[:, 8:9]
        chain(lambda e: e.tensor_tensor(lam, small[:, 6:7], small[:, 7:8], ALU.subtract), [t_lam])
        chain(lambda e: e.tensor_scalar(lam, lam, LAMBDA_INIT, None, ALU.add))
        sg = small[:, 3:4]
        t_small = chain(lambda e: e.tensor_scalar(sg, par("subln_g"), 1.0 - LAMBDA_INIT, None, ALU.mult))

        def qk_epilogue(m, bank, t):
            dst = tile(q_sb, m) if m < KD else tile(k_sb, m - KD)
            gain = qg if m < KD else par("k_g")
            t_raw = A.do(lambda e: e.activation(dst, bank[:, 0:S], ACT.Copy), [t])
            sn, s2, sfree = sq_ring.take()
            t_sq = A.do(lambda e: e.activation(s2, bank[:, 0:S], ACT.Square), [t] + sfree)

            def head_sums():
                n, b, free = banks.take()
                ts = mm(b[:, 0:S], con("block_ones"), s2, True, True, [t_sq] + free, signal=True)
                rn, rs, rfree = rs_ring.take()
                t2, t1 = rstd_of(b[:, 0:S], ts, HD, rfree, rs)
                banks.give(n, [t1])
                t3 = V.do(lambda e: e.scalar_tensor_tensor(dst, dst, gain, rs, ALU.mult, ALU.mult), [t2, t_raw, t_small])
                rs_ring.give(rn, [t3])

                def rotate():
                    n, b, free = banks.take()
                    tr = mm(b[:, 0:S], con("rope_perm"), dst, True, True, [t3] + free, signal=True)
                    t4 = V.do(lambda e: e.tensor_tensor(s2, b[:, 0:S], sin_sb, ALU.mult), [tr, t_sin])
                    banks.give(n, [t4])
                    t5 = V.do(lambda e: e.tensor_tensor(dst, dst, cos_sb, ALU.mult), [t_cos, tr])
                    qk_t[m] = V.do(lambda e: e.tensor_tensor(dst, dst, s2, ALU.add), [t4, t5])
                    sq_ring.give(sn, [qk_t[m]])
                later(1, rotate)
            later(1, head_sums)
            return [t_sq]
        qk_t = {}
        project("w_attn_in", range(2 * KD), KD, H, qk_epilogue)
        v_t = []
        for c in range(D // S):
            def v_epilogue(tt, bank, t, c=c):
                v_t.append(A.do(lambda e: e.activation(v_sb[:, tt * D + c * S:tt * D + (c + 1) * S], bank[:, 0:S],
                                                       ACT.Copy), [t]))
                return [v_t[-1]]
            project_rows("w_attn_v", S, H, v_epilogue)
        flush()

        ready = [qk_t[m] for m in range(2 * KD)] + v_t
        sc = Arena()
        sc.at = ar.at - 12 * S
        o_sq_ring = Ring([sc.get(S) for _ in range(2)])
        o_rs_ring = Ring([sc.get(S) for _ in range(2)])
        Y = Split(h_hi, h_lo, S)
        units = []

        def diff_unit(qb, heads):
            nk = (qb + 1) * P
            taken = {}

            def weigh(eb, rl, t):
                for j in range(2):
                    p0, p1 = (eb[:, (2 * c + j) * S:(2 * c + j) * S + nk] for c in range(2))
                    t1 = V.do(lambda e: e.tensor_scalar(p1, p1, rl[:, 2 + j:3 + j], lam, ALU.mult, ALU.mult), [t])
                    t2 = V.do(lambda e: e.scalar_tensor_tensor(p0, p0, rl[:, j:j + 1], p1, ALU.mult, ALU.subtract),
                              [t1])
                return t2

            def bank():
                taken["bank"] = banks.take()
                return taken["bank"][1:]

            def then(t):
                n, b, _ = taken["bank"]
                o, sums = b[:, 0:S], b[:, S:2 * S]
                sn, o_sq, sfree = o_sq_ring.take()
                t_sq = A.do(lambda e: e.activation(o_sq, o, ACT.Square), [t] + sfree)

                def norm():
                    t_sum = mm(sums, ones, o_sq, True, True, [t_sq], signal=True)
                    rn, rs, rfree = o_rs_ring.take()
                    t_rs, _ = rstd_of(sums, t_sum, 2 * HD, rfree, rs)
                    t_o = V.do(lambda e: e.scalar_tensor_tensor(o_sq, o, sg, rs, ALU.mult, ALU.mult), [t_rs])
                    banks.give(n, [t_o])
                    o_rs_ring.give(rn, [t_o])
                    view = lambda buf: buf[:, heads[0] * S:(heads[1] + 1) * S].rearrange(
                        "p (h c) -> p h c", h=2)[:, :, qb * P:(qb + 1) * P]
                    o3 = o_sq.rearrange("p (h c) -> p h c", h=2)
                    t_hi = A.do(lambda e: e.activation(view(h_hi), o3, ACT.Copy), [t_o])
                    t_lo = V.do(lambda e: e.tensor_tensor(view(h_lo), o3, view(h_hi).bitcast(F32), ALU.subtract),
                                [t_hi])
                    o_sq_ring.give(sn, [t_lo])
                    for h in heads:
                        Y.hi_t[h], Y.lo_t[h] = t_hi, t_lo
                later(1, norm)

            return dict(
                nk=nk, after=ready, weigh=weigh, bank=bank, then=then, start=True,
                scores=[(q_sb[c * HD:(c + 1) * HD, h * S + qb * P:h * S + (qb + 1) * P],
                         k_sb[c * HD:(c + 1) * HD, h * S:h * S + nk], con("chunk_mask", S - nk, nk))
                        for c in range(2) for h in heads],
                values=[[v_sb[:, kt * D + h * P:kt * D + (h + 1) * P] for kt in range(qb + 1)] for h in heads],
                out=lambda b, j: b[:, j * P:(j + 1) * P])

        for qb in range(TT):
            for pair in range(A_HEADS // 2):
                units.append(diff_unit(qb, (2 * pair, 2 * pair + 1)))
        attend(units, sc, 2)
        sums = take_sums()
        project("w_attn_out", range(KD), KD, Y, residual_epilogue(sums))
        flush()
        sums = ffn(1, sums)

        alibi = sb("alibi_sb", [P, H_HEADS * S])
        t_alibi = load(alibi[:, :], d["alibi"], s_alibi, 16)

        def hybrid(layer, sums):
            mod = mod_sb[:, layer * 3 * KD:(layer + 1) * 3 * KD]
            norm_into_h((sums[0], sums[1], sums[3]), lambda k: mod[:, KD + k:KD + k + 1], lambda k: mod[:, k:k + 1])
            ar = Arena()
            qn_sb, qm_sb, km_sb = ar.get(4 * S), ar.get(4 * S), ar.get(4 * S)
            zs = ar.get(8 * S)
            kdup = {"s": ar.get(2 * S), "w": ar.get(2 * S)}
            vm = ar.get(TT * 512)
            vsw = ar.get(TT * VSG)
            kc_pair = ar.get(H_GROUPS * 2 * CMP_W)
            vc_pair = ar.get(H_HEADS * HD)
            gates = ar.get(TT * 24)
            pc = ar.get(TT * H_HEADS * CMP_W)
            pcT = ar.get(TT * H_HEADS * CMP_W)
            st = ar.get(TT * 2 * H_HEADS)
            sc = Arena()
            sc.at = ar.at
            slab = {"k": ar.get(3 * S), "v": ar.get(3 * S)}
            ck = ar.get(2 * CMP_PAIRS * HD)
            ck2 = ar.get(2 * HD)
            gel = ar.get(2 * 32)
            done = [T.last(), V.last(), A.last()]
            t_ck = load(ck, d[f"ck1_{layer}"], s_cmp[layer], 16, done)
            t_ck = load(ck2[0:HD, :], d[f"ck2_{layer}"], s_cmp[layer], 32)
            t_zero = {}
            for kind in "kv":
                t_zero[kind] = V.do(lambda e, b=slab[kind]: e.memset(b, 0.0), done)
            pe_dst = {kind: slab[kind][:, 2 * S:2 * S + CMP_LEN].rearrange("p (j two) -> p j two", two=2)[:, :, 0:1]
                      for kind in "kv"}
            pe_in = gel
            t_ck = load(pe_in[:, 0:2 * CMP_PAIRS], d[f"pe_{layer}"], s_cmp[layer], 48)
            t_pe = {}
            for i, kind in enumerate("kv"):
                t_pe[kind] = V.do(lambda e, kind=kind, i=i: e.tensor_copy(
                    pe_dst[kind], pe_in[:, i * CMP_PAIRS:(i + 1) * CMP_PAIRS].unsqueeze(2)), [t_ck, t_zero[kind]])
            got = {}

            def kv_epilogue(m, bank, t):
                if m < 2:
                    b = slab["kv"[m]]
                    for g in range(2):
                        src = bank[g * HD:(g + 1) * HD, :]
                        V.do(lambda e, src=src, g=g: e.tensor_copy(b[0:HD, g * S:(g + 1) * S], src[:, 0:S]),
                             [t, t_pe["kv"[m]]])
                        t1 = V.do(lambda e, src=src, g=g: e.tensor_copy(b[HD:P, g * S:g * S + S - 1], src[:, 1:S]),
                                  [t])
                else:
                    b = kdup["sw"[m - 2]]
                    for g in range(2):
                        src = bank[g * HD:(g + 1) * HD, 0:S]
                        for half in range(2):
                            t1 = A.do(lambda e, src=src, g=g, half=half: e.activation(
                                b[half * HD:(half + 1) * HD, g * S:(g + 1) * S], src, ACT.Copy), [t] + done)
                got[("kv", m)] = t1
                return [t1]

            def vsg_epilogue(tt, bank, t):
                t1 = A.do(lambda e: e.activation(vsw[:, tt * VSG:(tt + 1) * VSG], bank[:, 0:VSG], ACT.Copy), [t] + done)
                got[("vsg", tt)] = t1
                t2 = A.do(lambda e: e.activation(gates[:, tt * 24:(tt + 1) * 24], bank[:, 2 * P:VSG], ACT.Sigmoid), [t])
                got[("gates", tt)] = t2
                return [t2]

            def qz_epilogue(m, bank, t):
                kind, k = ("qn", "qm", "km", "zm", "zn")[m // 4], m % 4
                if kind in ("zm", "zn"):
                    dst = tile(zs, k + (4 if kind == "zn" else 0))
                    got[m] = A.do(lambda e: e.activation(dst, bank[:, 0:S], ACT.Silu), [t] + done)
                else:
                    dst = tile({"qn": qn_sb, "qm": qm_sb, "km": km_sb}[kind], k)
                    scale = 1.0 if kind == "km" else HD ** -0.5
                    got[m] = A.do(lambda e: e.activation(dst, bank[:, 0:S], ACT.Copy, scale=scale), [t] + done)
                return [got[m]]

            project(f"w_kv{layer}", range(4), KD, H, kv_epilogue)
            project_rows(f"w_vsg{layer}", VSG, H, vsg_epilogue)

            for buf in (pc, kc_pair, vc_pair):
                zero_t = V.do(lambda e: e.memset(buf, 0.0), done)
            for i, kind in enumerate("kv"):
                n, bank, free = banks.take()
                s3 = slab[kind].rearrange("p (g t) -> p g t", g=3)
                for j in range(CMP_PAIRS):
                    rhs = s3[:, :, 2 * j:2 * j + (CMP_T - 1) * CMP_STRIDE + 1:CMP_STRIDE]
                    at = (i * CMP_PAIRS + j) * HD
                    t = mm(bank[0:HD, 0:3 * CMP_T].rearrange("p (g t) -> p g t", g=3), ck[:, at:at + HD], rhs,
                           j == 0, j == CMP_PAIRS - 1, [t_ck, got[("kv", i)]] + free, signal=j == CMP_PAIRS - 1)
                gp = gel[0:HD, 0:2 * 32].rearrange("p (g t) -> p g t", g=2)[:, :, 0:CMP_T]
                t1 = V.do(lambda e, bank=bank: e.tensor_copy(st[0:HD, 0:1], bank[0:HD, 2 * CMP_T:2 * CMP_T + 1]),
                          [t, t_pe["v"]] + done)
                t2 = A.do(lambda e, bank=bank, gp=gp: e.activation(
                    gp, bank[0:HD, 0:2 * CMP_T].rearrange("p (g t) -> p g t", g=2),
                    ACT.Gelu_apprx_tanh, bias=st[0:HD, 0:1]), [t1, t_pe["v"], T.last()])
                banks.give(n, [t2])
                n, bank, free = banks.take()
                for g in range(2):
                    gx = gel[0:HD, g * 32:g * 32 + CMP_T]
                    if kind == "k":
                        for half in range(2):
                            t = mm(bank[half * HD:(half + 1) * HD, g * 32:g * 32 + CMP_T], ck2[0:HD, 0:HD], gx,
                                   g == 0, True, [t2] + free, signal=True)
                    else:
                        t = mm(bank[0:CMP_T, g * HD:(g + 1) * HD], gx, ck2[0:HD, HD:2 * HD], g == 0, True,
                               [t2] + free, signal=True)
                if kind == "k":
                    for j in range(2):
                        rows = slice(j * HD, (j + 1) * HD)
                        t3 = V.do(lambda e: e.tensor_copy(
                            kc_pair[rows, :].rearrange("p (g t) -> p g t", g=2)[:, :, j * CMP_W:j * CMP_W + CMP_T],
                            bank[rows, 0:64].rearrange("p (g t) -> p g t", g=2)[:, :, 0:CMP_T]), [t, zero_t])
                else:
                    for r in range(HPG):
                        t3 = V.do(lambda e: e.tensor_copy(
                            vc_pair[CMP_W * r:CMP_W * r + CMP_T, :].rearrange("p (g c) -> p g c", g=2)[
                                :, :, r * HD:(r + 1) * HD],
                            bank[0:CMP_T, 0:2 * HD].rearrange("p (g c) -> p g c", g=2)), [t, zero_t])
                got[("cmp", kind)] = t3
                banks.give(n, [t3])
            for c in range(2):
                def vm_epilogue(tt, bank, t, c=c):
                    got[("vm", tt, c)] = A.do(lambda e: e.activation(
                        vm[:, tt * 512 + c * S:tt * 512 + (c + 1) * S], bank[:, 0:S], ACT.Copy), [t] + done)
                    return [got[("vm", tt, c)]]
                project_rows(f"w_vm{layer}", S, H, vm_epilogue)
            project(f"w_qz{layer}", range(20), KD, H, qz_epilogue)
            flush()

            ready = [A.last(), V.last(), t_alibi]
            Y = Split(h_hi, h_lo, S)
            units = []
            obank = {}
            KINDS = ("m", "s", "w")
            HEAD_PAIRS = ((0, 2), (1, 3), (4, 6), (5, 7))

            def head(kind, h, qb):
                r = (h % 2) * HD
                g = h // HPG
                q = (qm_sb if kind == "m" else qn_sb)[r:r + HD, (h // 2) * S + qb * P:(h // 2) * S + (qb + 1) * P]
                nk = (qb + 1) * P
                if kind == "m":
                    return q, km_sb[r:r + HD, (h // 2) * S:(h // 2) * S + nk], [
                        vm[:, kt * 512 + h * HD:kt * 512 + (h + 1) * HD] for kt in range(qb + 1)]
                at = 0 if kind == "s" else P
                return q, kdup[kind][r:r + HD, g * S:g * S + nk], [
                    vsw[:, kt * VSG + at + g * HD:kt * VSG + at + (g + 1) * HD] for kt in range(qb + 1)]

            def gate_out(qb, first_tile, bank, t):
                view = lambda buf: buf[:, first_tile * S:(first_tile + 4) * S].rearrange(
                    "p (h c) -> p h c", h=4)[:, :, qb * P:(qb + 1) * P]
                full = view(zs)
                t1 = V.do(lambda e: e.tensor_tensor(full, bank.rearrange("p (h c) -> p h c", h=4), full, ALU.mult), [t])
                t2 = A.do(lambda e: e.activation(view(h_hi), full, ACT.Copy), [t1])
                t3 = V.do(lambda e: e.tensor_tensor(view(h_lo), full, view(h_hi).bitcast(F32), ALU.subtract), [t2])
                for j in range(4):
                    Y.hi_t[first_tile + j], Y.lo_t[first_tile + j] = t2, t3
                return t1

            heads_of = lambda a: a.rearrange("p (h t) -> p h t", h=H_HEADS)
            g3 = lambda qb: gates[:, qb * 24:(qb + 1) * 24].rearrange("p (h i) -> p h i", i=3)
            W8 = H_HEADS * CMP_W

            def compressed_scores(qb):
                n, b, free = banks.take()
                for m in range(H_HEADS // 2):
                    t = mm(b[:, m * 2 * CMP_W:(m + 1) * 2 * CMP_W], qn_sb[:, m * S + qb * P:m * S + (qb + 1) * P],
                           kc_pair[:, (m // 2) * 2 * CMP_W:(m // 2 + 1) * 2 * CMP_W], m == 0, True,
                           ready + free, signal=True)
                v3 = heads_of(pc[:, qb * W8:(qb + 1) * W8])[:, :, 0:CMP_T]
                bias = heads_of(con("cmp_bias", qb * H_HEADS * CMP_T, H_HEADS * CMP_T))
                mx = st[:, qb * 2 * H_HEADS:qb * 2 * H_HEADS + H_HEADS]
                t = V.do(lambda e: e.tensor_tensor(v3, heads_of(b[:, 0:W8])[:, :, 0:CMP_T], bias, ALU.add),
                         [t, zero_t])
                banks.give(n, [t])
                t = V.do(lambda e: e.tensor_reduce(mx, v3, AX.X, ALU.max), [t])
                t = V.do(lambda e: e.tensor_tensor(v3, v3, mx.unsqueeze(2).to_broadcast([P, H_HEADS, CMP_T]),
                                                   ALU.subtract), [t])
                cmp_t[qb] = A.do(lambda e: e.activation(v3, v3, ACT.Exp), [t])

            def compressed_turn(qb):
                cols = pc[:, qb * W8:(qb + 1) * W8]
                v3 = heads_of(cols)[:, :, 0:CMP_T]
                ok = con("cmp_ok", qb * CMP_T, CMP_T).unsqueeze(1).to_broadcast([P, H_HEADS, CMP_T])
                sm = st[:, qb * 2 * H_HEADS + H_HEADS:(qb + 1) * 2 * H_HEADS]
                t = V.do(lambda e: e.tensor_reduce(sm, v3, AX.X, ALU.add), [cmp_t[qb]])
                t = V.do(lambda e: e.reciprocal(sm, sm), [t])
                t = V.do(lambda e: e.tensor_tensor(sm.unsqueeze(2), sm.unsqueeze(2), g3(qb)[:, :, 0:1], ALU.mult), [t])
                t = V.do(lambda e: e.tensor_tensor(v3, v3, sm.unsqueeze(2).to_broadcast([P, H_HEADS, CMP_T]),
                                                   ALU.mult), [t])
                t_p = V.do(lambda e: e.tensor_tensor(v3, v3, ok, ALU.mult), [t])

                def turn_it():
                    n, b, free = banks.take()
                    for g in range(2):
                        t = T.do(lambda e: e.transpose(b[:, g * P:(g + 1) * P], cols[:, g * P:(g + 1) * P],
                                                       con("ident")), [t_p] + free, signal=True)
                    cmp_t[qb] = V.do(lambda e: e.tensor_copy(pcT[:, qb * W8:(qb + 1) * W8], b[:, 0:W8]), [t])
                    banks.give(n, [cmp_t[qb]])
                later(1, turn_it)

            def compressed_values(qb, b, free):
                for m in range(H_HEADS // 2):
                    g = m // 2
                    mm(b[:, m * P:(m + 1) * P], vc_pair[:, m * P:(m + 1) * P],
                       pcT[:, qb * W8 + g * P:qb * W8 + (g + 1) * P], m == 0, False, [cmp_t[qb], got[("cmp", "v")]] + free)
            cmp_t = {}

            def hybrid_unit(qb, kn, kind, hn, pair):
                heads = [head(kind, h, qb) for h in pair]
                nk = (qb + 1) * P
                last = hn == len(HEAD_PAIRS) - 1

                def weigh(eb, rl, t):
                    for j, h in enumerate(pair):
                        p = eb[:, j * S:j * S + nk]
                        gate = None if kind == "m" else gates[:, qb * 24 + h * 3 + kn:qb * 24 + h * 3 + kn + 1]
                        t1 = V.do(lambda e: e.tensor_scalar(p, p, rl[:, j:j + 1], gate, ALU.mult,
                                                            *([] if gate is None else [ALU.mult])), [t])
                    return t1

                def bank():
                    if hn == 0 and kind != "w":
                        obank[kind] = banks.take()
                        if kind == "s":
                            compressed_values(qb, obank["s"][1], obank["s"][2])
                    n, b, free = obank["m" if kind == "m" else "s"]
                    return b, free

                def then(t):
                    if last and kind != "s":
                        n, b, _ = obank["m" if kind == "m" else "s"]
                        banks.give(n, [gate_out(qb, 0 if kind == "m" else 4, b, t)])

                return dict(nk=nk, after=ready, weigh=weigh, bank=bank, then=then, start=kind == "m",
                            scores=[(q, k, alibi[:, h * S + S - nk:(h + 1) * S]) for h, (q, k, _) in zip(pair, heads)],
                            values=[v for _, _, v in heads],
                            out=lambda b, j: b[(pair[j] % 2) * HD:(pair[j] % 2 + 1) * HD,
                                               (pair[j] // 2) * P:(pair[j] // 2 + 1) * P])

            for qb in range(TT):
                for kn, kind in enumerate(KINDS):
                    for hn, pair in enumerate(HEAD_PAIRS):
                        units.append(hybrid_unit(qb, kn, kind, hn, pair))
            for qb in range(TT):
                compressed_scores(qb)
                later(qb, lambda qb=qb: compressed_turn(qb))
            attend(units, sc, 1)

            y_sb = sq
            ys = arena[:, 0:KD * S]
            n_s, s_bank, s_free = banks.take()
            sum_t = [None]

            def out_epilogue(m, bank, t):
                t1 = V.do(lambda e: e.tensor_copy(tile(y_sb, m), bank[:, 0:S]), [t])
                t2 = A.do(lambda e: e.activation(tile(ys, m), tile(y_sb, m), ACT.Square), [t1])

                def add_up():
                    sum_t[0] = mm(s_bank[:, 0:S], ones, tile(ys, m), m == 0, m == KD - 1,
                                  [t2] + s_free, signal=True)
                later(1, add_up)
                return [t1]
            project(f"w_out{layer}", range(KD), KD, Y, out_epilogue)
            flush()
            t_rstd, t_free = rstd_of(s_bank[:, 0:S], sum_t[0], D, [V.last()])
            banks.give(n_s, [t_free])
            nxt = take_sums()
            for k in range(KD):
                t1 = V.do(lambda e, k=k: e.scalar_tensor_tensor(tile(y_sb, k), tile(y_sb, k),
                                                                mod[:, 2 * KD + k:2 * KD + k + 1], rstd_sb[:, :],
                                                                ALU.mult, ALU.mult), [t_rstd])
                t2 = V.do(lambda e, k=k: e.tensor_tensor(tile(xT, k), tile(xT, k), tile(y_sb, k), ALU.add), [t1])
                x_t[k] = t2
                if layer == DEPTH - 1:
                    continue
                t3 = A.do(lambda e, k=k: e.activation(tile(ys, k), tile(xT, k), ACT.Square), [t2, sum_t[0]])
                nxt[3] = mm(nxt[1][:, 0:S], ones, tile(ys, k), k == 0, k == KD - 1, [t3] + nxt[2], signal=True)
            return nxt

        x_t = {}
        for layer in range(DEPTH):
            sums = hybrid(layer, sums)
        for half in range(2):
            c = slice(half * KD * S // 2, (half + 1) * KD * S // 2)
            load(d["out"][:, c], xT[:, c], s_out, 16 * (half + 1), [x_t[(half + 1) * KD // 2 - 1]])
        L.wait([(s_out, 32)])
        assert W.loaded == len(plan) and W.used == len(W.units)


def _columns(a):
    a = np.asarray(a)
    n = a.shape[-1] // P
    a = a.reshape(-1, n, P)
    return a.transpose(2, 0, 1).reshape(P, -1)


def _tiles(w, per_chunk):
    k, m = w.shape[0] // P, w.shape[1] // P
    a = w.reshape(k, P, m, P).transpose(2, 1, 0, 3)
    a = a.reshape(m // per_chunk, per_chunk, P, k * P).transpose(0, 2, 1, 3)
    return np.ascontiguousarray(a.reshape(m // per_chunk, P, per_chunk * k * P))


def _rows(w, width):
    k, n = w.shape[0] // P, w.shape[1] // width
    return np.ascontiguousarray(w.reshape(k, P, n, width).transpose(2, 1, 0, 3).reshape(n, P, k * width))


def _pairs(w):
    k, m = w.shape[0] // P, w.shape[1]
    return np.ascontiguousarray(w.reshape(k // 2, 2, P, m).transpose(0, 2, 1, 3).reshape(k // 2, P, 2 * m))


def layout(i):
    a = {k: np.asarray(v) for k, v in i.items()}
    out = {}
    out["x"] = np.ascontiguousarray(a["x"][0].T.reshape(KD, P, S).transpose(1, 0, 2).reshape(P, KD * S))
    out["positions"] = np.ascontiguousarray(np.broadcast_to(a["positions"][0][None, :], (P, S)))
    p = np.zeros((P, NPARAMS), np.float32)

    def put(name, v, rows=P):
        at, n = PARAMS[name]
        p[0:rows, at:at + n] = np.asarray(v).reshape(rows, n)

    put("mix_g", _columns(a["norm_mix_g"]))
    put("ffn_g", _columns(a["norm_ffn_g"]))
    put("ssd_conv", _columns(np.concatenate([a["ssd_conv_w"][0], a["ssd_conv_b"]], 0)))
    put("ssd_norm_g", _columns(a["ssd_norm_g"]))
    put("ssd_d", _columns(np.repeat(a["ssd_d"][0], SSD_P)))
    put("dt_bias", a["ssd_dt_bias"][0], SSD_HEADS)
    put("a_log", a["ssd_a_log"][0], SSD_HEADS)
    put("ffn_conv", np.concatenate([_columns(np.concatenate([a["ffn_conv_w"][n], a["ffn_conv_b"][n:n + 1]], 0))
                                    for n in range(DEPTH)], 1))
    put("q_g", np.tile(a["attn_q_norm_g"][0], 2))
    put("k_g", np.tile(a["attn_k_norm_g"][0], 2))
    put("subln_g", a["attn_subln_g"][0])
    put("lam", np.broadcast_to(np.concatenate([a[f"attn_{n}"][0] for n in ("lq1", "lk1", "lq2", "lk2")])[None, :],
                               (P, 4 * HD)))
    put("c", _columns(a["c_2"]))
    put("b_ada", _columns(a["b_ada_2"]))
    put("g_pre", _columns(a["g_pre_2"]))
    put("g_post", _columns(a["g_post_2"]))
    out["params"] = p
    w = a["ssd_in_w"][0]
    z, xs, bc, dt = (w[:, 0:SSD_INNER], w[:, SSD_INNER:2 * SSD_INNER],
                     w[:, 2 * SSD_INNER:2 * SSD_INNER + 2 * SSD_GROUPS * SSD_N], w[:, -SSD_HEADS:])
    out["w_dt"] = _tiles(np.concatenate([dt, np.zeros((D, P - SSD_HEADS), np.float32)], 1), 1)
    out["w_ssd_in"] = _tiles(np.concatenate([bc, xs, z], 1), 2)
    out["w_ssd_out"] = _pairs(a["ssd_out_w"][0])
    for n in range(DEPTH):
        up = a["ffn_up_w"][n].reshape(D, 2, FF_TILES, P).transpose(0, 2, 1, 3).reshape(D, 2 * D_FF)
        out[f"w_up{n}"] = _tiles(up, 2)
        out[f"w_down{n}"] = _pairs(a["ffn_down_w"][n])
        out[f"w_ada{n}"] = np.ascontiguousarray(
            a["w_ada_2"][n].reshape(KD, P, 2, ADA_W).transpose(2, 0, 1, 3).reshape(2 * KD, P, ADA_W))
        u = a["w_in_2"][n]
        qm, km, vm, zm, qn = (u[:, j * 512:(j + 1) * 512] for j in range(5))
        kc, vc, ks, vs, kw, vw = (u[:, 2560 + j * P:2560 + (j + 1) * P] for j in range(6))
        gl, zn = u[:, 3328:3352], u[:, 3352:3864]
        out[f"w_kv{n}"] = _tiles(np.concatenate([kc, vc, ks, kw], 1), 2)
        out[f"w_vsg{n}"] = _rows(np.concatenate([vs, vw, gl], 1), VSG)
        out[f"w_vm{n}"] = _rows(vm, S)
        out[f"w_qz{n}"] = _tiles(np.concatenate([qn, qm, km, zm, zn], 1), 2)
        out[f"w_out{n}"] = _tiles(a["w_out_2"][n], 2)
        ck1 = np.stack([a["w_ck1_2"][n], a["w_cv1_2"][n]]).reshape(2, CMP_PAIRS, P, HD)
        out[f"ck1_{n}"] = np.ascontiguousarray(ck1.transpose(2, 0, 1, 3).reshape(P, 2 * CMP_PAIRS * HD))
        out[f"ck2_{n}"] = np.concatenate([a["w_ck2_2"][n], a["w_cv2_2"][n]], 1)
        pe = np.stack([a["pe_k_2"][n], a["pe_v_2"][n]]).reshape(2, CMP_PAIRS, P)
        out[f"pe_{n}"] = np.ascontiguousarray(pe.transpose(2, 0, 1).reshape(P, 2 * CMP_PAIRS))
    qkv = a["attn_in_w"][0]
    out["w_attn_in"] = _tiles(qkv[:, 0:2 * D], 2)
    out["w_attn_v"] = _rows(qkv[:, 2 * D:], S)
    out["w_attn_out"] = _tiles(a["attn_out_w"][0], 2)
    out["consts"], out["alibi"] = constants()
    return out


def kernel(**inputs):
    import concourse.bacc as _bacc
    from concourse import mybir as _mybir
    from concourse.bass_utils import run_bass_kernel_spmd as _run

    nc = _bacc.Bacc("TRN2", target_bir_lowering=False, num_devices=1)
    arrays = layout(inputs)
    d = {name: nc.dram_tensor(name, a.shape, _mybir.dt.from_np(a.dtype), kind="ExternalInput").ap()
         for name, a in arrays.items()}
    d["out"] = nc.dram_tensor("out", (P, KD * S), F32, kind="ExternalOutput").ap()
    build_program(nc, d)
    r = _run(nc, [arrays], core_ids=[0])
    got = np.asarray(r.results[0]["out"])
    return np.ascontiguousarray(got.reshape(P, KD, S).transpose(2, 1, 0).reshape(1, S, D))
```

```python
from contextlib import ExitStack
import math
import numpy as np

import concourse.bass as bass
from concourse import mybir

F32 = mybir.dt.float32
F32R = mybir.dt.float32r
I32 = mybir.dt.int32
ALU = mybir.AluOpType
ACT = mybir.ActivationFunctionType
AX = mybir.AxisListType

P = 128
S = 256
TT = S // P
D = 1024
KD = D // P
DEPTH = 2
SSD_INNER, SSD_HEADS, SSD_GROUPS, SSD_P, SSD_N, SSD_TAPS = 2048, 32, 4, 64, 128, 4
XS_TILES = SSD_INNER // P
CONV_TILES = XS_TILES + 2 * SSD_GROUPS
A_HEADS, HD = 8, 64
D_FF, FFN_TAPS = 2816, 3
FF_TILES = D_FF // P
ROPE_DIM, ROPE_THETA = 16, 500000.0
CHUNK = 64
LAMBDA_INIT = 0.8 - 0.6 * math.exp(-0.3 * 1)
H_HEADS, H_GROUPS = 8, 2
CMP_LEN, CMP_STRIDE = 32, 16
CMP_T = (S - CMP_LEN) // CMP_STRIDE + 1
HPG = H_HEADS // H_GROUPS
CMP_W = 32
CMP_PAIRS = CMP_LEN * HD // P
EPS = 1e-6
NEG = -1e9
FAR = -1e30
VSG = 2 * P + 3 * H_HEADS
UNIT_MAX = KD // 2 * VSG
RAW_MAX = 2 * UNIT_MAX
ADA_TILES = 2
ADA_CHUNKS = 3 * KD // ADA_TILES
TWO_PI_PARTS = (6.28125, 0.0019340515136718750, 1.2556240e-06)

PARAMS = {}


def _param(name, n):
    PARAMS[name] = (PARAMS.get("_n", 0), n)
    PARAMS["_n"] = PARAMS.get("_n", 0) + n


for _name, _n in (("mix_g", DEPTH * KD), ("ffn_g", DEPTH * KD),
                  ("ssd_conv", (SSD_TAPS + 1) * CONV_TILES), ("ssd_norm_g", XS_TILES), ("ssd_d", XS_TILES),
                  ("dt_bias", 1), ("a_log", 1),
                  ("ffn_conv", DEPTH * (FFN_TAPS + 1) * 2 * FF_TILES),
                  ("q_g", 1), ("k_g", 1), ("subln_g", 1), ("lam", 4 * HD),
                  ("b_ada", DEPTH * 3 * KD), ("g_pre", DEPTH * KD), ("g_post", DEPTH * KD)):
    _param(_name, _n)
NPARAMS = PARAMS["_n"]

CONSTS = {}


def _const(name, n):
    CONSTS[name] = (CONSTS.get("_n", 0), n)
    CONSTS["_n"] = CONSTS.get("_n", 0) + n


for _name, _n in (("ident", P), ("ones", P), ("block_ones", P), ("rope_perm", P), ("inv_freq", 1),
                  ("chunk_mask", S), ("causal_far", P), ("cmp_bias", TT * H_HEADS * CMP_T), ("cmp_ok", TT * CMP_T)):
    _const(_name, _n)
NCONSTS = CONSTS["_n"]


def constants():
    c = np.zeros((P, NCONSTS), np.float32)

    def put(name, a):
        at, n = CONSTS[name]
        c[:, at:at + n] = np.asarray(a, np.float32).reshape(P, n)

    r = np.arange(P)
    put("ident", np.eye(P))
    put("ones", np.ones((P, P)))
    put("block_ones", (r[:, None] // HD) == (r[None, :] // HD))
    perm = np.zeros((P, P))
    half = ROPE_DIM // 2
    for base in (0, HD):
        for i in range(half):
            perm[base + half + i, base + i] = -1.0
            perm[base + i, base + half + i] = 1.0
    put("rope_perm", perm)
    inv = np.float32(ROPE_THETA) ** (-np.arange(0, ROPE_DIM, 2, dtype=np.float32) / np.float32(ROPE_DIM))
    col = np.zeros(P)
    for base in (0, HD):
        col[base:base + half] = inv
        col[base + half:base + 2 * half] = inv
    put("inv_freq", col)
    chunk = np.where((r[None, :] // CHUNK) <= (r[:, None] // CHUNK), 0.0, FAR)
    put("chunk_mask", np.concatenate([np.zeros((P, P)), chunk], 1))
    put("causal_far", np.where(r[None, :] >= r[:, None], 0.0, FAR))
    slopes = (2.0 ** (-8.0 * np.arange(1, H_HEADS + 1) / H_HEADS)).astype(np.float32)
    t = np.arange(S).reshape(TT, P)
    ends = np.arange(CMP_T) * CMP_STRIDE + CMP_LEN - 1
    dist = (t[:, :, None] - ends).astype(np.float32)
    bias = np.where(dist[:, :, None, :] >= 0, -slopes[:, None] * dist[:, :, None, :], NEG)
    put("cmp_bias", bias.transpose(1, 0, 2, 3))
    put("cmp_ok", (dist >= 0).transpose(1, 0, 2))
    far = (P + r[:, None] - r[None, :]).astype(np.float32)
    own = (r[:, None] - r[None, :]).astype(np.float32)
    alibi = np.zeros((P, H_HEADS, S), np.float32)
    for h in range(H_HEADS):
        alibi[:, h, 0:P] = -slopes[h] * far
        alibi[:, h, P:S] = np.where(own >= 0, -slopes[h] * own, NEG)
    return c, alibi.reshape(P, H_HEADS * S)


class Queue:

    def __init__(self, engine, sem):
        self.engine, self.sem, self.count, self.seen = engine, sem, 0, {}

    def wait(self, tickets):
        for t in tickets:
            if t is None:
                continue
            sem, value = t
            if self.seen.get(id(sem), 0) < value:
                self.seen[id(sem)] = value
                self.engine.wait_ge(sem, value)

    def do(self, emit, after=(), signal=True):
        self.wait(after)
        ins = emit(self.engine)
        if not signal:
            return None
        self.count += 1
        ins.then_inc(self.sem, 1)
        return (self.sem, self.count)

    def last(self):
        return (self.sem, self.count) if self.count else None


class Ring:

    def __init__(self, slots):
        self.slots, self.free = slots, [(n, []) for n in range(len(slots))]

    def take(self):
        n, after = self.free.pop(0)
        return n, self.slots[n], after

    def give(self, n, tickets):
        assert n not in [m for m, _ in self.free]
        self.free.append((n, list(tickets)))


class Split:

    def __init__(self, hi, lo, width):
        self.hi, self.lo, self.width, self.hi_t, self.lo_t = hi, lo, width, {}, {}

    def part(self, which, k, a=0, b=None):
        b = self.width if b is None else b
        return (self.hi if which == "hi" else self.lo)[:, k * self.width + a:k * self.width + b]


def build_program(nc, d):
    ctx = ExitStack()
    with ctx:
        def sb(name, shape, dt=F32):
            return ctx.enter_context(nc.sbuf_tensor(name, shape, dt))

        def sem(name):
            return ctx.enter_context(nc.semaphore(name))

        params_sb = sb("params_sb", [P, NPARAMS])
        consts_sb = sb("consts_sb", [P, NCONSTS])
        xT = sb("xT", [P, KD * S])
        sq = sb("sq", [P, KD * S])
        h_hi, h_lo = sb("h_hi", [P, KD * S], F32R), sb("h_lo", [P, KD * S], F32R)
        GU_SLOTS = 6
        g_hi, g_lo = sb("g_hi", [P, GU_SLOTS * S], F32R), sb("g_lo", [P, GU_SLOTS * S], F32R)
        RAW_SLOTS, SPLIT_SLOTS = 4, 5
        raw_sb = sb("raw_sb", [P, RAW_SLOTS * RAW_MAX])
        w_hi = sb("w_hi", [P, SPLIT_SLOTS * UNIT_MAX], F32R)
        w_lo = sb("w_lo", [P, SPLIT_SLOTS * UNIT_MAX], F32R)
        rstd_sb = sb("rstd_sb", [P, S])
        mod_sb = sb("mod_sb", [P, DEPTH * 3 * KD])
        small = sb("small", [P, 64])
        ARENA = 16000
        arena = sb("arena", [P, ARENA])
        banks = Ring([ctx.enter_context(nc.psum_tensor(f"bank{i}", [P, 512], F32)) for i in range(8)])

        def par(name, at=0, n=1, rows=P):
            o = PARAMS[name][0] + at
            return params_sb[0:rows, o:o + n]

        def con(name, at=0, n=None, rows=P):
            o, size = CONSTS[name]
            n = size if n is None else n
            return consts_sb[0:rows, o + at:o + at + n]

        T, V, A, G, L = (Queue(engine, sem(n)) for engine, n in (
            (nc.tensor, "s_pe"), (nc.vector, "s_dve"), (nc.scalar, "s_act"), (nc.gpsimd, "s_pool"),
            (nc.sync, "s_sp")))
        loaded_table = [None]

        def table(name):
            if loaded_table[0] != name:
                A.engine.preload_act_table_set(name)
                loaded_table[0] = name
        LOG_EXP, SILU, SIGMOID, GELU = ("natural_log_exp_and_others", "silu_and_others", "sigmoid_and_others",
                                        "gelu_apprx_tanh_and_others")
        raw_sems = [sem(f"s_raw{i}") for i in range(RAW_SLOTS)]
        s_params, s_consts, s_pos, s_alibi, s_out = (sem(n) for n in (
            "s_params", "s_consts", "s_pos", "s_alibi", "s_out"))
        s_x = [sem(f"s_x{i}") for i in range(2)]
        ADA_SLOTS = 2
        s_c = sem("s_c")
        s_ada = [sem(f"s_ada{i}") for i in range(ADA_SLOTS)]
        s_cmp = [sem(f"s_cmp{i}") for i in range(DEPTH)]

        def load(out, src, s, value, after=()):
            L.wait(after)
            L.engine.dma_start(out, src).then_inc(s, 16)
            return (s, value)

        class Arena:
            def __init__(self):
                self.at = 0

            def get(self, n):
                a = arena[:, self.at:self.at + n]
                self.at += n
                assert self.at <= ARENA, self.at
                return a

        plan = []

        def plan_tiles(name, n, units, size):
            for i in range(n):
                plan.append((name, i, units, size))

        def plan_ffn(layer):
            for i in range(0, FF_TILES, 2):
                for j in range(2):
                    plan.append((f"w_up{layer}", i + j, 2, KD * P))
                if i >= 2:
                    plan.append((f"w_down{layer}", i // 2 - 1, 2, D))
            plan.append((f"w_down{layer}", FF_TILES // 2 - 1, 2, D))

        plan_tiles("w_dt", 1, 1, KD * P)
        GROUP_HEADS = SSD_HEADS // SSD_GROUPS
        GROUP_TILES = XS_TILES // SSD_GROUPS
        Z_PAIRS, OUT_PAIRS = XS_TILES // 2, XS_TILES // 2

        def core_schedule():
            z, out = GROUP_TILES // 2, 0
            for h in range(SSD_HEADS):
                g, i = divmod(h, GROUP_HEADS)
                if i in (1, 4) and z < Z_PAIRS:
                    yield h, "z", z
                    z += 1
                if i in ((), (5, 7), (5,), (5,))[g]:
                    yield h, "out", out
                    out += 1

        plan_tiles("w_ssd_in", (CONV_TILES + GROUP_TILES) // 2, 2, KD * P)
        OUT_AFTER = sum(what == "out" for _, what, _ in core_schedule())
        for _, what, n in core_schedule():
            plan.append(("w_ssd_in", CONV_TILES // 2 + n, 2, KD * P) if what == "z"
                        else ("w_ssd_out", n, 2, D))
        for n in range(OUT_AFTER, OUT_PAIRS):
            plan.append(("w_ssd_out", n, 2, D))
        plan_ffn(0)
        plan_tiles("w_attn_in", 2 * KD // 2, 2, KD * P)
        plan_tiles("w_attn_v", D // S, 2, KD * P)
        plan_tiles("w_attn_out", KD // 2, 2, KD * P)
        plan_ffn(1)
        for n in range(DEPTH):
            plan_tiles(f"w_kv{n}", 2, 2, KD * P)
            plan_tiles(f"w_vsg{n}", 1, 2, KD // 2 * VSG)
            plan_tiles(f"w_vm{n}", 2, 2, KD * P)
            plan_tiles(f"w_qz{n}", 10, 2, KD * P)
            plan_tiles(f"w_out{n}", KD // 2, 2, KD * P)

        class Stream:
            def __init__(self):
                self.loaded = self.used_chunk = 0
                self.raw_free = [[] for _ in range(RAW_SLOTS)]
                self.raw_t = {}
                self.units = []
                for i, (_, _, units, _) in enumerate(plan):
                    self.units += [(i, u) for u in range(units)]
                self.prepared = self.used = 0
                self.split_free = [[] for _ in range(SPLIT_SLOTS)]
                self.split_t = {}
                self.rest = []

            def load_ahead(self, upto=len(plan)):
                while self.loaded < upto and self.raw_free[self.loaded % RAW_SLOTS] is not None:
                    i = self.loaded
                    name, n, units, size = plan[i]
                    slot = i % RAW_SLOTS
                    self.raw_t[i] = load(raw_sb[:, slot * RAW_MAX:slot * RAW_MAX + units * size], d[name][n],
                                         raw_sems[slot], 16 * (i // RAW_SLOTS + 1), self.raw_free[slot])
                    self.raw_free[slot] = None
                    self.loaded += 1

            def prepare(self, upto):
                while self.prepared < min(upto, len(self.units)):
                    u = self.prepared
                    chunk, part = self.units[u]
                    if chunk not in self.raw_t or self.split_free[u % SPLIT_SLOTS] is None:
                        return
                    _, _, units, size = plan[chunk]
                    slot = u % SPLIT_SLOTS
                    raw_at = (chunk % RAW_SLOTS) * RAW_MAX + part * size
                    raw = raw_sb[:, raw_at:raw_at + size]
                    hi = w_hi[:, slot * UNIT_MAX:slot * UNIT_MAX + size]
                    lo = w_lo[:, slot * UNIT_MAX:slot * UNIT_MAX + size]
                    free = self.split_free[slot]
                    t_hi = A.do(lambda e: e.activation(hi, raw, ACT.Copy), [self.raw_t[chunk]] + free)
                    self.split_free[slot] = None
                    self.rest.append((u, chunk, raw, hi, lo, t_hi, free, part == units - 1))
                    self.prepared += 1

            def low_parts(self):
                for u, chunk, raw, hi, lo, t_hi, free, chunk_done in self.rest:
                    t_lo = V.do(lambda e: e.tensor_tensor(lo, raw, hi.bitcast(F32), ALU.subtract),
                                [self.raw_t[chunk], t_hi] + free)
                    self.split_t[u] = (t_hi, t_lo, hi, lo)
                    if chunk_done:
                        self.raw_free[chunk % RAW_SLOTS] = [t_lo]
                self.rest = []
                self.load_ahead()

            def unit(self, name):
                u = self.used
                assert plan[self.units[u][0]][0] == name, (name, plan[self.units[u][0]])
                self.prepare(u + SPLIT_SLOTS - 1)
                if u not in self.split_t:
                    self.low_parts()
                self.used += 1
                return u, self.split_t[u]

            def done(self, u, ticket):
                self.low_parts()
                self.split_free[u % SPLIT_SLOTS] = [ticket]
                self.prepare(self.used + SPLIT_SLOTS - 1)

        W = Stream()

        def mm(out, lhsT, rhs, start, stop, after=(), signal=False):
            return T.do(lambda e: e.matmul(out, lhsT, rhs, start=start, stop=stop, skip_group_check=True),
                        after, signal)

        delayed = []

        def later(n, fn):
            delayed.append([n, fn])

        def tick():
            W.low_parts()
            ready = [x for x in delayed if x[0] <= 0]
            for x in delayed:
                x[0] -= 1
            delayed[:] = [x for x in delayed if x not in ready]
            for _, fn in ready:
                fn()

        def flush():
            while delayed:
                tick()

        def project(name, tiles, acts, epilogue, together=1):
            tiles = list(tiles)
            while tiles:
                block, tiles = tiles[:together], tiles[together:]
                together = 1
                taken = [banks.take() for _ in block]
                units = [W.unit(name) for _ in block]
                done = []
                for k in range(KD):
                    for (n, bank, free), (u, (t_hi, t_lo, hi, lo)) in zip(taken, units):
                        out = bank[:, 0:S]
                        wh, wl = hi[:, k * P:(k + 1) * P], lo[:, k * P:(k + 1) * P]
                        mm(out, wh, acts.part("hi", k), k == 0, False,
                           [t_hi, acts.hi_t.get(k)] + (free if k == 0 else []))
                        mm(out, wh, acts.part("lo", k), False, False, [acts.lo_t.get(k)])
                        t = mm(out, wl, acts.part("hi", k), False, k == KD - 1, [t_lo], signal=k == KD - 1)
                        if k == KD - 1:
                            done.append(t)
                for m, (n, bank, _), (u, _), t in zip(block, taken, units, done):
                    W.done(u, t)
                    banks.give(n, epilogue(m, bank[:, 0:S], t))
                    tick()

        class OuterProjection:

            def __init__(self, name):
                self.name, self.first, self.banks = name, True, None

            def product(self, m, unit, operand, last):
                _, (t_hi, t_lo, hi, lo) = unit
                a_hi, a_lo, t_a_hi, t_a_lo = operand
                _, bank, free = self.banks[m // 2]
                out = bank[:, (m % 2) * S:(m % 2 + 1) * S]
                wh, wl = hi[:, m * P:(m + 1) * P], lo[:, m * P:(m + 1) * P]
                mm(out, wh, a_hi, self.first and m % 2 == 0, False, [t_hi, t_a_hi] + (free if self.first else []))
                mm(out, wh, a_lo, False, False, [t_a_lo])
                return mm(out, wl, a_hi, False, last, [t_lo], signal=m % 2 == 1)

            def step(self, operand):
                if self.first:
                    self.banks = [banks.take() for _ in range(KD // 2)]
                unit = W.unit(self.name)
                for m in range(KD):
                    t = self.product(m, unit, operand, False)
                W.done(unit[0], t)
                self.first = False
                return t

            def finish(self, operands, epilogue):
                units = [W.unit(self.name) for _ in operands]
                for m in range(KD):
                    for unit, operand in zip(units, operands):
                        t = self.product(m, unit, operand, operand is operands[-1])
                    if m % 2:
                        n, bank, _ = self.banks[m // 2]
                        banks.give(n, epilogue(m - 1, bank[:, 0:S], t) + epilogue(m, bank[:, S:2 * S], t))
                for unit in units:
                    W.done(unit[0], t)
                return t

        def project_rows(name, width, acts, epilogue):
            taken = [banks.take() for _ in range(TT)]
            half = KD // 2
            for part in range(2):
                u, (t_hi, t_lo, hi, lo) = W.unit(name)
                for tt in range(TT):
                    n, bank, free = taken[tt]
                    out = bank[:, 0:width]
                    for k in range(half):
                        kk = part * half + k
                        wh, wl = hi[:, k * width:(k + 1) * width], lo[:, k * width:(k + 1) * width]
                        ah, al = (acts.part(w, kk, tt * P, (tt + 1) * P) for w in ("hi", "lo"))
                        mm(out, ah, wh, kk == 0, False,
                           [t_hi, acts.hi_t.get(kk)] + (free if kk == 0 else []))
                        mm(out, ah, wl, False, False, [t_lo])
                        t = mm(out, al, wh, False, kk == KD - 1, [acts.lo_t.get(kk)], signal=k == half - 1)
                    if part == 1:
                        taken[tt] = (n, bank, t)
                W.done(u, t)
            for tt, (n, bank, t) in enumerate(taken):
                banks.give(n, epilogue(tt, bank, t))
            tick()

        def split_tile(dst, k, full, t_full, free=()):
            hi, lo = dst.part("hi", k), dst.part("lo", k)
            t = A.do(lambda e: e.activation(hi, full, ACT.Copy), [t_full] + list(free))
            dst.hi_t[k] = t
            dst.lo_t[k] = V.do(lambda e: e.tensor_tensor(lo, full, hi.bitcast(F32), ALU.subtract),
                                  [t, t_full] + list(free))
            return [dst.hi_t[k], dst.lo_t[k]]

        H = Split(h_hi, h_lo, S)
        gu_ring = Ring(list(range(GU_SLOTS)))

        def tile(buf, k, a=0, b=S):
            return buf[:, k * S + a:k * S + b]

        half = KD * S // 2
        t_x = [load(xT[:, i * half:(i + 1) * half], d["x"][:, i * half:(i + 1) * half], s_x[i], 16)
               for i in range(2)]
        W.load_ahead(1)
        t_params = load(params_sb[:, :], d["params"], s_params, 16)
        t_consts = load(consts_sb[:, :], d["consts"], s_consts, 16)
        W.load_ahead()

        eps_col = small[:, 0:1]
        t_eps = V.do(lambda e: e.memset(eps_col, EPS))
        ones = sb("ones", [P, P])[:, :]
        t_ones = V.do(lambda e: e.memset(ones, 1.0))
        half_pi = math.pi / 2

        class SquareSums:

            def __init__(self, squares, takers):
                self.squares, self.takers, self.left = squares, takers, []

            def add(self, m, t):
                who = self.takers[m]
                total = next((x for x in self.left if who and x[0] is who), None)
                if total:
                    self.left.remove(total)
                    _, at, t_at = total
                    out = tile(self.squares, at)
                    t = who.do(lambda e: e.tensor_tensor(out, out, tile(self.squares, m), ALU.add), [t, t_at])
                    m = at
                self.left.append((who, m, t))

            def finish(self):
                n, bank, free = banks.take()
                for _, at, t_at in self.left:
                    t = mm(bank[:, 0:S], ones, tile(self.squares, at), (_, at, t_at) == self.left[0],
                           (_, at, t_at) == self.left[-1], [t_at, t_ones] + free, signal=True)
                return n, bank[:, 0:S], t

        STEADY = [G] * (KD - 1) + [None]
        BURST = [G, V, G, V, G, V, V, None]

        def rstd_of(bank, t_bank, count, after, out=None):
            out = rstd_sb[:, :] if out is None else out
            table(LOG_EXP)
            t_ln = A.do(lambda e: e.activation(out, bank, ACT.Ln, bias=eps_col, scale=1.0 / count),
                        [t_bank, t_eps] + list(after))
            return A.do(lambda e: e.activation(out, out, ACT.Exp, scale=-0.5), [t_ln]), t_ln

        def norm_into_h(sums, gain, shift=None):
            n, bank, t_bank = sums.finish()
            t_rstd, t_free = rstd_of(bank, t_bank, D, [V.last()])
            banks.give(n, [t_free])

            def normalise(k):
                return V.do(lambda e: e.scalar_tensor_tensor(tile(sq, k), tile(xT, k), gain(k), rstd_sb[:, :],
                                                             ALU.mult, ALU.mult), [t_rstd, t_params, T.last()])
            t_next = normalise(0)
            for k in range(KD):
                t, full = t_next, tile(sq, k)
                hi, lo = H.part("hi", k), H.part("lo", k)
                bias = 0.0 if shift is None else shift(k)
                H.hi_t[k] = A.do(lambda e: e.activation(hi, full, ACT.Identity, bias=bias), [t])
                if k + 1 < KD:
                    t_next = normalise(k + 1)
                H.lo_t[k] = V.do(lambda e: e.scalar_tensor_tensor(lo, full, bias, hi.bitcast(F32),
                                                                  ALU.add, ALU.subtract), [t, H.hi_t[k]])

        def residual_epilogue(sums):
            def epilogue(m, bank, t):
                t_add = V.do(lambda e: e.tensor_tensor(tile(xT, m), bank, tile(xT, m), ALU.add), [t])
                sums.add(m, A.do(lambda e: e.activation(tile(sq, m), tile(xT, m), ACT.Square), [t_add]))
                return [t_add]
            return epilogue

        sums = SquareSums(sq, BURST)
        for k in range(KD):
            sums.add(k, A.do(lambda e: e.activation(tile(sq, k), tile(xT, k), ACT.Square), [t_x[k * 2 // KD]]))
        W.prepare(1)
        norm_into_h(sums, lambda k: par("mix_g", k))

        ar = Arena()
        z_sb = ar.get(XS_TILES * S)
        xs_sb = ar.get(XS_TILES * S)
        b_sb = ar.get(SSD_GROUPS * S)
        c_sb = ar.get(SSD_GROUPS * S)
        acc_ring = Ring([ar.get(S) for _ in range(4)])
        cb_ring = Ring([ar.get(3 * P) for _ in range(2)])
        ms_sb = ar.get(S)
        xs_tok_ring = Ring([ar.get(TT * GROUP_TILES * P) for _ in range(2)])
        tok = ar.get(5 * SSD_HEADS)
        dt_w = z_sb[:, 0:5 * P + 6 * S]
        hT = SSD_HEADS
        stack = dt_w[0:hT, 0:5 * P]
        dts, e_ab, u_ab, w_ab, acs = (dt_w[0:hT, 5 * P + i * S:5 * P + (i + 1) * S] for i in range(5))
        dA = dt_w[0:hT, 5 * P + 5 * S:5 * P + 6 * S]
        state = {}

        def dt_epilogue(_, bank, t):
            step = lambda fn, after=(): V.do(fn, [V.last()] + list(after))
            t_v = step(lambda e: e.tensor_scalar(dts, bank[0:hT, 0:S], par("dt_bias", rows=hT), None, ALU.add), [t])
            step(lambda e: e.tensor_scalar(w_ab, dts, -1.0, None, ALU.mult))
            step(lambda e: e.tensor_tensor(w_ab, dts, w_ab, ALU.max))
            table(LOG_EXP)
            t_e = A.do(lambda e: e.activation(e_ab, w_ab, ACT.Exp, scale=-1.0), [V.last()])
            step(lambda e: e.tensor_scalar(u_ab, e_ab, 1.0, None, ALU.add), [t_e])
            t_ln = A.do(lambda e: e.activation(acs, u_ab, ACT.Ln), [V.last()])
            t_a = A.do(lambda e: e.activation(small[0:hT, 1:2], par("a_log", rows=hT), ACT.Exp), [t_params])
            step(lambda e: e.scalar_tensor_tensor(e_ab, u_ab, -1.0, e_ab, ALU.add, ALU.subtract))
            step(lambda e: e.reciprocal(u_ab, u_ab), [t_ln])
            step(lambda e: e.tensor_tensor(e_ab, e_ab, u_ab, ALU.mult))
            step(lambda e: e.tensor_tensor(acs, acs, e_ab, ALU.subtract), [t_ln])
            step(lambda e: e.scalar_tensor_tensor(dts, dts, 0.0, acs, ALU.max, ALU.add))
            step(lambda e: e.tensor_scalar(dA, dts, small[0:hT, 1:2], -1.0, ALU.mult, ALU.mult), [t_a])
            step(lambda e: e.memset(w_ab, 1.0))
            for tt in range(TT):
                step(lambda e, tt=tt: e.tensor_tensor_scan(acs[:, tt * P:(tt + 1) * P], w_ab[:, tt * P:(tt + 1) * P],
                                                           dA[:, tt * P:(tt + 1) * P], 0.0, ALU.mult, ALU.add))
            step(lambda e: e.tensor_copy(stack[:, 0:S], dts))
            step(lambda e: e.tensor_scalar(stack[:, S:2 * S], acs, -1.0, None, ALU.mult))
            t_stack = step(lambda e: e.tensor_scalar(stack[:, 2 * S:2 * S + P], acs[:, 0:P], -1.0, acs[:, P - 1:P],
                                                     ALU.mult, ALU.add))
            state["acs_hi"] = A.do(lambda e: e.activation(acs_hi[:, :], acs, ACT.Copy), [t_stack])
            state["acs"] = V.do(lambda e: e.tensor_tensor(acs_lo[:, :], acs, acs_hi[:, :].bitcast(F32), ALU.subtract),
                                [state["acs_hi"]])

            def turn():
                n, b, free = banks.take()
                for i in range(5):
                    t = T.do(lambda e, i=i: e.transpose(b[:, i * hT:(i + 1) * hT], stack[:, i * P:(i + 1) * P],
                                                        con("ident", 0, hT, hT)),
                             [t_stack, t_consts] + free, signal=True)
                state["tok"] = V.do(lambda e: e.tensor_copy(tok, b[:, 0:5 * hT]), [t])
                banks.give(n, [state["tok"]])
            later(3, turn)
            return [t_v]

        acs_hi = sb("acs_hi", [hT, S], F32R)
        acs_lo = sb("acs_lo", [hT, S], F32R)
        sel = sb("sel", [hT, hT * 2], F32R)
        mask_r = sb("mask_r", [P, P], F32R)
        ident_r = sb("ident_r", [P, P], F32R)
        t_sel = A.do(lambda e: e.activation(sel[:, 0:hT], con("ident", 0, hT, hT), ACT.Copy), [t_consts])
        t_mask = A.do(lambda e: e.activation(mask_r[:, :], con("causal_far"), ACT.Copy), [t_consts])
        t_ident_r = A.do(lambda e: e.activation(ident_r[:, :], con("ident"), ACT.Copy), [t_consts])

        def conv_taps(bank, t, taps, weight, bias):
            n, acc, free = acc_ring.take()
            t_acc = A.do(lambda e: e.activation(acc, bank[:, 0:S], ACT.Identity, bias=bias,
                                                scale=weight(taps - 1)), [t, t_params] + free)
            for back in range(1, taps):
                t_acc = V.do(lambda e, back=back: e.scalar_tensor_tensor(
                    acc[:, back:S], bank[:, 0:S - back], weight(taps - 1 - back), acc[:, back:S],
                    ALU.mult, ALU.add), [t_acc])
            return n, acc, t_acc

        conv_out = ([b_sb[:, g * S:(g + 1) * S] for g in range(SSD_GROUPS)]
                    + [c_sb[:, g * S:(g + 1) * S] for g in range(SSD_GROUPS)]
                    + [tile(xs_sb, k) for k in range(XS_TILES)])
        conv_col = ([XS_TILES + g for g in range(2 * SSD_GROUPS)] + list(range(XS_TILES)))
        conv_t = {}

        def ssd_in_epilogue(m, bank, t):
            if m < CONV_TILES:
                col = conv_col[m]
                n, acc, t_acc = conv_taps(bank, t, SSD_TAPS, lambda k: par("ssd_conv", k * CONV_TILES + col),
                                          par("ssd_conv", SSD_TAPS * CONV_TILES + col))

                def silu_it():
                    table(SILU)
                    conv_t[m] = A.do(lambda e: e.activation(conv_out[m], acc, ACT.Silu), [t_acc])
                    acc_ring.give(n, [conv_t[m]])
                later(1, silu_it)
                return [t_acc]
            k = m - CONV_TILES
            z_t[k] = A.do(lambda e: e.activation(tile(z_sb, k), bank[:, 0:S], ACT.Copy),
                          [t, state["tok"], state["acs"]])
            return [z_t[k]]
        z_t = {}
        GT = GROUP_TILES

        project("w_dt", [0], H, dt_epilogue)
        project("w_ssd_in", range(CONV_TILES + GT), H, ssd_in_epilogue, together=3)
        flush()

        AHEAD = 3
        m_ring = Ring([sq[:, i * 3 * P:(i + 1) * 3 * P] for i in range(AHEAD + 1)])
        dec_ring = Ring([ar.get(3 * P) for _ in range(3)])
        ssd_out = OuterProjection("w_ssd_out")
        in_group, ybank, silu_t, group_sums = {}, {}, {}, {}

        def open_group(g):
            n, bank, free = banks.take()
            bg, cg = b_sb[:, g * S:(g + 1) * S], c_sb[:, g * S:(g + 1) * S]
            mm(bank[:, 0:S], bg[:, 0:P], cg, True, True, [conv_t[CONV_TILES - 1]] + free)
            t = mm(bank[:, S:S + P], bg[:, P:S], cg[:, P:S], False, True, signal=True)
            cn, cb, cfree = cb_ring.take()
            t_cb = V.do(lambda e: e.tensor_copy(cb, bank[:, 0:3 * P]), [t] + cfree)
            banks.give(n, [t_cb])
            xn, xt, xfree = xs_tok_ring.take()
            for tt in range(TT):
                n, bank, free = banks.take()
                for j in range(GT):
                    t = T.do(lambda e: e.transpose(bank[:, j * P:(j + 1) * P],
                                                   tile(xs_sb, g * GT + j, tt * P, (tt + 1) * P), con("ident")),
                             free, signal=True)
                t_xt = A.do(lambda e: e.activation(xt[:, tt * GT * P:(tt + 1) * GT * P], bank[:, :], ACT.Copy),
                            [t] + xfree)
                banks.give(n, [t_xt])
            in_group[g] = (cn, cb, t_cb, xn, xt, t_xt)

        def decays(h):
            n, b, free = banks.take()
            oneh = sel[:, h:h + 1].to_broadcast([hT, P])
            mm(b[:, 0:S], oneh, acs_hi[:, :], True, False, free + [t_sel, state["acs_hi"]])
            mm(b[:, 0:S], oneh, acs_lo[:, :], False, False, [state["acs"]])
            mm(b[:, S:S + P], oneh, acs_hi[:, P:S], False, False)
            mm(b[:, S:S + P], oneh, acs_lo[:, P:S], False, False)
            mm(b[:, 0:P], ident_r[:, :], mask_r[:, :], False, False, [t_mask, t_ident_r])
            t = mm(b[:, S:S + P], ident_r[:, :], mask_r[:, :], False, True, signal=True)
            dn, dec, dfree = dec_ring.take()
            table(LOG_EXP)
            bias = [tok[:, i * hT + h:i * hT + h + 1] for i in (2, 4, 3)]
            for i in range(3):
                te = A.do(lambda e: e.activation(dec[:, i * P:(i + 1) * P], b[:, i * P:(i + 1) * P],
                                                 ACT.Exp, bias=bias[i]), [t, state["tok"]] + dfree)
            banks.give(n, [te])
            return dn, dec, te

        def times_cb(h, made):
            dn, dec, te = made
            _, cb, t_cb, _, _, _ = in_group[h // GROUP_HEADS]
            mn, mt, mfree = m_ring.take()
            V.do(lambda e: e.scalar_tensor_tensor(mt[:, 0:S], dec[:, 0:S], tok[:, h:h + 1], cb[:, 0:S],
                                                  ALU.mult, ALU.mult), [te, t_cb] + mfree)
            tm = V.do(lambda e: e.scalar_tensor_tensor(mt[:, S:S + P], dec[:, S:S + P], tok[:, hT + h:hT + h + 1],
                                                       cb[:, S:S + P], ALU.mult, ALU.mult))
            dec_ring.give(dn, [tm])
            return mn, mt, tm

        def head_y(h, made):
            g, i = divmod(h, GROUP_HEADS)
            cn, _, _, xn, xt, t_xt = in_group[g]
            mn, mt, tm = made
            half, k = h % 2, h // 2
            if half == 0:
                ybank[k] = banks.take()
            n, b, free = ybank[k]
            rows = slice(half * SSD_P, (half + 1) * SSD_P)
            c0 = i * SSD_P
            mm(b[rows, 0:S], xt[:, c0:c0 + SSD_P], mt[:, 0:S], True, False, [tm, t_xt] + free)
            t = mm(b[rows, P:S], xt[:, GT * P + c0:GT * P + c0 + SSD_P], mt[:, S:S + P], False, True, signal=True)
            m_ring.give(mn, [t])
            if half == 1:
                t_y = V.do(lambda e: e.scalar_tensor_tensor(tile(xs_sb, k), tile(xs_sb, k), par("ssd_d", k),
                                                            b[:, 0:S], ALU.mult, ALU.add), [t])
                banks.give(n, [t_y])
                t_z = V.do(lambda e: e.tensor_tensor(tile(z_sb, k), tile(z_sb, k), tile(xs_sb, k), ALU.mult),
                           [t_y, silu_t[g]])

                def square():
                    t_sq = A.do(lambda e: e.activation(tile(xs_sb, k), tile(z_sb, k), ACT.Square), [t_z])
                    if k % GT == 0:
                        group_sums[g] = SquareSums(xs_sb[:, g * GT * S:(g + 1) * GT * S], [G] * GT)
                    group_sums[g].add(k % GT, t_sq)
                squares.append(square)
            if i == GROUP_HEADS - 1:
                cb_ring.give(cn, [tm])
                xs_tok_ring.give(xn, [t])

        def silu_group(g):
            table(SILU)
            zg = z_sb[:, g * GT * S:(g + 1) * GT * S]
            silu_t[g] = A.do(lambda e: e.activation(zg, zg, ACT.Silu), [z_t[(g + 1) * GT - 1]])

        normed = {}

        def norm_group(g):
            n, b, t = group_sums[g].finish()
            t_ms, t_free = rstd_of(b, t, GT * P, [V.last()], ms_sb)
            banks.give(n, [t_free])
            for k in range(g * GT, (g + 1) * GT):
                normed[k] = V.do(lambda e: e.scalar_tensor_tensor(tile(z_sb, k), tile(z_sb, k), par("ssd_norm_g", k),
                                                                  ms_sb, ALU.mult, ALU.mult), [t_ms])

        def split_for_out(k):
            slot, _, free = gu_ring.take()
            part = Split(g_hi, g_lo, S)
            split_tile(part, slot, tile(z_sb, k), normed[k], free)
            return slot, (part.part("hi", slot), part.part("lo", slot), part.hi_t[slot], part.lo_t[slot])

        split_out = {}

        def out_splits(n):
            split_out[n] = [split_for_out(k) for k in (2 * n, 2 * n + 1)]

        def out_steps(n):
            for slot, operand in split_out.pop(n):
                gu_ring.give(slot, [ssd_out.step(operand)])

        schedule = {}
        for h, what, n in core_schedule():
            schedule.setdefault(h, []).append((what, n))
        open_group(0)
        silu_group(0)
        squares = []
        made = {h: decays(h) for h in range(AHEAD)}
        for h in range(AHEAD - 1):
            made[h] = times_cb(h, made[h])
        for h in range(SSD_HEADS):
            g, i = divmod(h, GROUP_HEADS)
            if i == GROUP_HEADS - AHEAD - 1 and g + 1 < SSD_GROUPS:
                open_group(g + 1)
            ahead = h + AHEAD - 1
            if ahead < SSD_HEADS:
                made[ahead] = times_cb(ahead, made[ahead])
            if h + AHEAD < SSD_HEADS:
                made[h + AHEAD] = decays(h + AHEAD)
            while squares:
                squares.pop()()
            if i == 6 and g + 1 < SSD_GROUPS:
                silu_group(g + 1)
            if g and i == 2:
                norm_group(g - 1)
            for what, n in schedule.get(h + 1, []):
                if what == "out":
                    out_splits(n)
            for what, n in schedule.get(h, []):
                if what == "z":
                    m = CONV_TILES + 2 * n
                    project("w_ssd_in", [m, m + 1], H, ssd_in_epilogue)
                else:
                    out_steps(n)
            head_y(h, made.pop(h))
        squares.pop()()
        rest = list(range(OUT_AFTER, OUT_PAIRS))
        old, new = rest[:-GT // 2], rest[-GT // 2:]
        out_splits(old[0])
        for n in old:
            if n + 1 in old:
                out_splits(n + 1)
            out_steps(n)
            if n == old[0]:
                norm_group(SSD_GROUPS - 1)
                out_splits(new[0])
        out_splits(new[1])
        out_steps(new[0])
        sums = SquareSums(sq, BURST)
        last = split_out.pop(new[1])
        t = ssd_out.finish([operand for _, operand in last], residual_epilogue(sums))
        for slot, _ in last:
            gu_ring.give(slot, [t])
        flush()

        ADA_FROM = 4

        class Ada:

            def __init__(self, layer, ar):
                self.layer, self.i = layer, 0
                self.c = ar.get(D)
                self.raw = [ar.get(ADA_TILES * D) for _ in range(ADA_SLOTS)]
                self.sums = ar.get(3 * KD)
                self.raw_t = {}
                idle = [T.last(), V.last(), A.last()]
                t_c = load(self.c, d["c"], s_c, 16 * (layer + 1), idle)
                for i in range(ADA_SLOTS):
                    self.load(i, idle)
                table(SILU)
                self.t_cs = A.do(lambda e: e.activation(self.c, self.c, ACT.Silu), [t_c])

            def load(self, i, after):
                slot = i % ADA_SLOTS
                uses = (self.layer * ADA_CHUNKS + i) // ADA_SLOTS + 1
                self.raw_t[i] = load(self.raw[slot], d[f"w_ada{self.layer}"][i], s_ada[slot], 16 * uses, after)

            def step(self):
                chunk, j = divmod(self.i, ADA_TILES)
                w = self.raw[chunk % ADA_SLOTS][:, j * D:(j + 1) * D]
                self.t = V.do(lambda e: e.tensor_tensor_reduce(w, w, self.c, 1.0, 0.0, ALU.mult, ALU.add,
                                                               self.sums[:, self.i:self.i + 1]),
                              [self.raw_t[chunk], self.t_cs])
                if j == ADA_TILES - 1 and chunk + ADA_SLOTS < ADA_CHUNKS:
                    self.load(chunk + ADA_SLOTS, [self.t])
                self.i += 1

            def finish(self):
                assert self.i == 3 * KD
                lay = self.layer
                mod = mod_sb[:, lay * 3 * KD:(lay + 1) * 3 * KD]
                t = V.do(lambda e: e.tensor_tensor(mod, self.sums, par("b_ada", lay * 3 * KD, 3 * KD), ALU.add),
                         [self.t])
                t = V.do(lambda e: e.scalar_tensor_tensor(mod[:, KD:2 * KD], mod[:, KD:2 * KD], 1.0,
                                                          par("g_pre", lay * KD, KD), ALU.add, ALU.mult), [t])
                V.do(lambda e: e.tensor_tensor(mod[:, 2 * KD:3 * KD], mod[:, 2 * KD:3 * KD],
                                               par("g_post", lay * KD, KD), ALU.mult), [t])

        def ffn(layer, sums):
            norm_into_h(sums, lambda k: par("ffn_g", layer * KD + k))
            base = layer * (FFN_TAPS + 1) * 2 * FF_TILES
            ar = Arena()
            acc_ring = Ring([ar.get(S) for _ in range(5)])
            gate_ring = Ring([ar.get(S) for _ in range(2)])
            prod_ring = Ring([ar.get(S) for _ in range(3)])
            hold = {}
            ada = Ada(layer, ar)

            def epilogue(m, bank, t):
                i, is_up = m // 2, m % 2
                col = base + (FF_TILES if is_up else 0) + i
                n, acc, free = acc_ring.take()
                t_acc = A.do(lambda e: e.activation(acc, bank[:, 0:S], ACT.Identity,
                                                    bias=par("ffn_conv", col + FFN_TAPS * 2 * FF_TILES),
                                                    scale=par("ffn_conv", col + (FFN_TAPS - 1) * 2 * FF_TILES)),
                             [t] + free)
                for back in range(1, FFN_TAPS):
                    t_acc = V.do(lambda e, back=back: e.scalar_tensor_tensor(
                        acc[:, back:S], bank[:, 0:S - back],
                        par("ffn_conv", col + (FFN_TAPS - 1 - back) * 2 * FF_TILES), acc[:, back:S],
                        ALU.mult, ALU.add), [t_acc])
                if not is_up:
                    def gate_it():
                        gn, gate, gfree = gate_ring.take()
                        table(SILU)
                        tg = A.do(lambda e: e.activation(gate, acc, ACT.Silu), [t_acc] + gfree)
                        acc_ring.give(n, [tg])
                        hold[i] = (gn, gate, tg)
                    later(1, gate_it)
                    return [t_acc]

                def multiply():
                    gn, gate, tg = hold[i]
                    pn, prod, pfree = prod_ring.take()
                    tp = V.do(lambda e: e.tensor_tensor(prod, gate, acc, ALU.mult), [tg, t_acc] + pfree)
                    acc_ring.give(n, [tp])
                    gate_ring.give(gn, [tp])

                    def split_it():
                        slot, _, sfree = gu_ring.take()
                        part = Split(g_hi, g_lo, S)
                        prod_ring.give(pn, split_tile(part, slot, prod, tp, sfree))
                        products[i] = (slot, (part.part("hi", slot), part.part("lo", slot),
                                              part.hi_t[slot], part.lo_t[slot]))
                    later(1, split_it)
                later(1, multiply)
                return [t_acc]

            products = {}
            down = OuterProjection(f"w_down{layer}")
            for i in range(FF_TILES):
                while ada.i * (FF_TILES - ADA_FROM) < 3 * KD * (i + 1 - ADA_FROM):
                    ada.step()
                if i % 2 == 0:
                    tiles = range(2 * i, 2 * i + 4)
                    project(f"w_up{layer}", tiles, H, epilogue, together=3 if i == 0 else 1)
                    if i == FF_TILES - 2:
                        flush()
                    if i >= 2:
                        for k in (i - 2, i - 1):
                            slot, operand = products.pop(k)
                            gu_ring.give(slot, [down.step(operand)])
            ada.finish()
            table(LOG_EXP)
            out_sums = SquareSums(sq, BURST)
            t = down.finish([operand for _, operand in products.values()], residual_epilogue(out_sums))
            for slot, _ in products.values():
                gu_ring.give(slot, [t])
            flush()
            return out_sums

        sums = ffn(0, sums)

        def attend(units, scratch, groups):
            e_ring = Ring([scratch.get(groups * 2 * S) for _ in range(5)])
            p_ring = Ring([scratch.get(2 * S) for _ in range(3)])
            n_ring = Ring([scratch.get(4 * groups) for _ in range(5)])
            made = {}

            def scores(i):
                u = units[i]
                nk = u["nk"]
                table(LOG_EXP)
                en, eb, efree = e_ring.take()
                nn, columns, nfree = n_ring.take()
                sums = columns[:, 2 * groups:4 * groups]
                for g in range(groups):
                    n, bank, free = banks.take()
                    pair = u["scores"][2 * g:2 * g + 2]
                    for j, (q, k, _) in enumerate(pair):
                        t = mm(bank[:, j * S:j * S + nk], q, k, j == 0, True, u["after"] + free, signal=True)
                    for j, (_, _, bias) in enumerate(pair):
                        c = 2 * g + j
                        e_tile = eb[:, c * S:c * S + nk]
                        tv = V.do(lambda e: e.tensor_tensor_reduce(
                            e_tile, bank[:, j * S:j * S + nk], bias, -1.0, 3.0e38,
                            ALU.add, ALU.min, columns[:, c:c + 1]), [t] + efree + nfree + u["after"])
                        te = A.do(lambda e: e.activation(e_tile, e_tile, ACT.Exp, bias=columns[:, c:c + 1],
                                                         scale=-1.0, accum_out=sums[:, c:c + 1]), [tv])
                    banks.give(n, [tv])
                made[i] = [en, eb, nn, sums, te]

            def weigh(i):
                en, eb, nn, sums, te = made[i]
                t = V.do(lambda e: e.reciprocal(sums, sums), [te])
                t = units[i]["weigh"](eb, sums, t)
                n_ring.give(nn, [t])
                made[i] = [en, eb, t]

            def turn(i):
                nk = units[i]["nk"]
                en, eb, te = made[i]
                n, bank, free = banks.take()
                pn, pb, pfree = p_ring.take()
                kts = nk // P
                for j in range(2):
                    for kt in range(kts):
                        at = (j * kts + kt) * P
                        t = T.do(lambda e: e.transpose(bank[:, at:at + P], eb[:, j * S + kt * P:j * S + (kt + 1) * P],
                                                       con("ident")), [te] + free, signal=True)
                e_ring.give(en, [t])
                w = 2 * kts * P
                if groups == 1 or i % 2:
                    tc = A.do(lambda e: e.activation(pb[:, 0:w], bank[:, 0:w], ACT.Copy), [t] + pfree)
                else:
                    tc = V.do(lambda e: e.tensor_copy(pb[:, 0:w], bank[:, 0:w]), [t] + pfree)
                banks.give(n, [tc])
                made[i] = [pn, pb, tc]

            def values(i):
                u = units[i]
                kts = u["nk"] // P
                pn, pb, tc = made.pop(i)
                bank, after = u["bank"]()
                for j in range(2):
                    for kt in range(kts):
                        at = (j * kts + kt) * P
                        t = mm(u["out"](bank, j), u["values"][j][kt], pb[:, at:at + P], u["start"] and kt == 0,
                               kt == kts - 1, [tc] + after + u["after"], signal=kt == kts - 1)
                p_ring.give(pn, [t])
                u["then"](t)

            for i in range(len(units) + 4):
                if i < len(units):
                    scores(i)
                if 1 <= i < len(units) + 1:
                    weigh(i - 1)
                if 3 <= i < len(units) + 3:
                    turn(i - 3)
                if i >= 4:
                    values(i - 4)
                tick()
            flush()

        norm_into_h(sums, lambda k: par("mix_g", KD + k))
        ar = Arena()
        q_sb, k_sb = ar.get(KD * S), ar.get(KD * S)
        v_sb = ar.get(TT * D)
        cos_sb, sin_sb = ar.get(S), ar.get(S)
        pos_f, ang, kk_f = ar.get(S), ar.get(S), ar.get(S)
        pos_i = arena[:, ar.at:ar.at + S].bitcast(I32)
        ar.at += S
        sq_ring = Ring([ar.get(S) for _ in range(6)])
        rs_ring = Ring([ar.get(S) for _ in range(3)])
        t_pos = load(pos_i, d["positions"], s_pos, 16, [T.last(), V.last(), A.last()])
        chain = lambda fn, after=(): V.do(fn, [V.last()] + list(after))
        chain(lambda e: e.tensor_copy(pos_f, pos_i), [t_pos, T.last(), A.last()])
        chain(lambda e: e.tensor_scalar(ang, pos_f, con("inv_freq"), None, ALU.mult))
        chain(lambda e: e.tensor_scalar(kk_f, ang, 1.0 / (2 * math.pi), 12582912.0, ALU.mult, ALU.add))
        chain(lambda e: e.tensor_scalar(kk_f, kk_f, -12582912.0, None, ALU.add))
        for part in TWO_PI_PARTS:
            chain(lambda e, part=part: e.scalar_tensor_tensor(ang, kk_f, -part, ang, ALU.mult, ALU.add))
        chain(lambda e: e.tensor_scalar(ang, ang, 3.1415925, -3.1415925, ALU.min, ALU.max))
        table(SILU)
        t_sin = A.do(lambda e: e.activation(sin_sb, ang, ACT.Sin), [V.last()])
        chain(lambda e: e.tensor_scalar(kk_f, ang, -1.0, None, ALU.mult))
        chain(lambda e: e.tensor_tensor(kk_f, kk_f, ang, ALU.max))
        chain(lambda e: e.tensor_scalar(kk_f, kk_f, -1.0, half_pi, ALU.mult, ALU.add))
        t_cos = A.do(lambda e: e.activation(cos_sb, kk_f, ACT.Sin), [V.last()])
        qg = small[:, 2:3]
        chain(lambda e: e.tensor_scalar(qg, par("q_g"), 1.0 / math.sqrt(HD), None, ALU.mult), [t_params])
        for i in range(2):
            chain(lambda e, i=i: e.tensor_tensor_reduce(kk_f[:, 0:HD], par("lam", 2 * i * HD, HD),
                                                        par("lam", (2 * i + 1) * HD, HD), 1.0, 0.0, ALU.mult, ALU.add,
                                                        small[:, 4 + i:5 + i]), [t_cos])
        table(LOG_EXP)
        t_lam = A.do(lambda e: e.activation(small[:, 6:8], small[:, 4:6], ACT.Exp), [V.last()])
        lam = small[:, 8:9]
        chain(lambda e: e.tensor_tensor(lam, small[:, 6:7], small[:, 7:8], ALU.subtract), [t_lam])
        chain(lambda e: e.tensor_scalar(lam, lam, LAMBDA_INIT, None, ALU.add))
        sg = small[:, 3:4]
        t_small = chain(lambda e: e.tensor_scalar(sg, par("subln_g"), 1.0 - LAMBDA_INIT, None, ALU.mult))

        def qk_epilogue(m, bank, t):
            dst = tile(q_sb, m) if m < KD else tile(k_sb, m - KD)
            gain = qg if m < KD else par("k_g")
            t_raw = V.do(lambda e: e.tensor_copy(dst, bank[:, 0:S]), [t])
            sn, s2, sfree = sq_ring.take()
            t_sq = A.do(lambda e: e.activation(s2, dst, ACT.Square), [t_raw] + sfree)

            def head_sums():
                n, b, free = banks.take()
                ts = mm(b[:, 0:S], con("block_ones"), s2, True, True, [t_sq] + free, signal=True)
                rn, rs, rfree = rs_ring.take()
                t2, t1 = rstd_of(b[:, 0:S], ts, HD, rfree, rs)
                banks.give(n, [t1])
                t3 = V.do(lambda e: e.scalar_tensor_tensor(dst, dst, gain, rs, ALU.mult, ALU.mult), [t2, t_raw, t_small])
                rs_ring.give(rn, [t3])

                def rotate():
                    n, b, free = banks.take()
                    tr = mm(b[:, 0:S], con("rope_perm"), dst, True, True, [t3] + free, signal=True)
                    t4 = V.do(lambda e: e.tensor_tensor(s2, b[:, 0:S], sin_sb, ALU.mult), [tr, t_sin])
                    banks.give(n, [t4])
                    t5 = V.do(lambda e: e.tensor_tensor(dst, dst, cos_sb, ALU.mult), [t_cos, tr])
                    qk_t[m] = V.do(lambda e: e.tensor_tensor(dst, dst, s2, ALU.add), [t4, t5])
                    sq_ring.give(sn, [qk_t[m]])
                later(1, rotate)
            later(2, head_sums)
            return [t_raw]
        qk_t = {}
        project("w_attn_in", range(2 * KD), H, qk_epilogue, together=3)
        v_t = []
        for c in range(D // S):
            def v_epilogue(tt, bank, t, c=c):
                v_t.append(A.do(lambda e: e.activation(v_sb[:, tt * D + c * S:tt * D + (c + 1) * S], bank[:, 0:S],
                                                       ACT.Copy), [t]))
                return [v_t[-1]]
            project_rows("w_attn_v", S, H, v_epilogue)
        flush()

        ready = [qk_t[m] for m in range(2 * KD)] + v_t
        sc = Arena()
        sc.at = ar.at - 12 * S
        o_sq_ring = Ring([sc.get(S) for _ in range(2)])
        o_rs_ring = Ring([sc.get(S) for _ in range(2)])
        Y = Split(h_hi, h_lo, S)
        units = []

        def diff_unit(qb, heads):
            nk = (qb + 1) * P
            taken = {}

            def weigh(eb, rl, t):
                for j in range(2):
                    p0, p1 = (eb[:, (2 * c + j) * S:(2 * c + j) * S + nk] for c in range(2))
                    t1 = V.do(lambda e: e.tensor_scalar(p1, p1, rl[:, 2 + j:3 + j], lam, ALU.mult, ALU.mult), [t])
                    t2 = V.do(lambda e: e.scalar_tensor_tensor(p0, p0, rl[:, j:j + 1], p1, ALU.mult, ALU.subtract),
                              [t1])
                return t2

            def bank():
                taken["bank"] = banks.take()
                return taken["bank"][1:]

            def then(t):
                n, b, _ = taken["bank"]
                o, sums = b[:, 0:S], b[:, S:2 * S]
                sn, o_sq, sfree = o_sq_ring.take()
                t_sq = A.do(lambda e: e.activation(o_sq, o, ACT.Square), [t] + sfree)

                def norm():
                    t_sum = mm(sums, ones, o_sq, True, True, [t_sq], signal=True)
                    rn, rs, rfree = o_rs_ring.take()
                    t_rs, _ = rstd_of(sums, t_sum, 2 * HD, rfree, rs)
                    t_o = V.do(lambda e: e.scalar_tensor_tensor(o_sq, o, sg, rs, ALU.mult, ALU.mult), [t_rs])
                    banks.give(n, [t_o])
                    o_rs_ring.give(rn, [t_o])
                    view = lambda buf: buf[:, heads[0] * S:(heads[1] + 1) * S].rearrange(
                        "p (h c) -> p h c", h=2)[:, :, qb * P:(qb + 1) * P]
                    o3 = o_sq.rearrange("p (h c) -> p h c", h=2)
                    t_hi = A.do(lambda e: e.activation(view(h_hi), o3, ACT.Copy), [t_o])
                    t_lo = V.do(lambda e: e.tensor_tensor(view(h_lo), o3, view(h_hi).bitcast(F32), ALU.subtract),
                                [t_hi])
                    o_sq_ring.give(sn, [t_lo])
                    for h in heads:
                        Y.hi_t[h], Y.lo_t[h] = t_hi, t_lo
                later(1, norm)

            return dict(
                nk=nk, after=ready, weigh=weigh, bank=bank, then=then, start=True,
                scores=[(q_sb[c * HD:(c + 1) * HD, h * S + qb * P:h * S + (qb + 1) * P],
                         k_sb[c * HD:(c + 1) * HD, h * S:h * S + nk], con("chunk_mask", S - nk, nk))
                        for c in range(2) for h in heads],
                values=[[v_sb[:, kt * D + h * P:kt * D + (h + 1) * P] for kt in range(qb + 1)] for h in heads],
                out=lambda b, j: b[:, j * P:(j + 1) * P])

        for qb in range(TT):
            for pair in range(A_HEADS // 2):
                units.append(diff_unit(qb, (2 * pair, 2 * pair + 1)))
        attend(units, sc, 2)
        sums = SquareSums(sq, STEADY)
        project("w_attn_out", range(KD), Y, residual_epilogue(sums))
        flush()
        sums = ffn(1, sums)

        alibi = sb("alibi_sb", [P, H_HEADS * S])
        t_alibi = load(alibi[:, :], d["alibi"], s_alibi, 16)

        def hybrid(layer, sums):
            mod = mod_sb[:, layer * 3 * KD:(layer + 1) * 3 * KD]
            norm_into_h(sums, lambda k: mod[:, KD + k:KD + k + 1], lambda k: mod[:, k:k + 1])
            ar = Arena()
            qn_sb, qm_sb, km_sb = ar.get(4 * S), ar.get(4 * S), ar.get(4 * S)
            zs = ar.get(8 * S)
            kdup = {"s": ar.get(2 * S), "w": ar.get(2 * S)}
            vm = ar.get(TT * 512)
            vsw = ar.get(TT * VSG)
            kc_pair = ar.get(H_GROUPS * 2 * CMP_W)
            vc_pair = ar.get(H_HEADS * HD)
            gates = ar.get(TT * 24)
            pc = ar.get(TT * H_HEADS * CMP_W)
            pcT = ar.get(TT * H_HEADS * CMP_W)
            st = ar.get(TT * 2 * H_HEADS)
            sc = Arena()
            sc.at = ar.at
            slab = {"k": ar.get(3 * S), "v": ar.get(3 * S)}
            ck = ar.get(2 * CMP_PAIRS * HD)
            ck2 = ar.get(2 * HD)
            gel = ar.get(2 * 64)
            done = [T.last(), V.last(), A.last()]
            t_ck = load(ck, d[f"ck1_{layer}"], s_cmp[layer], 16, done)
            t_ck = load(ck2[0:HD, :], d[f"ck2_{layer}"], s_cmp[layer], 32)
            t_zero = {}
            for kind in "kv":
                t_zero[kind] = V.do(lambda e, b=slab[kind]: e.memset(b, 0.0), done)
            pe_dst = {kind: slab[kind][:, 2 * S:2 * S + CMP_LEN].rearrange("p (j two) -> p j two", two=2)[:, :, 0:1]
                      for kind in "kv"}
            pe_in = gel
            t_ck = load(pe_in[:, 0:2 * CMP_PAIRS], d[f"pe_{layer}"], s_cmp[layer], 48)
            t_pe = {}
            for i, kind in enumerate("kv"):
                t_pe[kind] = V.do(lambda e, kind=kind, i=i: e.tensor_copy(
                    pe_dst[kind], pe_in[:, i * CMP_PAIRS:(i + 1) * CMP_PAIRS].unsqueeze(2)), [t_ck, t_zero[kind]])
            got = {}

            def kv_epilogue(m, bank, t):
                if m < 2:
                    b = slab["kv"[m]]
                    for g in range(2):
                        src = bank[g * HD:(g + 1) * HD, :]
                        V.do(lambda e, src=src, g=g: e.tensor_copy(b[0:HD, g * S:(g + 1) * S], src[:, 0:S]),
                             [t, t_pe["kv"[m]]])
                        t1 = V.do(lambda e, src=src, g=g: e.tensor_copy(b[HD:P, g * S:g * S + S - 1], src[:, 1:S]),
                                  [t])
                else:
                    b = kdup["sw"[m - 2]]
                    for g in range(2):
                        src = bank[g * HD:(g + 1) * HD, 0:S]
                        for half in range(2):
                            t1 = A.do(lambda e, src=src, g=g, half=half: e.activation(
                                b[half * HD:(half + 1) * HD, g * S:(g + 1) * S], src, ACT.Copy), [t] + done)
                got[("kv", m)] = t1
                return [t1]

            def vsg_epilogue(tt, bank, t):
                t1 = A.do(lambda e: e.activation(vsw[:, tt * VSG:(tt + 1) * VSG], bank[:, 0:VSG], ACT.Copy), [t] + done)
                got[("vsg", tt)] = t1
                table(SIGMOID)
                t2 = A.do(lambda e: e.activation(gates[:, tt * 24:(tt + 1) * 24], bank[:, 2 * P:VSG], ACT.Sigmoid), [t])
                got[("gates", tt)] = t2
                return [t2]

            def qz_epilogue(m, bank, t):
                kind, k = ("qn", "qm", "km", "zm", "zn")[m // 4], m % 4
                if kind in ("zm", "zn"):
                    dst = tile(zs, k + (4 if kind == "zn" else 0))
                    table(SILU)
                    got[m] = A.do(lambda e: e.activation(dst, bank[:, 0:S], ACT.Silu), [t] + done)
                else:
                    dst = tile({"qn": qn_sb, "qm": qm_sb, "km": km_sb}[kind], k)
                    scale = 1.0 if kind == "km" else HD ** -0.5
                    got[m] = A.do(lambda e: e.activation(dst, bank[:, 0:S], ACT.Copy, scale=scale), [t] + done)
                return [got[m]]

            project(f"w_kv{layer}", range(4), H, kv_epilogue, together=3)
            project_rows(f"w_vsg{layer}", VSG, H, vsg_epilogue)

            for buf in (pc, kc_pair, vc_pair):
                zero_t = V.do(lambda e: e.memset(buf, 0.0), done)
            t_gelu = {}
            for i, kind in enumerate("kv"):
                n, bank, free = banks.take()
                s3 = slab[kind].rearrange("p (g t) -> p g t", g=3)
                for j in range(CMP_PAIRS):
                    rhs = s3[:, :, 2 * j:2 * j + (CMP_T - 1) * CMP_STRIDE + 1:CMP_STRIDE]
                    at = (i * CMP_PAIRS + j) * HD
                    t = mm(bank[0:HD, 0:3 * CMP_T].rearrange("p (g t) -> p g t", g=3), ck[:, at:at + HD], rhs,
                           j == 0, j == CMP_PAIRS - 1, [t_ck, got[("kv", i)]] + free, signal=j == CMP_PAIRS - 1)
                gp = gel[0:HD, i * 64:(i + 1) * 64].rearrange("p (g t) -> p g t", g=2)[:, :, 0:CMP_T]
                t1 = V.do(lambda e, bank=bank: e.tensor_copy(st[0:HD, i:i + 1], bank[0:HD, 2 * CMP_T:2 * CMP_T + 1]),
                          [t, t_pe["v"]] + done)
                table(GELU)
                t_gelu[kind] = A.do(lambda e, bank=bank, gp=gp: e.activation(
                    gp, bank[0:HD, 0:2 * CMP_T].rearrange("p (g t) -> p g t", g=2),
                    ACT.Gelu_apprx_tanh, bias=st[0:HD, i:i + 1]), [t1, t_pe["v"], T.last()])
                banks.give(n, [t_gelu[kind]])

            def compress_out(i, kind):
                n, bank, free = banks.take()
                t2 = t_gelu[kind]
                for g in range(2):
                    gx = gel[0:HD, i * 64 + g * 32:i * 64 + g * 32 + CMP_T]
                    if kind == "k":
                        for half in range(2):
                            t = mm(bank[half * HD:(half + 1) * HD, g * 32:g * 32 + CMP_T], ck2[0:HD, 0:HD], gx,
                                   g == 0, True, [t2] + free, signal=True)
                    else:
                        t = mm(bank[0:CMP_T, g * HD:(g + 1) * HD], gx, ck2[0:HD, HD:2 * HD], g == 0, True,
                               [t2] + free, signal=True)
                if kind == "k":
                    for j in range(2):
                        rows = slice(j * HD, (j + 1) * HD)
                        t3 = V.do(lambda e: e.tensor_copy(
                            kc_pair[rows, :].rearrange("p (g t) -> p g t", g=2)[:, :, j * CMP_W:j * CMP_W + CMP_T],
                            bank[rows, 0:64].rearrange("p (g t) -> p g t", g=2)[:, :, 0:CMP_T]), [t, zero_t])
                else:
                    for r in range(HPG):
                        t3 = V.do(lambda e: e.tensor_copy(
                            vc_pair[CMP_W * r:CMP_W * r + CMP_T, :].rearrange("p (g c) -> p g c", g=2)[
                                :, :, r * HD:(r + 1) * HD],
                            bank[0:CMP_T, 0:2 * HD].rearrange("p (g c) -> p g c", g=2)), [t, zero_t])
                got[("cmp", kind)] = t3
                banks.give(n, [t3])

            for c in range(2):
                def vm_epilogue(tt, bank, t, c=c):
                    got[("vm", tt, c)] = A.do(lambda e: e.activation(
                        vm[:, tt * 512 + c * S:tt * 512 + (c + 1) * S], bank[:, 0:S], ACT.Copy), [t] + done)
                    return [got[("vm", tt, c)]]
                project_rows(f"w_vm{layer}", S, H, vm_epilogue)
                compress_out(c, "kv"[c])
            project(f"w_qz{layer}", range(20), H, qz_epilogue)
            flush()

            ready = [A.last(), V.last(), t_alibi]
            Y = Split(h_hi, h_lo, S)
            units = []
            obank = {}
            KINDS = ("m", "s", "w")
            HEAD_PAIRS = ((0, 2), (1, 3), (4, 6), (5, 7))

            def head(kind, h, qb):
                r = (h % 2) * HD
                g = h // HPG
                q = (qm_sb if kind == "m" else qn_sb)[r:r + HD, (h // 2) * S + qb * P:(h // 2) * S + (qb + 1) * P]
                nk = (qb + 1) * P
                if kind == "m":
                    return q, km_sb[r:r + HD, (h // 2) * S:(h // 2) * S + nk], [
                        vm[:, kt * 512 + h * HD:kt * 512 + (h + 1) * HD] for kt in range(qb + 1)]
                at = 0 if kind == "s" else P
                return q, kdup[kind][r:r + HD, g * S:g * S + nk], [
                    vsw[:, kt * VSG + at + g * HD:kt * VSG + at + (g + 1) * HD] for kt in range(qb + 1)]

            def gate_out(qb, first_tile, bank, t):
                view = lambda buf: buf[:, first_tile * S:(first_tile + 4) * S].rearrange(
                    "p (h c) -> p h c", h=4)[:, :, qb * P:(qb + 1) * P]
                full = view(zs)
                t1 = V.do(lambda e: e.tensor_tensor(full, bank.rearrange("p (h c) -> p h c", h=4), full, ALU.mult), [t])
                t2 = A.do(lambda e: e.activation(view(h_hi), full, ACT.Copy), [t1])
                t3 = V.do(lambda e: e.tensor_tensor(view(h_lo), full, view(h_hi).bitcast(F32), ALU.subtract), [t2])
                for j in range(4):
                    Y.hi_t[first_tile + j], Y.lo_t[first_tile + j] = t2, t3
                return t1

            heads_of = lambda a: a.rearrange("p (h t) -> p h t", h=H_HEADS)
            g3 = lambda qb: gates[:, qb * 24:(qb + 1) * 24].rearrange("p (h i) -> p h i", i=3)
            W8 = H_HEADS * CMP_W

            def compressed_scores(qb):
                n, b, free = banks.take()
                for m in range(H_HEADS // 2):
                    t = mm(b[:, m * 2 * CMP_W:(m + 1) * 2 * CMP_W], qn_sb[:, m * S + qb * P:m * S + (qb + 1) * P],
                           kc_pair[:, (m // 2) * 2 * CMP_W:(m // 2 + 1) * 2 * CMP_W], m == 0, True,
                           ready + free, signal=True)
                v3 = heads_of(pc[:, qb * W8:(qb + 1) * W8])[:, :, 0:CMP_T]
                bias = heads_of(con("cmp_bias", qb * H_HEADS * CMP_T, H_HEADS * CMP_T))
                mx = st[:, qb * 2 * H_HEADS:qb * 2 * H_HEADS + H_HEADS]
                t = V.do(lambda e: e.tensor_tensor(v3, heads_of(b[:, 0:W8])[:, :, 0:CMP_T], bias, ALU.add),
                         [t, zero_t])
                banks.give(n, [t])
                t = V.do(lambda e: e.tensor_reduce(mx, v3, AX.X, ALU.max), [t])
                t = V.do(lambda e: e.tensor_tensor(v3, v3, mx.unsqueeze(2).to_broadcast([P, H_HEADS, CMP_T]),
                                                   ALU.subtract), [t])
                table(LOG_EXP)
                cmp_t[qb] = A.do(lambda e: e.activation(v3, v3, ACT.Exp), [t])

            def compressed_turn(qb):
                cols = pc[:, qb * W8:(qb + 1) * W8]
                v3 = heads_of(cols)[:, :, 0:CMP_T]
                ok = con("cmp_ok", qb * CMP_T, CMP_T).unsqueeze(1).to_broadcast([P, H_HEADS, CMP_T])
                sm = st[:, qb * 2 * H_HEADS + H_HEADS:(qb + 1) * 2 * H_HEADS]
                t = V.do(lambda e: e.tensor_reduce(sm, v3, AX.X, ALU.add), [cmp_t[qb]])
                t = V.do(lambda e: e.reciprocal(sm, sm), [t])
                t = V.do(lambda e: e.tensor_tensor(sm.unsqueeze(2), sm.unsqueeze(2), g3(qb)[:, :, 0:1], ALU.mult), [t])
                t = V.do(lambda e: e.tensor_tensor(v3, v3, sm.unsqueeze(2).to_broadcast([P, H_HEADS, CMP_T]),
                                                   ALU.mult), [t])
                t_p = V.do(lambda e: e.tensor_tensor(v3, v3, ok, ALU.mult), [t])

                def turn_it():
                    n, b, free = banks.take()
                    for g in range(2):
                        t = T.do(lambda e: e.transpose(b[:, g * P:(g + 1) * P], cols[:, g * P:(g + 1) * P],
                                                       con("ident")), [t_p] + free, signal=True)
                    cmp_t[qb] = V.do(lambda e: e.tensor_copy(pcT[:, qb * W8:(qb + 1) * W8], b[:, 0:W8]), [t])
                    banks.give(n, [cmp_t[qb]])
                later(1, turn_it)

            def compressed_values(qb, b, free):
                for m in range(H_HEADS // 2):
                    g = m // 2
                    mm(b[:, m * P:(m + 1) * P], vc_pair[:, m * P:(m + 1) * P],
                       pcT[:, qb * W8 + g * P:qb * W8 + (g + 1) * P], m == 0, False, [cmp_t[qb], got[("cmp", "v")]] + free)
            cmp_t = {}

            def hybrid_unit(qb, kn, kind, hn, pair):
                heads = [head(kind, h, qb) for h in pair]
                nk = (qb + 1) * P
                last = hn == len(HEAD_PAIRS) - 1

                def weigh(eb, rl, t):
                    for j, h in enumerate(pair):
                        p = eb[:, j * S:j * S + nk]
                        gate = None if kind == "m" else gates[:, qb * 24 + h * 3 + kn:qb * 24 + h * 3 + kn + 1]
                        t1 = V.do(lambda e: e.tensor_scalar(p, p, rl[:, j:j + 1], gate, ALU.mult,
                                                            *([] if gate is None else [ALU.mult])), [t])
                    return t1

                def bank():
                    if hn == 0 and kind != "w":
                        obank[kind] = banks.take()
                        if kind == "s":
                            compressed_values(qb, obank["s"][1], obank["s"][2])
                    n, b, free = obank["m" if kind == "m" else "s"]
                    return b, free

                def then(t):
                    if last and kind != "s":
                        n, b, _ = obank["m" if kind == "m" else "s"]
                        banks.give(n, [gate_out(qb, 0 if kind == "m" else 4, b, t)])

                return dict(nk=nk, after=ready, weigh=weigh, bank=bank, then=then, start=kind == "m",
                            scores=[(q, k, alibi[:, h * S + S - nk:(h + 1) * S]) for h, (q, k, _) in zip(pair, heads)],
                            values=[v for _, _, v in heads],
                            out=lambda b, j: b[(pair[j] % 2) * HD:(pair[j] % 2 + 1) * HD,
                                               (pair[j] // 2) * P:(pair[j] // 2 + 1) * P])

            for qb in range(TT):
                for kn, kind in enumerate(KINDS):
                    for hn, pair in enumerate(HEAD_PAIRS):
                        units.append(hybrid_unit(qb, kn, kind, hn, pair))
            for qb in range(TT):
                compressed_scores(qb)
                later(qb, lambda qb=qb: compressed_turn(qb))
            attend(units, sc, 1)

            y_sb = sq
            ys = arena[:, 0:KD * S]
            y_sums = SquareSums(ys, STEADY)

            def out_epilogue(m, bank, t):
                t1 = V.do(lambda e: e.tensor_copy(tile(y_sb, m), bank[:, 0:S]), [t])
                y_sums.add(m, A.do(lambda e: e.activation(tile(ys, m), tile(y_sb, m), ACT.Square), [t1]))
                return [t1]
            project(f"w_out{layer}", range(KD), Y, out_epilogue)
            flush()
            n, bank, t_sum = y_sums.finish()
            t_rstd, t_free = rstd_of(bank, t_sum, D, [V.last()])
            banks.give(n, [t_free])
            nxt = SquareSums(ys, [G, None, G, None, G, None, None, None])
            for k in range(KD):
                t1 = V.do(lambda e, k=k: e.scalar_tensor_tensor(tile(y_sb, k), tile(y_sb, k),
                                                                mod[:, 2 * KD + k:2 * KD + k + 1], rstd_sb[:, :],
                                                                ALU.mult, ALU.mult), [t_rstd])
                adder = G if layer == DEPTH - 1 and k % 2 else V
                t2 = adder.do(lambda e, k=k: e.tensor_tensor(tile(xT, k), tile(xT, k), tile(y_sb, k), ALU.add), [t1])
                x_t[k] = t2
                if layer < DEPTH - 1:
                    nxt.add(k, A.do(lambda e, k=k: e.activation(tile(ys, k), tile(xT, k), ACT.Square), [t2, t_sum]))
            return nxt

        x_t = {}
        for layer in range(DEPTH):
            sums = hybrid(layer, sums)
        parts = 4
        for i in range(parts):
            c = slice(i * KD * S // parts, (i + 1) * KD * S // parts)
            load(d["out"][:, c], xT[:, c], s_out, 16 * (i + 1), [x_t[k] for k in range(i * KD // parts, (i + 1) * KD // parts)])
        L.wait([(s_out, 16 * parts)])
        assert W.loaded == len(plan) and W.used == len(W.units)


def _columns(a):
    a = np.asarray(a)
    n = a.shape[-1] // P
    a = a.reshape(-1, n, P)
    return a.transpose(2, 0, 1).reshape(P, -1)


def _tiles(w, per_chunk):
    k, m = w.shape[0] // P, w.shape[1] // P
    a = w.reshape(k, P, m, P).transpose(2, 1, 0, 3)
    a = a.reshape(m // per_chunk, per_chunk, P, k * P).transpose(0, 2, 1, 3)
    return np.ascontiguousarray(a.reshape(m // per_chunk, P, per_chunk * k * P))


def _rows(w, width):
    k, n = w.shape[0] // P, w.shape[1] // width
    return np.ascontiguousarray(w.reshape(k, P, n, width).transpose(2, 1, 0, 3).reshape(n, P, k * width))


def _pairs(w):
    k, m = w.shape[0] // P, w.shape[1]
    return np.ascontiguousarray(w.reshape(k // 2, 2, P, m).transpose(0, 2, 1, 3).reshape(k // 2, P, 2 * m))


def layout(i):
    a = {k: np.asarray(v) for k, v in i.items()}
    out = {}
    out["x"] = np.ascontiguousarray(a["x"][0].T.reshape(KD, P, S).transpose(1, 0, 2).reshape(P, KD * S))
    out["positions"] = np.ascontiguousarray(np.broadcast_to(a["positions"][0][None, :], (P, S)))
    p = np.zeros((P, NPARAMS), np.float32)

    def put(name, v, rows=P):
        at, n = PARAMS[name]
        p[0:rows, at:at + n] = np.asarray(v).reshape(rows, n)

    put("mix_g", _columns(a["norm_mix_g"]))
    put("ffn_g", _columns(a["norm_ffn_g"]))
    put("ssd_conv", _columns(np.concatenate([a["ssd_conv_w"][0], a["ssd_conv_b"]], 0)))
    put("ssd_norm_g", _columns(a["ssd_norm_g"]))
    put("ssd_d", _columns(np.repeat(a["ssd_d"][0], SSD_P)))
    put("dt_bias", a["ssd_dt_bias"][0], SSD_HEADS)
    put("a_log", a["ssd_a_log"][0], SSD_HEADS)
    put("ffn_conv", np.concatenate([_columns(np.concatenate([a["ffn_conv_w"][n], a["ffn_conv_b"][n:n + 1]], 0))
                                    for n in range(DEPTH)], 1))
    put("q_g", np.tile(a["attn_q_norm_g"][0], 2))
    put("k_g", np.tile(a["attn_k_norm_g"][0], 2))
    put("subln_g", a["attn_subln_g"][0])
    put("lam", np.broadcast_to(np.concatenate([a[f"attn_{n}"][0] for n in ("lq1", "lk1", "lq2", "lk2")])[None, :],
                               (P, 4 * HD)))
    out["c"] = np.ascontiguousarray(np.broadcast_to(a["c_2"], (P, D)))
    put("b_ada", _columns(a["b_ada_2"]))
    put("g_pre", _columns(a["g_pre_2"]))
    put("g_post", _columns(a["g_post_2"]))
    out["params"] = p
    w = a["ssd_in_w"][0]
    z, xs, bc, dt = (w[:, 0:SSD_INNER], w[:, SSD_INNER:2 * SSD_INNER],
                     w[:, 2 * SSD_INNER:2 * SSD_INNER + 2 * SSD_GROUPS * SSD_N], w[:, -SSD_HEADS:])
    out["w_dt"] = _tiles(np.concatenate([dt, np.zeros((D, P - SSD_HEADS), np.float32)], 1), 1)
    out["w_ssd_in"] = _tiles(np.concatenate([bc, xs, z], 1), 2)
    out["w_ssd_out"] = _pairs(a["ssd_out_w"][0])
    for n in range(DEPTH):
        up = a["ffn_up_w"][n].reshape(D, 2, FF_TILES, P).transpose(0, 2, 1, 3).reshape(D, 2 * D_FF)
        out[f"w_up{n}"] = _tiles(up, 2)
        out[f"w_down{n}"] = _pairs(a["ffn_down_w"][n])
        out[f"w_ada{n}"] = np.ascontiguousarray(
            a["w_ada_2"][n].T.reshape(ADA_CHUNKS, ADA_TILES, P, D).transpose(0, 2, 1, 3).reshape(
                ADA_CHUNKS, P, ADA_TILES * D))
        u = a["w_in_2"][n]
        qm, km, vm, zm, qn = (u[:, j * 512:(j + 1) * 512] for j in range(5))
        kc, vc, ks, vs, kw, vw = (u[:, 2560 + j * P:2560 + (j + 1) * P] for j in range(6))
        gl, zn = u[:, 3328:3352], u[:, 3352:3864]
        out[f"w_kv{n}"] = _tiles(np.concatenate([kc, vc, ks, kw], 1), 2)
        out[f"w_vsg{n}"] = _rows(np.concatenate([vs, vw, gl], 1), VSG)
        out[f"w_vm{n}"] = _rows(vm, S)
        out[f"w_qz{n}"] = _tiles(np.concatenate([qn, qm, km, zm, zn], 1), 2)
        out[f"w_out{n}"] = _tiles(a["w_out_2"][n], 2)
        ck1 = np.stack([a["w_ck1_2"][n], a["w_cv1_2"][n]]).reshape(2, CMP_PAIRS, P, HD)
        out[f"ck1_{n}"] = np.ascontiguousarray(ck1.transpose(2, 0, 1, 3).reshape(P, 2 * CMP_PAIRS * HD))
        out[f"ck2_{n}"] = np.concatenate([a["w_ck2_2"][n], a["w_cv2_2"][n]], 1)
        pe = np.stack([a["pe_k_2"][n], a["pe_v_2"][n]]).reshape(2, CMP_PAIRS, P)
        out[f"pe_{n}"] = np.ascontiguousarray(pe.transpose(2, 0, 1).reshape(P, 2 * CMP_PAIRS))
    qkv = a["attn_in_w"][0]
    out["w_attn_in"] = _tiles(qkv[:, 0:2 * D], 2)
    out["w_attn_v"] = _rows(qkv[:, 2 * D:], S)
    out["w_attn_out"] = _tiles(a["attn_out_w"][0], 2)
    out["consts"], out["alibi"] = constants()
    return out


def kernel(**inputs):
    import concourse.bacc as _bacc
    from concourse import mybir as _mybir
    from concourse.bass_utils import run_bass_kernel_spmd as _run

    nc = _bacc.Bacc("TRN2", target_bir_lowering=False, num_devices=1)
    arrays = layout(inputs)
    d = {name: nc.dram_tensor(name, a.shape, _mybir.dt.from_np(a.dtype), kind="ExternalInput").ap()
         for name, a in arrays.items()}
    d["out"] = nc.dram_tensor("out", (P, KD * S), F32, kind="ExternalOutput").ap()
    build_program(nc, d)
    r = _run(nc, [arrays], core_ids=[0])
    got = np.asarray(r.results[0]["out"])
    return np.ascontiguousarray(got.reshape(P, KD, S).transpose(2, 1, 0).reshape(1, S, D))
```
